# Optimizing a Trainium2 kernel written in Bass

```python
import math
import jax
import jax.numpy as jnp
from jax import lax
import numpy as np

D_MODEL = 1024
BATCH = 1
SEQ = 256
DEPTH = 2

HEAD_DIM = 64
NSA_HEADS = 8
NSA_KV_HEADS = 2
NSA_GROUP = NSA_HEADS // NSA_KV_HEADS
CMP_BLOCK = 32
CMP_STRIDE = 16
CMP_HIDDEN = 128
SEL_BLOCK = 64
N_SELECT = 16
N_LOCAL_SEL = 2
WINDOW = 512
NSA_Q_BLOCK = 64
FOX_HEADS = 8
Q_BLOCK = 128
REL_BUCKETS = 32
REL_MAX_DIST = 128
D_FF_DENSE = 2816
N_EXPERTS = 8
TOP_K = 2
D_FF_EXPERT = 3584
DN_ALPHA = (2 * DEPTH) ** 0.25
DN_BETA = (8 * DEPTH) ** -0.25
LN_EPS = 1e-5
FORCED_SCORE = 1e4
NEG_INF = -1e30

NSA_Q_W = NSA_HEADS * HEAD_DIM
NSA_KV_W = NSA_KV_HEADS * HEAD_DIM
FOX_W = FOX_HEADS * HEAD_DIM
IN_SPLITS = (NSA_Q_W, 6 * NSA_KV_W, 3 * NSA_HEADS, 3 * FOX_W, FOX_HEADS, 2 * D_MODEL)
D_IN_PROJ = NSA_Q_W + 6 * NSA_KV_W + 3 * NSA_HEADS + 3 * FOX_W + FOX_HEADS + 2 * D_MODEL
N_DENSE_LAYERS = (DEPTH + 1) // 2
N_MOE_LAYERS = DEPTH // 2

kernel_name = 'hybrid_nsa_fox_moe_deepnorm'

def layer_norm(x, g, b):
    xf = x.astype(jnp.float32)
    mu = xf.mean(-1, keepdims=True)
    var = jnp.square(xf - mu).mean(-1, keepdims=True)
    return ((xf - mu) * lax.rsqrt(var + LN_EPS) * g + b).astype(x.dtype)

def masked_softmax(s, mask, axis):
    s = jnp.where(mask, s.astype(jnp.float32), NEG_INF)
    s = s - s.max(axis=axis, keepdims=True)
    e = jnp.where(mask, jnp.exp(s), 0.0)
    return e / jnp.maximum(e.sum(axis=axis, keepdims=True), 1e-30)

def t5_bucket(dist):
    n = jnp.maximum(dist, 0)
    max_exact = REL_BUCKETS // 2
    large = max_exact + (jnp.log(jnp.maximum(n, 1).astype(jnp.float32) / max_exact)
                         / math.log(REL_MAX_DIST / max_exact) * (REL_BUCKETS - max_exact)).astype(jnp.int32)
    large = jnp.minimum(large, REL_BUCKETS - 1)
    return jnp.where(n < max_exact, n, large)

def compress_blocks(kv, pe, w1, w2):
    B, S, Hkv, dk = kv.shape
    r = CMP_BLOCK // CMP_STRIDE
    n_half = S // CMP_STRIDE
    n_cmp = n_half - r + 1
    h = kv.reshape(B, n_half, CMP_STRIDE, Hkv, dk)
    blocks = jnp.concatenate([h[:, j:j + n_cmp] for j in range(r)], axis=2)
    blocks = blocks + pe[None, None, :, None, :]
    blocks = blocks.transpose(0, 1, 3, 2, 4).reshape(B, n_cmp, Hkv, CMP_BLOCK * dk)
    return jax.nn.gelu(blocks @ w1) @ w2

def cmp_to_sel_overlap(n_cmp, n_sel):
    c0 = np.arange(n_cmp)[:, None] * CMP_STRIDE
    s0 = np.arange(n_sel)[None, :] * SEL_BLOCK
    ov = np.maximum(np.minimum(c0 + CMP_BLOCK, s0 + SEL_BLOCK) - np.maximum(c0, s0), 0)
    return jnp.asarray(ov / CMP_BLOCK, dtype=jnp.float32)

def nsa_attention(q, k_c, v_c, k_s, v_s, k_w, v_w, gates, rel_bias):
    B, S, Hkv, G, dk = q.shape
    n_cmp = k_c.shape[1]
    n_sel = S // SEL_BLOCK
    top_n = min(N_SELECT, n_sel)
    n_qb = S // NSA_Q_BLOCK
    scale = dk ** -0.5
    tab = rel_bias.astype(jnp.float32).reshape(REL_BUCKETS, Hkv, G)
    tab_h = tab.transpose(1, 0, 2)
    cmp_end = jnp.arange(n_cmp) * CMP_STRIDE + CMP_BLOCK - 1
    overlap = cmp_to_sel_overlap(n_cmp, n_sel)
    blk = jnp.arange(n_sel)
    k_sb = k_s.reshape(B, n_sel, SEL_BLOCK, Hkv, dk).transpose(0, 3, 1, 2, 4)
    v_sb = v_s.reshape(B, n_sel, SEL_BLOCK, Hkv, dk).transpose(0, 3, 1, 2, 4)
    b_idx = jnp.arange(B)[:, None, None, None]
    h_idx = jnp.arange(Hkv)[None, :, None, None]
    pad = ((0, 0), (WINDOW, 0), (0, 0), (0, 0))
    k_wp = jnp.pad(k_w, pad)
    v_wp = jnp.pad(v_w, pad)
    qi = jnp.arange(NSA_Q_BLOCK)
    kj = jnp.arange(NSA_Q_BLOCK + WINDOW)
    rel_w = qi[:, None] + WINDOW - kj[None, :]
    band = (rel_w >= 0) & (rel_w < WINDOW)
    bias_w = tab[t5_bucket(rel_w)].transpose(2, 3, 0, 1)

    def block(args):
        c, qb, gb = args
        t = c * NSA_Q_BLOCK + qi
        s_c = jnp.einsum('bqhgd,bchd->bhgqc', qb, k_c) * scale
        vis_c = cmp_end[None, :] <= t[:, None]
        bias_c = tab[t5_bucket(t[:, None] - cmp_end[None, :])].transpose(2, 3, 0, 1)
        p_c = masked_softmax(s_c + bias_c, vis_c, -1)
        o_c = jnp.einsum('bhgqc,bchd->bqhgd', p_c.astype(v_c.dtype), v_c)
        imp = jnp.einsum('bhgqc,cj->bhqj', p_c, overlap)
        cur = (t // SEL_BLOCK)[:, None]
        forced = (blk[None, :] == 0) | ((blk[None, :] <= cur) & (blk[None, :] > cur - N_LOCAL_SEL))
        imp = jnp.where(forced, FORCED_SCORE, jnp.where(blk[None, :] <= cur, imp, -1.0))
        _, idx = lax.top_k(imp, top_n)
        k_g = k_sb[b_idx, h_idx, idx]
        v_g = v_sb[b_idx, h_idx, idx]
        pos = idx[..., None] * SEL_BLOCK + jnp.arange(SEL_BLOCK)
        rel_s = t[:, None, None] - pos
        vis_s = (rel_s >= 0)[:, :, None]
        bias_s = tab_h[h_idx[..., None], t5_bucket(rel_s)].transpose(0, 1, 5, 2, 3, 4)
        s_s = jnp.einsum('bqhgd,bhqnld->bhgqnl', qb, k_g) * scale + bias_s
        p_s = masked_softmax(s_s, vis_s, (-2, -1))
        o_s = jnp.einsum('bhgqnl,bhqnld->bqhgd', p_s.astype(v_g.dtype), v_g)
        k_wb = lax.dynamic_slice_in_dim(k_wp, c * NSA_Q_BLOCK, NSA_Q_BLOCK + WINDOW, axis=1)
        v_wb = lax.dynamic_slice_in_dim(v_wp, c * NSA_Q_BLOCK, NSA_Q_BLOCK + WINDOW, axis=1)
        s_w = jnp.einsum('bqhgd,bkhd->bhgqk', qb, k_wb) * scale + bias_w
        vis_w = band & ((c * NSA_Q_BLOCK - WINDOW + kj) >= 0)[None, :]
        p_w = masked_softmax(s_w, vis_w, -1)
        o_w = jnp.einsum('bhgqk,bkhd->bqhgd', p_w.astype(v_wb.dtype), v_wb)
        return gb[..., 0:1] * o_c + gb[..., 1:2] * o_s + gb[..., 2:3] * o_w

    q_blocks = q.reshape(B, n_qb, NSA_Q_BLOCK, Hkv, G, dk).transpose(1, 0, 2, 3, 4, 5)
    g_blocks = gates.reshape(B, n_qb, NSA_Q_BLOCK, Hkv, G, 3).transpose(1, 0, 2, 3, 4, 5)
    out = lax.map(block, (jnp.arange(n_qb), q_blocks, g_blocks))
    return out.transpose(1, 0, 2, 3, 4, 5).reshape(B, S, Hkv * G * dk)

def forgetting_attention(q, k, v, log_f):
    B, S, H, dk = q.shape
    n_qb = S // Q_BLOCK
    scale = dk ** -0.5
    F = jnp.cumsum(log_f, axis=1)
    F_k = F.transpose(0, 2, 1)
    key_pos = jnp.arange(S)

    def block(args):
        c, qb, Fq = args
        t = c * Q_BLOCK + jnp.arange(Q_BLOCK)
        s = jnp.einsum('bqhd,bkhd->bhqk', qb, k).astype(jnp.float32) * scale
        s = s + (Fq.transpose(0, 2, 1)[..., None] - F_k[:, :, None, :])
        p = masked_softmax(s, key_pos[None, :] <= t[:, None], -1)
        return jnp.einsum('bhqk,bkhd->bqhd', p.astype(v.dtype), v)

    q_blocks = q.reshape(B, n_qb, Q_BLOCK, H, dk).transpose(1, 0, 2, 3, 4)
    f_blocks = F.reshape(B, n_qb, Q_BLOCK, H).transpose(1, 0, 2, 3)
    out = lax.map(block, (jnp.arange(n_qb), q_blocks, f_blocks))
    return out.transpose(1, 0, 2, 3, 4).reshape(B, S, H * dk)

def hybrid_mixer(x, w_in, cmp_pe, cmp_w1, cmp_w2, f_bias, w_nsa_br, w_fox_br, w_o, rel_bias):
    B, S, _ = x.shape
    proj = x @ w_in
    offsets = np.cumsum(IN_SPLITS)[:-1].tolist()
    nsa_q, nsa_kv, nsa_g, fox_qkv, fox_f, merge_g = jnp.split(proj, offsets, axis=-1)
    q = nsa_q.reshape(B, S, NSA_KV_HEADS, NSA_GROUP, HEAD_DIM)
    k_c, v_c, k_s, v_s, k_w, v_w = [a.reshape(B, S, NSA_KV_HEADS, HEAD_DIM)
                                    for a in jnp.split(nsa_kv, 6, axis=-1)]
    k_c = compress_blocks(k_c, cmp_pe[0], cmp_w1[0], cmp_w2[0])
    v_c = compress_blocks(v_c, cmp_pe[1], cmp_w1[1], cmp_w2[1])
    gates = jax.nn.sigmoid(nsa_g).reshape(B, S, NSA_KV_HEADS, NSA_GROUP, 3)
    y_nsa = nsa_attention(q, k_c, v_c, k_s, v_s, k_w, v_w, gates, rel_bias)
    fq, fk, fv = [a.reshape(B, S, FOX_HEADS, HEAD_DIM) for a in jnp.split(fox_qkv, 3, axis=-1)]
    log_f = jax.nn.log_sigmoid(fox_f.astype(jnp.float32) + f_bias.astype(jnp.float32))
    y_fox = forgetting_attention(fq, fk, fv, log_f)
    g_nsa, g_fox = jnp.split(jax.nn.sigmoid(merge_g), 2, axis=-1)
    merged = g_nsa * (y_nsa @ w_nsa_br) + g_fox * (y_fox @ w_fox_br)
    return merged @ w_o

def swiglu(x, w_gate, w_up, w_down):
    return (jax.nn.silu(x @ w_gate) * (x @ w_up)) @ w_down

def moe_swiglu(x, router, w_gate, w_up, w_down):
    logits = (x @ router).astype(jnp.float32)
    top_val, top_idx = lax.top_k(logits, TOP_K)
    top_w = jax.nn.softmax(top_val, axis=-1)
    gate = jnp.sum(jax.nn.one_hot(top_idx, N_EXPERTS, dtype=jnp.float32) * top_w[..., None], axis=-2)
    gate = gate.astype(x.dtype)
    out = jnp.zeros_like(x)
    for e in range(N_EXPERTS):
        out = out + gate[..., e:e + 1] * swiglu(x, w_gate[e], w_up[e], w_down[e])
    return out

def setup_inputs(seed: int = 0) -> dict:
    key = jax.random.key(seed)
    ks = jax.random.split(key, 21)
    f32 = jnp.float32

    def nrm(k, shape, scale):
        return jax.random.normal(k, shape, f32) * scale

    return {
        'x': nrm(ks[0], (BATCH, SEQ, D_MODEL), 1.0),
        'w_in': nrm(ks[1], (DEPTH, D_MODEL, D_IN_PROJ), D_MODEL ** -0.5),
        'nsa_cmp_pe': nrm(ks[2], (DEPTH, 2, CMP_BLOCK, HEAD_DIM), 0.1),
        'nsa_cmp_w1': nrm(ks[3], (DEPTH, 2, CMP_BLOCK * HEAD_DIM, CMP_HIDDEN), (CMP_BLOCK * HEAD_DIM) ** -0.5),
        'nsa_cmp_w2': nrm(ks[4], (DEPTH, 2, CMP_HIDDEN, HEAD_DIM), CMP_HIDDEN ** -0.5),
        'fox_f_bias': jax.random.uniform(ks[5], (DEPTH, FOX_HEADS), f32, 1.0, 4.0),
        'w_nsa_branch': nrm(ks[6], (DEPTH, NSA_Q_W, D_MODEL), NSA_Q_W ** -0.5),
        'w_fox_branch': nrm(ks[7], (DEPTH, FOX_W, D_MODEL), FOX_W ** -0.5),
        'w_out': nrm(ks[8], (DEPTH, D_MODEL, D_MODEL), DN_BETA * D_MODEL ** -0.5),
        'rel_bias': nrm(ks[9], (REL_BUCKETS, NSA_HEADS), 0.5),
        'ln1_g': 1.0 + nrm(ks[10], (DEPTH, D_MODEL), 0.02),
        'ln1_b': nrm(ks[11], (DEPTH, D_MODEL), 0.02),
        'ln2_g': 1.0 + nrm(ks[12], (DEPTH, D_MODEL), 0.02),
        'ln2_b': nrm(ks[13], (DEPTH, D_MODEL), 0.02),
        'dense_w_gate': nrm(ks[14], (N_DENSE_LAYERS, D_MODEL, D_FF_DENSE), D_MODEL ** -0.5),
        'dense_w_up': nrm(ks[15], (N_DENSE_LAYERS, D_MODEL, D_FF_DENSE), D_MODEL ** -0.5),
        'dense_w_down': nrm(ks[16], (N_DENSE_LAYERS, D_FF_DENSE, D_MODEL), DN_BETA * D_FF_DENSE ** -0.5),
        'moe_router': nrm(ks[17], (N_MOE_LAYERS, D_MODEL, N_EXPERTS), D_MODEL ** -0.5),
        'moe_w_gate': nrm(ks[18], (N_MOE_LAYERS, N_EXPERTS, D_MODEL, D_FF_EXPERT), D_MODEL ** -0.5),
        'moe_w_up': nrm(ks[19], (N_MOE_LAYERS, N_EXPERTS, D_MODEL, D_FF_EXPERT), D_MODEL ** -0.5),
        'moe_w_down': nrm(ks[20], (N_MOE_LAYERS, N_EXPERTS, D_FF_EXPERT, D_MODEL), DN_BETA * D_FF_EXPERT ** -0.5),
    }

def reference(x, w_in, nsa_cmp_pe, nsa_cmp_w1, nsa_cmp_w2, fox_f_bias, w_nsa_branch, w_fox_branch,
              w_out, rel_bias, ln1_g, ln1_b, ln2_g, ln2_b, dense_w_gate, dense_w_up, dense_w_down,
              moe_router, moe_w_gate, moe_w_up, moe_w_down):
    for layer in range(DEPTH):
        h = hybrid_mixer(x, w_in[layer], nsa_cmp_pe[layer], nsa_cmp_w1[layer], nsa_cmp_w2[layer],
                         fox_f_bias[layer], w_nsa_branch[layer], w_fox_branch[layer], w_out[layer], rel_bias)
        x = layer_norm(DN_ALPHA * x + h, ln1_g[layer], ln1_b[layer])
        j = layer // 2
        if layer % 2 == 0:
            f = swiglu(x, dense_w_gate[j], dense_w_up[j], dense_w_down[j])
        else:
            f = moe_swiglu(x, moe_router[j], moe_w_gate[j], moe_w_up[j], moe_w_down[j])
        x = layer_norm(DN_ALPHA * x + f, ln2_g[layer], ln2_b[layer])
    return x


_drawn_inputs = setup_inputs


def setup_inputs(seed=0):
    import zlib

    import numpy as np

    out = dict(_drawn_inputs(seed))
    spreads = {}
    factors = {'nsa_cmp_pe': 5.705}
    for name, (base, spread) in spreads.items():
        noise = np.random.default_rng([zlib.crc32(name.encode()), seed]).standard_normal(out[name].shape)
        drawn = base * np.exp(spread * noise) if base else spread * noise
        out[name] = jnp.asarray(drawn.astype(out[name].dtype))
    for name, factor in factors.items():
        out[name] = (out[name] * factor).astype(out[name].dtype)
    return out
```

```python
from contextlib import ExitStack

import numpy as np

import concourse.bass as bass
from concourse import mybir

F32 = mybir.dt.float32
F32R = mybir.dt.float32r
U32 = mybir.dt.uint32
I32 = mybir.dt.int32
ALU = mybir.AluOpType
ACT = mybir.ActivationFunctionType
AX = mybir.AxisListType.X

P = 128
D = 1024
KD = D // P
SEQ = 256
TT = SEQ // P
DEPTH = 2
DH = 64
NH = 8
NKV = 2
FH = 8
CMP_BLOCK, CMP_STRIDE, CMP_HID = 32, 16, 128
NC = SEQ // CMP_STRIDE - CMP_BLOCK // CMP_STRIDE + 1
NCP = 16
CM = CMP_BLOCK // 2
BUCKETS, MAX_DIST = 32, 128
FF = 2816
FE = 3584
NE = 8
ALPHA = (2 * DEPTH) ** 0.25
LN_EPS = 1e-5
NEG = -1e30
SCALE = DH ** -0.5
FAR = 1e4

C_Q, C_KC, C_KS, C_KW = 0, 512, 768, 1024
C_FQ, C_FK, C_FV = 1304, 1816, 2328
C_MERGE = 2848
NG = 3 * NH

RAW = 6
CONV = 3
UNIT = 2048
CHUNK = 512
CAP = P

K_ID, K_U, K_MASK, K_VIS, K_IOTA, K_SU, K_ONE, K_BLK = 0, 128, 384, 640, 896, 1024, 1152, 1280
K_END = K_BLK + NH
OH_DOWN, OH_UP0 = 384, 272
OH_UP = OH_UP0 + SEQ


def constants():
    c = np.zeros((P, K_END), np.float32)
    p = np.arange(P)[:, None]
    c[:, K_ID:K_ID + P] = np.eye(P)
    c[:, K_U:K_U + SEQ] = p <= np.arange(SEQ)[None]
    c[:, K_MASK:K_MASK + SEQ] = np.where(np.arange(SEQ)[None] > p + P, NEG, 0.0)
    end = np.arange(NCP) * CMP_STRIDE + CMP_BLOCK - 1
    for t in range(TT):
        vis = (end[None] <= t * P + p) & (np.arange(NCP)[None] < NC)
        for hp in range(2):
            for i in range(NH // 2):
                at = K_VIS + hp * P + t * 64 + i * NCP
                c[:, at:at + NCP] = vis
    c[:, K_IOTA:K_IOTA + P] = np.where(np.arange(P) < CAP, np.arange(P), -2 * FAR)[None]
    c[:, K_SU:K_SU + P] = p < np.arange(P)[None]
    c[:, K_ONE:K_ONE + P] = 1.0
    c[:, K_BLK:K_BLK + NH] = p // NCP == np.arange(NH)[None]

    def onehot(dist):
        n = np.maximum(dist, 0)
        exact = BUCKETS // 2
        far = exact + (np.log(np.maximum(n, 1).astype(np.float32) / exact) / np.log(MAX_DIST / exact)
                       * (BUCKETS - exact)).astype(np.int32)
        bucket = np.where(n < exact, n, np.minimum(far, BUCKETS - 1))
        out = np.zeros((BUCKETS + 1, len(dist)), np.float32)
        out[bucket, np.arange(len(dist))] = dist >= 0
        out[BUCKETS] = dist < 0
        return out

    oh = np.concatenate([onehot(SEQ - 1 - np.arange(OH_DOWN)), onehot(np.arange(OH_UP) - OH_UP0)], 1)
    return c, np.ascontiguousarray(oh)


def free(ap, dims):
    return bass.AP(tensor=ap.tensor, offset=ap.offset, ap=[list(ap.ap[0])] + [list(d) for d in dims])


class Tally:

    def __init__(self, n=0):
        self.n, self.reg, self.per, self.start = n, None, 0, 0

    def at(self, more=0):
        v = self.n + more
        return v if self.reg is None else self.reg * self.per + v

    def enter(self, reg, per):
        self.reg, self.per, self.start = reg, per, self.n

    def leave(self, trips):
        assert self.n == self.start + self.per, (self.n, self.start, self.per)
        self.reg, self.n = None, self.start + self.per * trips


def wait(eng, sem, value):
    if isinstance(value, int) and value <= 0:
        return
    eng.wait_ge(sem, value)


def hybrid_kernel(nc, io, stop=None):
    w_in, w_nb, w_fb, w_out = io["w_in"], io["w_nsa_branch"], io["w_fox_branch"], io["w_out"]

    units = []

    def add(nk, width, parts):
        units.append((nk, width, parts))

    def rows(w, k0, nk, c0, width):
        return w[k0 * P:(k0 + nk) * P, c0:c0 + width].rearrange("(k p) n -> p k n", p=P)

    def add_cols(w, c0, width, kt=KD):
        n = 1 if kt * width <= UNIT else 2
        for h in range(n):
            add(kt // n, width, rows(w, h * kt // n, kt // n, c0, width))

    def add_mixer(L):
        add_cols(w_in[L], C_Q, 512)
        add_cols(w_in[L], C_KC, 256)
        add_cols(w_in[L], C_KS, 256)
        add_cols(w_in[L], C_KW, 256 + NG)
        for kv in range(2):
            add(CM, CMP_HID, rows(io["nsa_cmp_w1"][L, kv], 0, CM, 0, CMP_HID))
        add_cols(w_in[L], C_FQ, 512)
        add_cols(w_in[L], C_FK, 512)
        add_cols(w_in[L], C_FV, 256)
        add_cols(w_in[L], C_FV + 256, 256 + FH)
        for half in range(2):
            for g in range(2):
                add_cols(w_in[L], C_MERGE + g * D + half * 512, 512)
            add_cols(w_nb[L], half * 512, 512, 4)
            add_cols(w_fb[L], half * 512, 512, 4)
        for half in range(2):
            add_cols(w_out[L], half * 512, 512)

    def chunks(total):
        return [min(CHUNK, total - c) for c in range(0, total, CHUNK)]

    def down_units(width):
        return width // P // 2

    def ffn_order(total):
        ws = chunks(total)
        out = []
        for c, width in enumerate(ws):
            out += [("gate", c, 0), ("gate", c, 1), ("up", c, 0), ("up", c, 1)]
            if c:
                out += [("down", c - 1, i) for i in range(down_units(ws[c - 1]))]
        return out + [("down", len(ws) - 1, i) for i in range(down_units(ws[-1]))]

    def ffn_unit(gate, up, down, total, kind, c, i):
        width = chunks(total)[c]
        if kind == "down":
            return 2, D, rows(down, c * CHUNK // P + 2 * i, 2, 0, D)
        return KD // 2, width, rows(gate if kind == "gate" else up, i * KD // 2, KD // 2, c * CHUNK, width)

    add_mixer(0)
    for u in ffn_order(FF):
        add(*ffn_unit(io["dense_w_gate"][0], io["dense_w_up"][0], io["dense_w_down"][0], FF, *u))
    add_mixer(1)
    moe_units = ffn_order(FE)

    ctx = ExitStack()
    with ctx:
        def sb(name, shape, dt=F32):
            return ctx.enter_context(nc.sbuf_tensor(name, shape, dt))

        def sem(name):
            return ctx.enter_context(nc.semaphore(name))

        raw = sb("raw", [P, RAW, UNIT])
        hi = sb("hi", [P, CONV, UNIT], F32R)
        lo = sb("lo", [P, CONV, UNIT], F32R)
        x = sb("x", [P, TT, D])
        xTh = sb("xTh", [P, KD, SEQ], F32R)
        xTl = sb("xTl", [P, KD, SEQ], F32R)
        yTh = sb("yTh", [P, KD, SEQ], F32R)
        yTl = sb("yTl", [P, KD, SEQ], F32R)
        table = sb("table", [P, K_END])
        toep = sb("toep", [P, NH, SEQ])
        cbias = sb("cbias", [P, 2, TT * 4 * NCP])
        qk = sb("qk", [P, 8, SEQ])
        kv = sb("kv", [P, 8, SEQ])
        ksw = sb("ksw", [P, 2, SEQ])
        vsw = sb("vsw", [P, 2, TT, P])
        gates = sb("gates", [P, TT, NG])
        logf = sb("logf", [P, 4, TT, FH])
        fcum = sb("fcum", [P, TT, FH])
        blocks = sb("blocks", [P, 2, CM, 2 * NCP])
        small = sb("small", [P, 480])
        pbuf = sb("pbuf", [P, 3, 2, SEQ])
        ptb = sb("ptb", [P, 2, 512])
        lng = sb("lng", [P, 2, D])
        hTh = sb("hTh", [P, 4, SEQ], F32R)
        hTl = sb("hTl", [P, 4, SEQ], F32R)
        vcb = sb("vcb", [P, NH, DH])
        cmpw2 = sb("cmpw2", [P, 2, DH])
        pe_rows = sb("pe_rows", [32, P])
        pe_cols = sb("pe_cols", [P, 2, CM])
        fbias = sb("fbias", [P, FH])
        stats = sb("stats", [P, TT, 16])
        eps = sb("eps", [P, 1])
        flag = sb("flag", [P, 1], I32)
        ps = ctx.enter_context(nc.psum_tensor("ps", [P, 8, 512], F32))

        ident = table[:, K_ID:K_ID + P]
        tri = table[:, K_U:K_U + SEQ]
        merged = qk[:, :, :].rearrange("p a b -> p (a b)").rearrange("p (t n) -> p t n", t=TT)
        sig = kv[:, :, :].rearrange("p a b -> p (a b)").rearrange("p (g t n) -> p g t n", g=2, t=TT)
        fkT = kv[:, 0:4, :]
        fv = kv[:, 4:8, :].rearrange("p a b -> p (a b)").rearrange("p (t n) -> p t n", t=TT)
        blh = yTh[:, 0:4, :].rearrange("p a b -> p (a b)").rearrange("p (v m n) -> p v m n", v=2, m=CM)
        bll = yTl[:, 0:4, :].rearrange("p a b -> p (a b)").rearrange("p (v m n) -> p v m n", v=2, m=CM)
        h = blocks[:, :, :, :].rearrange("p v m n -> p (v m n)").rearrange("p (t n) -> p t n", t=TT)
        onehot = kv[0:BUCKETS + 1, 0:4, :].rearrange("p a b -> p (a b)")[:, 0:OH_DOWN + OH_UP]
        tab = small[0:BUCKETS + 1, 0:NH]
        vrow = ptb[0:NH, 0, 0:OH_DOWN]
        gkT = small[:, 0:2 * NCP]
        kcT = small[:, 64:64 + NCP]
        gvT = small[:, 128:256]
        pct = small[:, 128:384]
        csum = small[:, 384:448].rearrange("p (a b) -> p a b", a=4)
        cs = pbuf[:, 0, :, :].rearrange("p a b -> p (a b)")

        scratch = nc.dram_tensor("bias_rows", (P, NH, OH_DOWN), F32, kind="Internal").ap()

        const_in, x_in, small_in, lng_in = sem("const_in"), sem("x_in"), sem("small_in"), sem("lng_in")
        onehot_in, vrow_out, toep_in = sem("onehot_in"), sem("vrow_out"), sem("toep_in")
        raw_in = [sem(f"raw_in{i}") for i in range(RAW)]
        hi_ready, lo_ready, unit_used = sem("hi_ready"), sem("lo_ready"), sem("unit_used")
        pair_full = [sem("pair_full0"), sem("pair_full1")]
        pair_free = [sem("pair_free0"), sem("pair_free1")]
        dve_step, act_step = sem("dve_step"), sem("act_step")
        eps_set, tab_set, vrow_set, pe_turned, pe_cols_set = (
            sem("eps_set"), sem("tab_set"), sem("vrow_set"), sem("pe_turned"), sem("pe_cols_set"))
        split_hi, split_lo = sem("split_hi"), sem("split_lo")
        q_set, keys_set, blocks_set, blh_set, bll_set = (
            sem("q_set"), sem("keys_set"), sem("blocks_set"), sem("blh_set"), sem("bll_set"))
        gelu_set, kc_set, vc_set, fox_set, logits_set, lexp_set, lln_set, logf_set, fcum_set = (
            sem("gelu_set"), sem("kc_set"), sem("vc_set"), sem("fox_set"), sem("logits_set"), sem("lexp_set"),
            sem("lln_set"), sem("logf_set"), sem("fcum_set"))
        cs_ready, cs_exp, cs_prob, pct_turned, pct_set, cs_sub = (
            sem("cs_ready"), sem("cs_exp"), sem("cs_prob"), sem("pct_turned"), sem("pct_set"), sem("cs_sub"))
        s_ready, s_taken, negmax_set, exp_done, norm_set, p_scaled = (
            sem("s_ready"), sem("s_taken"), sem("negmax_set"), sem("exp_done"), sem("norm_set"), sem("p_scaled"))
        pt_ready, pt_copied, o_ready, y_hi, y_lo = (
            sem("pt_ready"), sem("pt_copied"), sem("o_ready"), sem("y_hi"), sem("y_lo"))
        sig_set, merged_set = sem("sig_set"), sem("merged_set")
        var_set, std_set, x_set, y_full = sem("var_set"), sem("std_set"), sem("x_set"), sem("y_full")
        act_h, h_set, hT_hi, hT_lo = sem("act_h"), sem("h_set"), sem("hT_hi"), sem("hT_lo")
        out_done = sem("out_done")
        router_in, router_hi, router_lo = sem("router_in"), sem("router_hi"), sem("router_lo")
        top_set, texp_set, picks_set, routed, flag_set = (
            sem("top_set"), sem("texp_set"), sem("picks_set"), sem("routed"), sem("flag_set"))

        route = pbuf[:, 2, :, :].rearrange("p a b -> p (a b)")

        def routing(at, n, width):
            return route[:, at:at + n * width].rearrange("p (t e) -> p t e", t=n)

        r_logits, r_top, r_index = routing(0, 2, NE), routing(16, 2, 8), routing(32, 2, 8)
        r_indexf, r_one, r_two, r_mask = routing(48, 2, 8), routing(64, 2, NE), routing(80, 2, NE), routing(96, 2, NE)
        r_gate, r_slot = routing(112, 2, NE + 1), routing(130, 2, NE + 1)
        r_w = route[:, 148:156].rearrange("p (a t) -> p a t", t=2)
        r_count, r_gs = route[:, 156:157], route[:, 157:158]
        pick = pbuf[:, 0, :, 0:P]
        rout = small[:, 0:KD * NE]
        rout_h = hTh[:, 0, 0:KD * NE]
        rout_l = hTl[:, 0, 0:KD * NE]
        pickT = xTh[:, 0, :]
        xeh = yTh[:, 0:4, :].rearrange("p a b -> p (a b)")
        xel = yTl[:, 0:4, :].rearrange("p a b -> p (a b)")
        yeh = yTh[:, 4:8, :].rearrange("p a b -> p (a b)")
        yel = yTl[:, 4:8, :].rearrange("p a b -> p (a b)")
        acc = merged

        class Pass:

            def __init__(self, p):
                def own(name):
                    return sem(f"{name}_pass{p}")
                self.p = p
                if p == 0:
                    self.u0, self.raw_in, self.hi_ready, self.lo_ready, self.unit_used = (
                        len(units), raw_in, hi_ready, lo_ready, unit_used)
                else:
                    self.u0, self.raw_in = RAW, [own(f"raw_in{i}") for i in range(RAW)]
                    self.hi_ready, self.lo_ready, self.unit_used = own("hi_ready"), own("lo_ready"), own("unit_used")
                self.pick_set, self.pt_full, self.pt_set = own("pick_set"), own("pt_full"), own("pt_set")
                self.xe_full, self.xe_hi, self.xe_lo = own("xe_full"), own("xe_hi"), own("xe_lo")
                self.act_h, self.h_set, self.hT_full = own("act_h"), own("h_set"), own("hT_full")
                self.hT_hi, self.hT_lo = own("hT_hi"), own("hT_lo")
                self.ye_hi, self.ye_lo = own("ye_hi"), own("ye_lo")
                self.sum_full, self.sum_taken = own("sum_full"), own("sum_taken")

        passes = [Pass(0), Pass(1)]
        slots_moved = sem("slots_moved")
        EU = len(moe_units)
        CH = len(chunks(FE))
        FT = CHUNK // P

        hTh1 = hTh[:, 0:2, :].rearrange("p a b -> p (a b)")
        hTl1 = hTl[:, 0:2, :].rearrange("p a b -> p (a b)")

        def sum_bank(k):
            return (1, 3, 6, 7)[k]

        block = ctx.enter_context(nc.Block())

        def unit_view(buf, slot, nk, width):
            return buf[:, slot, 0:nk * width].rearrange("p (k n) -> p k n", k=nk)

        N_ATT = 2 * NH + FH
        SMALL = 4
        NLN = 2
        NSPLIT = 6

        def att_step(u):
            if u < 2 * NH:
                i, r = divmod(u, 4)
                return "nsa", r // 2, i + (NH // NKV) * (r % 2)
            i, t = divmod(u - 2 * NH, 2)
            return "fox", t, i

        def norm_col(u):
            return stats[:, u % 2, 8:10]

        def scores_at(u, nk):
            kind, t, a = att_step(u)
            if kind == "nsa":
                return free(ps[:, 4 + a // 4, 0:1], [[SEQ, 2], [1, nk]])
            return free(ps[:, 4, (u % 2) * SEQ:(u % 2) * SEQ + 1], [[512, 2], [1, nk]])

        @block.sync
        def _(sp):
            sp.dma_start(x[:, :, :], io["x"][0].rearrange("(t p) n -> p t n", p=P)).then_inc(x_in, 16)
            sp.dma_start(table[:, :], io["table"]).then_inc(const_in, 16)
            for n, (nk, width, src) in enumerate(units):
                wait(sp, lo_ready, n - RAW + 1)
                sp.dma_start(unit_view(raw, n % RAW, nk, width), src).then_inc(raw_in[n % RAW], 16)
                if stop and n == stop.get("units", 10 ** 9) - 1:
                    break

            def experts(S):
                with sp.Fori(0, NE) as e:
                    for k, u in enumerate(moe_units):
                        n = S.u0 + k
                        nk, width, src = ffn_unit(*(io[f"moe_w_{w}"][0, 0] for w in ("gate", "up", "down")), FE, *u)
                        start = sp.snap(e * (FE * D) + src.offset)
                        src = bass.AP(tensor=src.tensor, offset=start, ap=[list(d) for d in src.ap])
                        need = sp.snap(e * EU + (n - RAW + 1))
                        sp.wait_ge(S.lo_ready, need)
                        sp.dma_start(unit_view(raw, n % RAW, nk, width), src).then_inc(S.raw_in[n % RAW], 16)

            if not stop:
                experts(passes[0])
                sp.wait_ge(flag_set, 1)
                again = sp.value_load(flag[0:1, 0:1], min_val=0, max_val=1)
                with sp.If(again == 1):
                    sp.wait_ge(lo_ready, len(units) + NE * EU)
                    experts(passes[1])
            last = stop["x_set"] if stop else 4 * TT
            sp.wait_ge(x_set, last)
            sp.dma_start(io["out"][0].rearrange("(t p) n -> p t n", p=P), x[:, :, :]).then_inc(out_done, 16)
            sp.wait_ge(out_done, 16)

        @block.gpsimd
        def _(pool):
            pool.dma_start(onehot, io["onehot"]).then_inc(onehot_in, 16)
            pool.dma_start(tab[0:BUCKETS, :], io["rel_bias"]).then_inc(onehot_in, 16)

            def small_loads(L):
                if L:
                    pool.wait_ge(y_lo, N_ATT * L)
                pool.dma_start(pe_rows[:, :],
                               io["nsa_cmp_pe"][L].rearrange("v l d -> (v l d)").rearrange("(r n) -> r n", n=P)
                               ).then_inc(small_in, 16)
                pool.dma_start(cmpw2[:, :, :], io["nsa_cmp_w2"][L].rearrange("v p d -> p v d")).then_inc(small_in, 16)
                pool.dma_start(fbias[:, :], io["fox_f_bias"][L].partition_broadcast(P)).then_inc(small_in, 16)

            def norm_loads(L, which):
                wait(pool, x_set, TT * (NLN * L + which))
                pool.dma_start(lng[:, 0, :], io[f"ln{which + 1}_g"][L].partition_broadcast(P)).then_inc(lng_in, 16)
                pool.dma_start(lng[:, 1, :], io[f"ln{which + 1}_b"][L].partition_broadcast(P)).then_inc(lng_in, 16)

            def attention(L):
                for u in range(N_ATT):
                    t = att_step(u)[1]
                    nk = P * (t + 1)
                    pool.wait_ge(norm_set, N_ATT * L + u + 1)
                    pu = pbuf[:, u % 3, :, 0:nk]
                    pool.tensor_tensor(pu, pu, free(norm_col(u), [[1, 2], [0, nk]]), ALU.mult).then_inc(p_scaled, 1)

            small_loads(0)
            pool.wait_ge(vrow_set, 1)
            pool.dma_start(scratch.rearrange("p h n -> h p n"), free(vrow, [[0, P], [1, OH_DOWN]])
                           ).then_inc(vrow_out, 16)
            pool.wait_ge(vrow_out, 16)
            pool.dma_start(toep[:, :, :], bass.AP(tensor=scratch.tensor, offset=scratch.offset + P - 1,
                                                  ap=[[NH * OH_DOWN - 1, P], [OH_DOWN, NH], [1, SEQ]])).then_inc(toep_in, 16)
            norm_loads(0, 0)
            attention(0)
            small_loads(1)
            norm_loads(0, 1)
            if stop and stop["x_set"] <= 4:
                return
            norm_loads(1, 0)
            attention(1)
            pool.wait_ge(y_lo, 2 * N_ATT)
            pool.dma_start(rout.rearrange("p (k e) -> p k e", k=KD),
                           io["moe_router"][0].rearrange("(k p) e -> p k e", p=P)).then_inc(router_in, 16)
            norm_loads(1, 1)

        @block.tensor
        def _(pe):
            unit, step = Tally(), [Tally(), Tally()]

            def next_unit():
                nk, width, _ = units[unit.n]
                pe.wait_ge(lo_ready, unit.at(1))
                s = unit.n % CONV
                return nk, unit_view(hi, s, nk, width), unit_view(lo, s, nk, width)

            def used(mm):
                mm.then_inc(unit_used, 1)
                unit.n += 1

            def claim(pair):
                wait(pe, pair_free[pair], step[pair].at())

            def full(mm, pair):
                mm.then_inc(pair_full[pair], 1)
                step[pair].n += 1

            def three(out, stat_h, stat_l, mov_h, mov_l, start, stop_):
                pe.matmul(out, stat_h, mov_h, start=start, stop=False, skip_group_check=True)
                pe.matmul(out, stat_h, mov_l, start=False, stop=False, skip_group_check=True)
                return pe.matmul(out, stat_l, mov_h, start=False, stop=stop_, skip_group_check=True)

            def project(outs, pair, k_units):
                claim(pair)
                k = 0
                for un in range(k_units):
                    nk, wh, wl = next_unit()
                    for j in range(nk):
                        last = un == k_units - 1 and j == nk - 1
                        for out, kind, c0, a, first in outs:
                            start = first and k == 0
                            if kind == "T":
                                mm = three(out, wh[:, j, c0:c0 + P], wl[:, j, c0:c0 + P],
                                           xTh[:, k, :], xTl[:, k, :], start, last)
                            else:
                                xs = slice(kind * P, kind * P + P)
                                mm = three(out, xTh[:, k, xs], xTl[:, k, xs],
                                           wh[:, j, c0:c0 + a], wl[:, j, c0:c0 + a], start, last)
                        k += 1
                    used(mm)
                step[pair].n += 1

            def turn(src):
                for pair in range(2):
                    claim(pair)
                    for k in range(4 * pair, 4 * pair + 4):
                        for t in range(TT):
                            mm = pe.transpose(ps[:, k // 2, (k % 2) * SEQ + t * P:(k % 2) * SEQ + (t + 1) * P],
                                              src[:, t, k * P:(k + 1) * P], ident)
                    full(mm, pair)

            def mixer(L):
                pe.wait_ge(split_lo, NSPLIT * L + 2)
                project([(ps[:, b // 2, (b % 2) * SEQ:(b % 2 + 1) * SEQ], "T", b * P, 0, b % 2 == 0)
                         for b in range(4)], 0, 2)
                project([(ps[:, 2 + v, 0:SEQ], "T", v * P, 0, True) for v in range(2)], 1, 1)
                for w, (wide, n) in enumerate(((P, 1), (P + NG, 2))):
                    project([(ps[:, 2 * w, 0:SEQ], "T", 0, 0, True)]
                            + [(ps[:, 2 * w + 1, t * SEQ:t * SEQ + wide], t, P, wide, t == 0) for t in range(2)], w, n)
                claim(0)
                pe.wait_ge(bll_set, L + 1)
                for v in range(2):
                    nk, wh, wl = next_unit()
                    for m in range(nk):
                        mm = three(ps[:, v, 0:2 * NCP], wh[:, m, :], wl[:, m, :], blh[:, v, m, :], bll[:, v, m, :],
                                   m == 0, m == nk - 1)
                    used(mm)
                step[0].n += 1
                project([(ps[:, 2 + b // 2, (b % 2) * SEQ:(b % 2 + 1) * SEQ], "T", b * P, 0, b % 2 == 0)
                         for b in range(4)], 1, 2)
                claim(0)
                pe.wait_ge(gelu_set, L + 1)
                pe.wait_ge(small_in, 16 * 3 * (L + 1))
                for g in range(NKV):
                    pe.matmul(ps[g * DH:(g + 1) * DH, 0, 0:NCP], cmpw2[:, 0, :], gkT[:, g * NCP:(g + 1) * NCP],
                              start=True, stop=True)
                mm = pe.matmul(ps[:, 1, 0:DH], gvT, cmpw2[:, 1, :], start=True, stop=True)
                full(mm, 0)
                project([(ps[:, 2 + b // 2, (b % 2) * SEQ:(b % 2 + 1) * SEQ], "T", b * P, 0, b % 2 == 0)
                         for b in range(4)], 1, 2)
                project([(ps[:, 0, t * SEQ:(t + 1) * SEQ], t, 0, 256, t == 0) for t in range(2)], 0, 1)
                project([(ps[:, 2 + t, 0:256 + FH], t, 0, 256 + FH, True) for t in range(2)], 1, 2)
                claim(0)
                pe.wait_ge(logf_set, L + 1)
                for t in range(TT):
                    for j in range(t + 1):
                        mm = pe.matmul(ps[:, 0, t * FH:(t + 1) * FH], tri[:, (t - j) * P:(t - j + 1) * P],
                                       logf[:, 2, j, :], start=(t == 0), stop=(j == t), skip_group_check=True)
                full(mm, 0)
                claim(1)
                pe.wait_ge(kc_set, L + 1)
                pe.wait_ge(q_set, L + 1)
                for t in range(TT):
                    for hd in range(NH):
                        g, i = divmod(hd, NH // NKV)
                        b = DH * g
                        at = t * 64 + i * NCP
                        mm = pe.matmul(ps[:, 2 + g, at:at + NCP], qk[b:b + DH, i, t * P:(t + 1) * P],
                                       kcT[b:b + DH, :], start=True, stop=True)
                full(mm, 1)
                attention(L)
                for half in range(2):
                    for g in range(2):
                        project([(ps[:, 2 * g + t, :], t, 0, 512, True) for t in range(2)], g, 2)
                    for g in range(2):
                        claim(g)
                        nk, wh, wl = next_unit()
                        for t in range(TT):
                            for j in range(nk):
                                k = 4 * g + j
                                mm = three(ps[:, 2 * g + t, :], yTh[:, k, t * P:(t + 1) * P],
                                           yTl[:, k, t * P:(t + 1) * P], wh[:, j, :], wl[:, j, :], j == 0, j == nk - 1)
                        used(mm)
                        step[g].n += 1
                pe.wait_ge(merged_set, 2 * (L + 1))
                turn(merged)
                pe.wait_ge(split_lo, NSPLIT * L + 4)
                for half in range(2):
                    project([(ps[:, 2 * half + t, :], t, 0, 512, True) for t in range(2)], half, 2)

            def attention(L):
                a0 = N_ATT * L

                def scores(u):
                    kind, t, a = att_step(u)
                    nk = P * (t + 1)
                    wait(pe, s_taken, a0 + u - 1)
                    if kind == "nsa":
                        g, i = divmod(a, NH // NKV)
                        b = DH * g
                        for br in range(2):
                            mm = pe.matmul(ps[:, 4 + a // 4, br * SEQ:br * SEQ + nk],
                                           qk[b:b + DH, i, t * P:(t + 1) * P], ksw[b:b + DH, br, 0:nk],
                                           start=True, stop=True)
                    else:
                        c0 = (u % 2) * SEQ
                        for hh in range(2):
                            b, head = DH * hh, 2 * a + hh
                            out = ps[:, 4 + hh, c0:c0 + nk]
                            pe.matmul(out, qk[b:b + DH, 4 + a, t * P:(t + 1) * P], fkT[b:b + DH, a, 0:nk],
                                      start=True, stop=False, skip_group_check=True)
                            for j in range(t + 1):
                                mm = pe.matmul(ps[:, 4 + hh, c0 + j * P:c0 + nk],
                                               free(logf[:, 3, j, head:head + 1], [[0, P]]), tri[:, 0:nk - j * P],
                                               start=False, stop=(j == t), skip_group_check=True)
                    mm.then_inc(s_ready, 1)

                def turn_probs(u):
                    t = att_step(u)[1]
                    pe.wait_ge(p_scaled, a0 + u + 1)
                    wait(pe, pt_copied, a0 + u - 1)
                    for br in range(2):
                        for j in range(t + 1):
                            c = (br * (t + 1) + j) * P
                            mm = pe.transpose(ps[:, 6 + u % 2, c:c + P], pbuf[:, u % 3, br, j * P:(j + 1) * P], ident)
                    mm.then_inc(pt_ready, 1)

                def values(u):
                    kind, t, a = att_step(u)
                    pe.wait_ge(pt_copied, a0 + u + 1)
                    wait(pe, y_lo, a0 + u - 1)
                    for br in range(2):
                        b = DH * (a // 4 if kind == "nsa" else br)
                        out = ps[b:b + DH, u % 2, 0:P]
                        for j in range(t + 1):
                            c = (br * (t + 1) + j) * P
                            if kind == "nsa":
                                g = a // (NH // NKV)
                                mm = pe.matmul(out, vsw[:, br, j, g * DH:(g + 1) * DH], ptb[:, u % 2, c:c + P],
                                               start=(br == 0 and j == 0), stop=False, skip_group_check=True)
                            else:
                                head = 2 * a + br
                                mm = pe.matmul(out, fv[:, j, head * DH:(head + 1) * DH], ptb[:, u % 2, c:c + P],
                                               start=(j == 0), stop=(j == t), skip_group_check=True)
                    if kind == "nsa":
                        mm = pe.matmul(out, vcb[:, a, :], pct[:, t * P:(t + 1) * P],
                                       start=False, stop=True, skip_group_check=True)
                    mm.then_inc(o_ready, 1)

                pe.wait_ge(keys_set, 2 * (L + 1))
                scores(0)
                pe.wait_ge(cs_prob, L + 1)
                wait(pe, pt_copied, a0)
                for t in range(TT):
                    mm = pe.transpose(ps[:, 6, t * P:(t + 1) * P],
                                      pbuf[:, 1, :, :].rearrange("p a b -> p (a b)")[:, t * P:(t + 1) * P], ident)
                mm.then_inc(pct_turned, 1)
                pe.wait_ge(pct_set, L + 1)
                pe.wait_ge(vc_set, L + 1)
                claim(0)
                for u in range(N_ATT):
                    if u + 1 < N_ATT:
                        if u + 1 == 2 * NH:
                            pe.wait_ge(fox_set, 3 * (L + 1))
                        scores(u + 1)
                    turn_probs(u)
                    if u:
                        values(u - 1)
                values(N_ATT - 1)
                pe.wait_ge(y_lo, a0 + N_ATT)

            def dense_ffn(names):
                ws = chunks(FF)

                def down(c):
                    pe.wait_ge(hT_lo, names["h0"] + c + 1)
                    kt = ws[c] // P
                    for i in range(down_units(ws[c])):
                        nk, wh, wl = next_unit()
                        for j in range(nk):
                            k = 2 * i + j
                            for t in range(TT):
                                for half in range(2):
                                    cs_ = slice(half * 512, (half + 1) * 512)
                                    mm = three(ps[:, 4 + 2 * t + half, :], hTh[:, k, t * P:(t + 1) * P],
                                               hTl[:, k, t * P:(t + 1) * P], wh[:, j, cs_], wl[:, j, cs_],
                                               c == 0 and k == 0, c == len(ws) - 1 and k == kt - 1)
                        used(mm)

                for c, width in enumerate(ws):
                    for g in range(2):
                        project([(ps[:, 2 * g + t, 0:width], t, 0, width, True) for t in range(2)], g, 2)
                    if c:
                        down(c - 1)
                    claim(1)
                    pe.wait_ge(h_set, names["h0"] + c + 1)
                    for f in range(width // P):
                        for t in range(TT):
                            a = (f % 2) * SEQ + t * P
                            mm = pe.transpose(ps[:, 2 + f // 2, a:a + P], h[:, t, f * P:(f + 1) * P], ident)
                    full(mm, 1)
                down(len(ws) - 1)

            pe.wait_ge(tab_set, 1)
            pe.wait_ge(onehot_in, 32)
            claim(0)
            mm = pe.matmul(ps[0:NH, 0, 0:OH_DOWN], tab, onehot[:, 0:OH_DOWN], start=True, stop=True)
            full(mm, 0)
            claim(1)
            for t in range(TT):
                for c in range(NCP):
                    a = OH_DOWN + OH_UP0 + t * P - (c * CMP_STRIDE + CMP_BLOCK - 1)
                    mm = pe.matmul(ps[:, 2 + t, c * NH:(c + 1) * NH], onehot[:, a:a + P], tab, start=True, stop=True)
            full(mm, 1)

            def turn_pe():
                claim(0)
                pe.wait_ge(small_in, 16 * 3 * (turn_pe.n + 1))
                turn_pe.n += 1
                full(pe.transpose(ps[:, 0, 0:32], pe_rows[:, :], ident[0:32, 0:32]), 0)
            turn_pe.n = 0

            pe.wait_ge(const_in, 16)
            pe.wait_ge(x_in, 16)
            turn_pe()
            turn(x)
            mixer(0)
            pe.wait_ge(x_set, TT)
            turn(x)
            pe.wait_ge(split_lo, 6)
            if stop and stop["x_set"] <= 2:
                return
            dense_ffn({"h0": 0})
            turn_pe()
            pe.wait_ge(x_set, 2 * TT)
            turn(x)
            if stop and stop["x_set"] <= 4:
                return
            mixer(1)
            pe.wait_ge(x_set, 3 * TT)
            turn(x)
            pe.wait_ge(split_lo, 12)
            pe.wait_ge(router_lo, 1)
            claim(0)
            for t in range(TT):
                for k in range(KD):
                    es = slice(k * NE, (k + 1) * NE)
                    mm = three(ps[:, t, 0:NE], xTh[:, k, t * P:(t + 1) * P], xTl[:, k, t * P:(t + 1) * P],
                               rout_h[:, es], rout_l[:, es], k == 0, k == KD - 1)
            full(mm, 0)
            claim(1)
            pe.wait_ge(picks_set, 1)
            before, ones = table[:, K_SU:K_SU + P], table[:, K_ONE:K_ONE + P]
            for at, lhs in ((0, (before,)), (NE, (ones, before)), (2 * NE, (ones, ones))):
                for j, m in enumerate(lhs):
                    mm = pe.matmul(ps[:, 2, at:at + NE], m, r_mask[:, j, :], start=(at == 0), stop=(j == len(lhs) - 1),
                                   skip_group_check=True)
            full(mm, 1)

            claim(0)
            claim(1)

            def experts(S):
                unit = Tally(S.u0)

                def gather():
                    for k in range(KD):
                        for t in range(TT):
                            mm = pe.matmul(ps[:, 6 + k // 4, (k % 4) * P:(k % 4 + 1) * P], x[:, t, k * P:(k + 1) * P],
                                           pick[:, t, :], start=(t == 0), stop=(t == TT - 1), skip_group_check=True)
                    mm.then_inc(S.xe_full, 1)

                def take(nk, width):
                    pe.wait_ge(S.lo_ready, unit.at(1))
                    s = unit.n % CONV
                    return unit_view(hi, s, nk, width), unit_view(lo, s, nk, width)

                def leave_unit(mm):
                    mm.then_inc(S.unit_used, 1)
                    unit.n += 1

                def gate_or_up(bank):
                    for i in range(2):
                        wh, wl = take(KD // 2, CHUNK)
                        for j in range(KD // 2):
                            k = i * KD // 2 + j
                            mm = three(ps[:, bank, :], xeh[:, k * P:(k + 1) * P], xel[:, k * P:(k + 1) * P],
                                       wh[:, j, :], wl[:, j, :], k == 0, k == KD - 1)
                        leave_unit(mm)

                def down(e, c):
                    pe.wait_ge(S.hT_lo, e * CH + (c + 2))
                    for i in range(FT // 2):
                        wh, wl = take(2, D)
                        for j in range(2):
                            k = 2 * i + j
                            for half in range(2):
                                cols = slice(half * 512, (half + 1) * 512)
                                mm = three(ps[:, 4 + half, :], hTh1[:, k * P:(k + 1) * P], hTl1[:, k * P:(k + 1) * P],
                                           wh[:, j, cols], wl[:, j, cols], c == 0 and k == 0,
                                           c == CH - 1 and k == FT - 1)
                        leave_unit(mm)

                if S.p:
                    pe.wait_ge(passes[0].sum_taken, 4 * (NE + 1))
                    pe.nop().then_inc(S.unit_used, RAW)
                pe.wait_ge(S.pick_set, 1)
                gather()
                with pe.Fori(0, NE) as e:
                    unit.enter(e, EU)
                    pe.wait_ge(S.sum_taken, e * 4 + 1)
                    for t in range(TT):
                        pe.transpose(ps[:, 1, t * P:(t + 1) * P], pick[:, t, :], ident)
                    for t in range(TT):
                        mm = pe.matmul(ps[:, 1, SEQ:SEQ + 1], pick[:, t, :], r_gate[:, t, bass.ds(e, 1)],
                                       start=False, stop=(t == TT - 1), skip_group_check=True)
                    mm.then_inc(S.pt_full, 1)
                    pe.wait_ge(S.xe_lo, e + 1)
                    for c in range(CH):
                        pe.wait_ge(S.act_h, e * CH + (c + 1))
                        gate_or_up(0)
                        pe.wait_ge(S.hT_lo, e * CH + (c + 1))
                        gate_or_up(2)
                        if c == 1:
                            pe.wait_ge(S.ye_lo, e + 1)
                        if c:
                            down(e, c - 1)
                        pe.wait_ge(S.h_set, e * CH + (c + 1))
                        for f in range(FT):
                            mm = pe.transpose(ps[:, 2, f * P:(f + 1) * P], h[:, 0, f * P:(f + 1) * P], ident)
                        mm.then_inc(S.hT_full, 1)
                    pe.wait_ge(S.pick_set, e + 2)
                    pe.wait_ge(S.sum_taken, e * 4 + 4)
                    gather()
                    down(e, CH - 1)
                    pe.wait_ge(S.ye_lo, e + 2)
                    pe.wait_ge(S.xe_lo, e + 2)
                    for k in range(4):
                        t, half = divmod(k, 2)
                        out, cols = ps[:, sum_bank(k), :], slice(half * 512, (half + 1) * 512)
                        pe.matmul(out, pickT[:, t * P:(t + 1) * P], yeh[:, cols], start=True, stop=False)
                        pe.matmul(out, pickT[:, t * P:(t + 1) * P], yel[:, cols], start=False, stop=True)\
                          .then_inc(S.sum_full, 1)
                    unit.leave(NE)

            experts(passes[0])
            pe.wait_ge(flag_set, 1)
            again = pe.value_load(flag[0:1, 0:1], min_val=0, max_val=1)
            with pe.If(again == 1):
                experts(passes[1])

        AHEAD = 2

        @block.scalar
        def _(act):
            unit, use = Tally(), [Tally(), Tally()]

            def convert_to(n):
                while unit.n < min(n, len(units)):
                    nk, width, _ = units[unit.n]
                    size = nk * width
                    act.wait_ge(raw_in[unit.n % RAW], 16 * (unit.n // RAW + 1))
                    wait(act, unit_used, unit.n - CONV + 1)
                    act.activation(hi[:, unit.n % CONV, 0:size], raw[:, unit.n % RAW, 0:size], ACT.Copy
                                   ).then_inc(hi_ready, 1)
                    unit.n += 1

            def is_full(pair):
                use[pair].n += 1
                act.wait_ge(pair_full[pair], use[pair].at())

            def projected(n):
                act.wait_ge(unit_used, n)

            chain = Tally()

            def link(ins):
                chain.n += 1
                ins.then_inc(act_step, 1)
                act.wait_ge(act_step, chain.at())

            def pair(i):
                return ps[:, 2 * i:2 * i + 2, :].rearrange("p a b -> p (a b)")

            splits = Tally()

            def split_turned(pt):
                is_full(pt)
                act.activation(xTh[:, 4 * pt:4 * pt + 4, :].rearrange("p a b -> p (a b)"), pair(pt), ACT.Copy
                               ).then_inc(split_hi, 1)

            def mixer(L, u0):
                convert_to(u0 + 2 + AHEAD)
                projected(u0 + 2)
                act.activation(qk[:, 0:4, :].rearrange("p a b -> p (a b)"), pair(0), ACT.Copy, scale=SCALE)\
                   .then_inc(q_set, 1)
                act.wait_ge(q_set, L + 1)
                act.nop().then_inc(pair_free[0], 1)
                convert_to(u0 + 3 + AHEAD)
                projected(u0 + 4)
                act.activation(ksw[:, 0, :], ps[:, 0, 0:SEQ], ACT.Copy)
                act.activation(vsw[:, 0, :, :], free(ps[:, 1, 0:1], [[SEQ, 2], [1, P]]), ACT.Copy)\
                   .then_inc(pair_free[0], 1)
                act.wait_ge(blocks_set, L + 1)
                act.activation(yTh[:, 0:4, :].rearrange("p a b -> p (a b)"),
                               blocks[:, :, :, :].rearrange("p v m n -> p (v m n)"), ACT.Copy).then_inc(blh_set, 1)
                convert_to(u0 + 6 + AHEAD)
                projected(u0 + 6)
                act.activation(ksw[:, 1, :], ps[:, 2, 0:SEQ], ACT.Copy)
                act.activation(vsw[:, 1, :, :], free(ps[:, 3, 0:1], [[SEQ, 2], [1, P]]), ACT.Copy)\
                   .then_inc(keys_set, 1)
                act.activation(gates[:, :, :], free(ps[:, 3, P:P + 1], [[SEQ, 2], [1, NG]]), ACT.Sigmoid)\
                   .then_inc(keys_set, 1)
                act.wait_ge(keys_set, 2 * (L + 1))
                act.nop().then_inc(pair_free[1], 1)
                convert_to(u0 + 8 + AHEAD)
                projected(u0 + 8)
                act.activation(gkT, ps[:, 0, 0:2 * NCP], ACT.Gelu_apprx_tanh)
                act.activation(gvT.rearrange("p (g i c) -> p g i c", g=2, i=4),
                               free(ps[:, 1, 0:1], [[NCP, 2], [0, 4], [1, NCP]]), ACT.Gelu_apprx_tanh)\
                   .then_inc(gelu_set, 1)
                act.wait_ge(gelu_set, L + 1)
                act.nop().then_inc(pair_free[0], 1)
                convert_to(u0 + 10 + AHEAD)
                projected(u0 + 10)
                act.activation(qk[:, 4:8, :].rearrange("p a b -> p (a b)"), pair(1), ACT.Copy, scale=SCALE)\
                   .then_inc(fox_set, 1)
                act.wait_ge(fox_set, 3 * L + 1)
                act.nop().then_inc(pair_free[1], 1)
                is_full(0)
                act.activation(kcT, ps[:, 0, 0:NCP], ACT.Copy).then_inc(kc_set, 1)
                convert_to(u0 + 12 + AHEAD)
                projected(u0 + 12)
                act.activation(kv[:, 0:4, :].rearrange("p a b -> p (a b)"), pair(1), ACT.Copy).then_inc(fox_set, 1)
                act.wait_ge(fox_set, 3 * L + 2)
                act.nop().then_inc(pair_free[1], 1)
                convert_to(u0 + 13 + AHEAD)
                projected(u0 + 13)
                act.activation(fv[:, :, 0:256], free(ps[:, 0, 0:1], [[SEQ, 2], [1, 256]]), ACT.Copy)\
                   .then_inc(pair_free[0], 1)
                convert_to(u0 + 15 + AHEAD)
                projected(u0 + 15)
                act.activation(fv[:, :, 256:512], free(ps[:, 2, 0:1], [[512, 2], [1, 256]]), ACT.Copy)\
                   .then_inc(fox_set, 1)
                act.wait_ge(logits_set, L + 1)
                act.activation(logf[:, 1, :, :], logf[:, 1, :, :], ACT.Exp, scale=-1.0).then_inc(lexp_set, 1)
                act.wait_ge(lexp_set, L + 1)
                act.activation(logf[:, 1, :, :], logf[:, 1, :, :], ACT.Ln, bias=1.0).then_inc(lln_set, 1)
                use[0].n += 1
                use[1].n += 1
                act.wait_ge(cs_sub, L + 1)
                act.activation(cs[:, 0:256], cs[:, 0:256], ACT.Exp).then_inc(cs_exp, 1)
                convert_to(u0 + 15 + 3)
                attention(L)
                m0 = u0 + 15
                for half in range(2):
                    for g in range(2):
                        convert_to(m0 + 6 * half + 2 * g + 2 + AHEAD)
                        projected(m0 + 6 * half + 2 * g + 2)
                        act.activation(sig[:, g, :, :].rearrange("p t n -> p (t n)"), pair(g), ACT.Sigmoid)\
                           .then_inc(sig_set, 1)
                        act.wait_ge(sig_set, 4 * L + 2 * half + g + 1)
                        act.nop().then_inc(pair_free[g], 1)
                    convert_to(m0 + 6 * half + 6 + AHEAD)
                    act.wait_ge(merged_set, 2 * L + half + 1)
                for pt in range(2):
                    split_turned(pt)
                convert_to(m0 + 12 + 4)
                norm(L * NLN)
                for pt in range(2):
                    split_turned(pt)

            def attention(L):
                a0 = N_ATT * L
                def exps(u):
                    t = att_step(u)[1]
                    nk = P * (t + 1)
                    act.wait_ge(negmax_set, a0 + u + 1)
                    wait(act, pt_ready, a0 + u - 2)
                    for br in range(2):
                        ins = act.activation(pbuf[:, u % 3, br, 0:nk], pbuf[:, u % 3, br, 0:nk], ACT.Exp,
                                             bias=stats[:, u % 2, br:br + 1],
                                             accum_out=stats[:, u % 2, 4 + br:5 + br])
                    ins.then_inc(exp_done, 1)

                def copy_probs(u):
                    t = att_step(u)[1]
                    n = 2 * (t + 1) * P
                    act.wait_ge(pt_ready, a0 + u + 1)
                    wait(act, o_ready, a0 + u - 1)
                    act.activation(ptb[:, u % 2, 0:n], ps[:, 6 + u % 2, 0:n], ACT.Copy).then_inc(pt_copied, 1)

                def out_hi(u):
                    kind, t, a = att_step(u)
                    act.wait_ge(o_ready, a0 + u + 1)
                    b, n = (DH * (a // 4), DH) if kind == "nsa" else (0, P)
                    k = a % 4 if kind == "nsa" else 4 + a
                    act.activation(yTh[b:b + n, k, t * P:(t + 1) * P], ps[b:b + n, u % 2, 0:P], ACT.Copy)\
                       .then_inc(y_hi, 1)

                act.wait_ge(pct_turned, L + 1)
                act.activation(pct, ps[:, 6, 0:256], ACT.Copy).then_inc(pct_set, 1)
                exps(0)
                for u in range(N_ATT):
                    if u + 1 < N_ATT:
                        exps(u + 1)
                    copy_probs(u)
                    if u:
                        out_hi(u - 1)
                out_hi(N_ATT - 1)

            def norm(n):
                for t in range(TT):
                    act.wait_ge(var_set, TT * n + t + 1)
                    act.activation(stats[:, t, 14:15], stats[:, t, 13:14], ACT.Sqrt, bias=eps[:, 0:1])\
                       .then_inc(std_set, 1)

            def dense_ffn(u0, n_norm):
                ws = chunks(FF)
                at = u0
                for c, width in enumerate(ws):
                    convert_to(at + 2 + AHEAD)
                    projected(at + 2)
                    at += 4
                    for t in range(TT):
                        ins = act.activation(h[:, t, 0:width], ps[:, t, 0:width], ACT.Silu)
                    ins.then_inc(act_h, 1)
                    if c:
                        at += down_units(ws[c - 1])
                    convert_to(at + AHEAD)
                    is_full(1)
                    act.activation(hTh[:, 0:width // P, :].rearrange("p a b -> p (a b)"), pair(1)[:, 0:2 * width], ACT.Copy)\
                       .then_inc(hT_hi, 1)
                at += down_units(ws[-1])
                convert_to(at)
                norm(n_norm)
                return at

            act.wait_ge(eps_set, 1)
            is_full(0)
            act.activation(vrow, ps[0:NH, 0, 0:OH_DOWN], ACT.Copy).then_inc(vrow_set, 1)
            act.wait_ge(vrow_set, 1)
            act.nop().then_inc(pair_free[0], 1)
            is_full(1)
            for t in range(TT):
                for hp in range(2):
                    ins = act.activation(cbias[:, hp, t * 64:(t + 1) * 64].rearrange("p (i c) -> p i c", c=NCP),
                                         free(ps[:, 2 + t, 4 * hp:4 * hp + 1], [[1, 4], [NH, NCP]]), ACT.Copy)
            ins.then_inc(pair_free[1], 1)

            def pe_columns():
                is_full(0)
                act.activation(pe_cols[:, :, :].rearrange("p v m -> p (v m)"), ps[:, 0, 0:32], ACT.Copy)\
                   .then_inc(pe_cols_set, 1)
                act.wait_ge(pe_cols_set, pe_columns.n + 1)
                pe_columns.n += 1
                act.nop().then_inc(pair_free[0], 1)
            pe_columns.n = 0

            pe_columns()
            for pt in range(2):
                split_turned(pt)
            mixer(0, 0)
            if stop and stop["x_set"] <= 2:
                return
            at = dense_ffn(31, 1)
            pe_columns()
            for pt in range(2):
                split_turned(pt)
            if stop and stop["x_set"] <= 4:
                return
            mixer(1, at)
            act.wait_ge(router_in, 16)
            act.activation(rout_h, rout, ACT.Copy).then_inc(router_hi, 1)
            act.wait_ge(top_set, 1)
            act.activation(r_w[:, 1, :], r_w[:, 0, :], ACT.Exp).then_inc(texp_set, 1)

            def experts(S):
                unit = Tally(S.u0)

                def convert_to(n):
                    while unit.n < S.u0 + min(n, EU):
                        act.wait_ge(S.raw_in[unit.n % RAW],
                                    unit.reg * (16 * EU // RAW) + 16 * (unit.n // RAW + 1 - S.p))
                        act.wait_ge(S.unit_used, unit.at(1 - CONV))
                        act.activation(hi[:, unit.n % CONV, :], raw[:, unit.n % RAW, :], ACT.Copy
                                       ).then_inc(S.hi_ready, 1)
                        unit.n += 1

                def tokens_hi(n):
                    act.wait_ge(S.xe_full, n)
                    act.activation(xeh, ps[:, 6:8, :].rearrange("p a b -> p (a b)"), ACT.Copy).then_inc(S.xe_hi, 1)

                act.nop().then_inc(S.act_h, 1)
                if S.p:
                    act.nop().then_inc(S.hi_ready, RAW)
                tokens_hi(1)
                with act.Fori(0, NE) as e:
                    unit.enter(e, EU)
                    act.wait_ge(S.pt_full, e + 1)
                    act.activation(pickT, ps[:, 1, 0:SEQ], ACT.Copy)
                    act.activation(r_gs, ps[:, 1, SEQ:SEQ + 1], ACT.Copy).then_inc(S.pt_set, 1)
                    at = 0
                    for c in range(CH):
                        convert_to(at + 2 + AHEAD)
                        act.wait_ge(S.unit_used, e * EU + (S.u0 + at + 2))
                        act.activation(h[:, 0, :], ps[:, 0, :], ACT.Silu).then_inc(S.act_h, 1)
                        at += 6 if c else 4
                        convert_to(at + AHEAD)
                        act.wait_ge(S.hT_full, e * CH + (c + 1))
                        act.activation(hTh1, ps[:, 2, :], ACT.Copy).then_inc(S.hT_hi, 1)
                    tokens_hi(e + 2)
                    convert_to(EU)
                    act.wait_ge(S.unit_used, e * EU + (S.u0 + EU))
                    act.wait_ge(S.pt_set, e + 1)
                    act.activation(yeh, ps[:, 4:6, :].rearrange("p a b -> p (a b)"), ACT.Copy, scale=r_gs)\
                       .then_inc(S.ye_hi, 1)
                    unit.leave(NE)

            experts(passes[0])
            act.wait_ge(flag_set, 1)
            again = act.value_load(flag[0:1, 0:1], min_val=0, max_val=1)
            with act.If(again == 1):
                experts(passes[1])
            norm(3)

        @block.vector
        def _(dve):
            unit, use, chain, splits = Tally(), [Tally(), Tally()], Tally(), Tally()

            def link(ins):
                chain.n += 1
                ins.then_inc(dve_step, 1)
                dve.wait_ge(dve_step, chain.at())

            def convert_to(n):
                while unit.n < min(n, len(units)):
                    nk, width, _ = units[unit.n]
                    size = nk * width
                    s = unit.n % CONV
                    dve.wait_ge(hi_ready, unit.at(1))
                    dve.tensor_tensor(lo[:, s, 0:size], raw[:, unit.n % RAW, 0:size], hi[:, s, 0:size].bitcast(F32),
                                      ALU.subtract).then_inc(lo_ready, 1)
                    unit.n += 1

            def is_full(pair):
                use[pair].n += 1
                dve.wait_ge(pair_full[pair], use[pair].at())

            def projected(n):
                dve.wait_ge(unit_used, n)

            def pair(i):
                return ps[:, 2 * i:2 * i + 2, :].rearrange("p a b -> p (a b)")

            def split_turned(pt):
                splits.n += 1
                use[pt].n += 1
                dve.wait_ge(split_hi, splits.n)
                sl = (slice(None), slice(4 * pt, 4 * pt + 4), slice(None))
                dve.tensor_tensor(xTl[sl].rearrange("p a b -> p (a b)"), pair(pt),
                                  xTh[sl].rearrange("p a b -> p (a b)").bitcast(F32), ALU.subtract)\
                   .then_inc(split_lo, 1)
                dve.wait_ge(split_lo, splits.n)
                dve.nop().then_inc(pair_free[pt], 1)

            def mixer(L, u0):
                convert_to(u0 + 3 + AHEAD)
                projected(u0 + 3)
                dve.wait_ge(pe_cols_set, L + 1)
                dve.memset(free(blocks[:, 0, 0, NC:NC + 1], [[NCP, 4 * CM]]), 0.0)
                for v in range(2):
                    for g in range(2):
                        for j in range(2):
                            src = ps[g * DH:(g + 1) * DH, 2 + v, j:j + 1]
                            ins = dve.tensor_tensor(
                                free(blocks[j * DH:(j + 1) * DH, v, 0, g * NCP:g * NCP + 1], [[2 * NCP, CM], [1, NC]]),
                                free(src, [[2, CM], [CMP_STRIDE, NC]]),
                                free(pe_cols[j * DH:(j + 1) * DH, v, 0:1], [[1, CM], [0, NC]]), ALU.add)
                link(ins)
                dve.nop().then_inc(blocks_set, 1)
                dve.nop().then_inc(pair_free[1], 1)
                convert_to(u0 + 4 + AHEAD)
                dve.wait_ge(blh_set, L + 1)
                dve.tensor_tensor(yTl[:, 0:4, :].rearrange("p a b -> p (a b)"),
                                  blocks[:, :, :, :].rearrange("p v m n -> p (v m n)"),
                                  yTh[:, 0:4, :].rearrange("p a b -> p (a b)").bitcast(F32), ALU.subtract)\
                   .then_inc(bll_set, 1)
                convert_to(u0 + 8 + AHEAD)
                convert_to(u0 + 10 + AHEAD)
                is_full(0)
                dve.wait_ge(const_in, 16)
                dve.wait_ge(kc_set, L + 1)
                link(dve.tensor_tensor(vcb[:, :, :], free(ps[:, 1, 0:1], [[0, NH], [1, DH]]),
                                       free(table[:, K_BLK:K_BLK + 1], [[1, NH], [0, DH]]), ALU.mult))
                dve.nop().then_inc(vc_set, 1)
                dve.nop().then_inc(pair_free[0], 1)
                convert_to(u0 + 12 + AHEAD)
                convert_to(u0 + 13 + AHEAD)
                convert_to(u0 + 15 + AHEAD)
                projected(u0 + 15)
                dve.wait_ge(small_in, 16 * 3 * (L + 1))
                dve.wait_ge(fox_set, 3 * (L + 1))
                link(dve.tensor_tensor(logf[:, 0, :, :], free(ps[:, 2, 256:257], [[512, 2], [1, FH]]),
                                       free(fbias[:, 0:1], [[0, 2], [1, FH]]), ALU.add))
                dve.nop().then_inc(pair_free[1], 1)
                link(dve.tensor_scalar(logf[:, 2, :, :], logf[:, 0, :, :], 0.0, None, ALU.min))
                link(dve.scalar_tensor_tensor(logf[:, 1, :, :], logf[:, 2, :, :], -2.0, logf[:, 0, :, :],
                                              ALU.mult, ALU.add))
                dve.nop().then_inc(logits_set, 1)
                dve.wait_ge(lln_set, L + 1)
                link(dve.tensor_tensor(logf[:, 2, :, :], logf[:, 2, :, :], logf[:, 1, :, :], ALU.subtract))
                link(dve.tensor_scalar(logf[:, 3, :, :], logf[:, 2, :, :], -1.0, None, ALU.mult))
                dve.nop().then_inc(logf_set, 1)
                is_full(0)
                link(dve.tensor_copy(fcum[:, :, :].rearrange("p t h -> p (t h)"), ps[:, 0, 0:TT * FH]))
                dve.nop().then_inc(pair_free[0], 1)
                is_full(1)
                c3 = cs[:, 0:256].rearrange("p (a c) -> p a c", c=NCP)
                if L:
                    dve.wait_ge(pt_ready, N_ATT * L)
                link(dve.tensor_tensor(cs[:, 0:256].rearrange("p (a b) -> p a b", a=2), ps[:, 2:4, 0:P],
                                       cbias[:, :, :], ALU.add))
                dve.nop().then_inc(pair_free[1], 1)
                link(dve.tensor_reduce(csum[:, 0, :], c3, AX, ALU.max))
                link(dve.tensor_tensor(c3, c3, free(csum[:, 0, 0:1], [[1, 16], [0, NCP]]), ALU.subtract))
                dve.nop().then_inc(cs_sub, 1)
                dve.wait_ge(cs_exp, L + 1)
                link(dve.tensor_tensor(cs[:, 0:256], cs[:, 0:256], table[:, K_VIS:K_VIS + 256], ALU.mult))
                link(dve.tensor_reduce(csum[:, 1, :], c3, AX, ALU.add))
                link(dve.tensor_scalar(csum[:, 1, :], csum[:, 1, :], 1e-30, None, ALU.max))
                link(dve.reciprocal(csum[:, 2, :], csum[:, 1, :]))
                dve.wait_ge(keys_set, 2 * (L + 1))
                link(dve.tensor_tensor(csum[:, 3, :].rearrange("p (a t i) -> p a t i", a=2, t=2),
                                       csum[:, 2, :].rearrange("p (a t i) -> p a t i", a=2, t=2),
                                       free(gates[:, 0, 0:1], [[12, 2], [NG, 2], [3, 4]]), ALU.mult))
                cp = pbuf[:, 1, :, :].rearrange("p a b -> p (a b)")
                for hp in range(2):
                    ins = dve.tensor_tensor(
                        free(cp[:, hp * 64:hp * 64 + 1], [[P, 2], [NCP, 4], [1, NCP]]),
                        c3[:, 8 * hp:8 * hp + 8, :].rearrange("p (t i) c -> p t i c", t=2),
                        free(csum[:, 3, 8 * hp:8 * hp + 1], [[4, 2], [1, 4], [0, NCP]]), ALU.mult)
                link(ins)
                dve.nop().then_inc(cs_prob, 1)
                convert_to(u0 + 15 + 3)
                attention(L)
                m0 = u0 + 15
                for half in range(2):
                    convert_to(m0 + 6 * half + 6 + AHEAD)
                    mh = merged[:, :, half * 512:(half + 1) * 512]
                    for g in range(2):
                        projected(m0 + 6 * half + 5 + g)
                        dve.wait_ge(sig_set, 4 * L + 2 * half + g + 1)
                        out = mh if g == 0 else sig[:, 1, :, :]
                        link(dve.tensor_tensor(out, ps[:, 2 * g:2 * g + 2, :], sig[:, g, :, :], ALU.mult))
                        dve.nop().then_inc(pair_free[g], 1)
                    link(dve.tensor_tensor(mh, mh, sig[:, 1, :, :], ALU.add))
                    dve.nop().then_inc(merged_set, 1)
                for pt in range(2):
                    split_turned(pt)
                convert_to(m0 + 12 + 4)
                projected(m0 + 12 + 4)
                norm(L * NLN, lambda t, half: ps[:, 2 * half + t, :])
                for pt in range(2):
                    dve.nop().then_inc(pair_free[pt], 1)
                for pt in range(2):
                    split_turned(pt)

            def attention(L):
                a0 = N_ATT * L

                def scores(u):
                    kind, t, a = att_step(u)
                    nk = P * (t + 1)
                    dve.wait_ge(s_ready, a0 + u + 1)
                    wait(dve, pt_ready, a0 + u - 2)
                    pu = pbuf[:, u % 3, :, 0:nk]
                    k0 = SEQ - nk
                    if kind == "nsa":
                        ins = dve.tensor_tensor(pu, scores_at(u, nk), free(toep[:, a, k0:k0 + 1], [[0, 2], [1, nk]]),
                                                ALU.add)
                    else:
                        for hh in range(2):
                            c0 = (u % 2) * SEQ
                            ins = dve.scalar_tensor_tensor(pu[:, hh, :], ps[:, 4 + hh, c0:c0 + nk],
                                                           fcum[:, t, 2 * a + hh:2 * a + hh + 1],
                                                           table[:, K_MASK + k0:K_MASK + SEQ], ALU.add, ALU.add)
                    link(ins)
                    dve.nop().then_inc(s_taken, 1)
                    dve.tensor_reduce(stats[:, u % 2, 0:2], pu, AX, ALU.max, negate=True).then_inc(negmax_set, 1)

                def factors(u):
                    kind, t, a = att_step(u)
                    dve.wait_ge(exp_done, a0 + u + 1)
                    wait(dve, p_scaled, a0 + u - 1)
                    st = stats[:, u % 2, :]
                    link(dve.tensor_scalar(st[:, 4:6], st[:, 4:6], 1e-30, None, ALU.max))
                    if kind == "nsa":
                        link(dve.reciprocal(st[:, 6:8], st[:, 4:6]))
                        ins = dve.tensor_tensor(st[:, 8:10], st[:, 6:8], gates[:, t, 3 * a + 1:3 * a + 3], ALU.mult)
                    else:
                        ins = dve.reciprocal(st[:, 8:10], st[:, 4:6])
                    ins.then_inc(norm_set, 1)

                def out_lo(u):
                    kind, t, a = att_step(u)
                    dve.wait_ge(y_hi, a0 + u + 1)
                    b, n = (DH * (a // 4), DH) if kind == "nsa" else (0, P)
                    k = a % 4 if kind == "nsa" else 4 + a
                    dve.tensor_tensor(yTl[b:b + n, k, t * P:(t + 1) * P], ps[b:b + n, u % 2, 0:P],
                                      yTh[b:b + n, k, t * P:(t + 1) * P].bitcast(F32), ALU.subtract).then_inc(y_lo, 1)

                if L == 0:
                    dve.wait_ge(toep_in, 16)
                scores(0)
                dve.wait_ge(pct_turned, L + 1)
                for u in range(N_ATT):
                    if u + 1 < N_ATT:
                        scores(u + 1)
                    factors(u)
                    if u > 1:
                        out_lo(u - 2)
                out_lo(N_ATT - 2)
                out_lo(N_ATT - 1)

            def norm(n, src, tiles=range(TT)):
                dve.wait_ge(lng_in, 32 * (n + 1))
                for t in tiles:
                    st = stats[:, t, :]
                    for half in range(2):
                        xs = x[:, t, half * 512:(half + 1) * 512]
                        ins = dve.scalar_tensor_tensor(xs, xs, ALPHA, src(t, half), ALU.mult, ALU.add)
                    link(ins)
                    bn = small[:, 448 + 16 * t:448 + 16 * t + 12].rearrange("p (a b) -> p a b", a=2)
                    for half in range(2):
                        ins = dve.bn_stats(bn[:, half, :], x[:, t, half * 512:(half + 1) * 512])
                    link(ins)
                    dve.bn_aggr(st[:, 12:14], small[:, 448 + 16 * t:448 + 16 * t + 12]).then_inc(var_set, 1)
                for t in tiles:
                    st, xs = stats[:, t, :], x[:, t, :]
                    dve.wait_ge(std_set, TT * n + t + 1)
                    link(dve.reciprocal(st[:, 15:16], st[:, 14:15]))
                    link(dve.tensor_scalar(xs, xs, st[:, 12:13], st[:, 15:16], ALU.subtract, ALU.mult))
                    link(dve.tensor_tensor(xs, xs, lng[:, 0, :], ALU.mult))
                    dve.tensor_tensor(xs, xs, lng[:, 1, :], ALU.add).then_inc(x_set, 1)
                dve.wait_ge(x_set, TT * (n + 1))

            def dense_ffn(u0, n_norm):
                ws = chunks(FF)
                at = u0
                for c, width in enumerate(ws):
                    at += 4
                    convert_to(at + AHEAD)
                    projected(at)
                    dve.wait_ge(act_h, c + 1)
                    dve.nop().then_inc(pair_free[0], 1)
                    hc = h[:, :, 0:width]
                    link(dve.tensor_tensor(hc, hc, ps[:, 2:4, 0:width], ALU.mult))
                    dve.nop().then_inc(h_set, 1)
                    dve.nop().then_inc(pair_free[1], 1)
                    if c:
                        at += down_units(ws[c - 1])
                    convert_to(at + AHEAD)
                    use[1].n += 1
                    dve.wait_ge(hT_hi, c + 1)
                    n = 2 * width
                    link(dve.tensor_tensor(hTl[:, 0:width // P, :].rearrange("p a b -> p (a b)"), pair(1)[:, 0:n],
                                           hTh[:, 0:width // P, :].rearrange("p a b -> p (a b)").bitcast(F32),
                                           ALU.subtract))
                    dve.nop().then_inc(hT_lo, 1)
                    dve.nop().then_inc(pair_free[1], 1)
                at += down_units(ws[-1])
                convert_to(at)
                projected(at)
                norm(n_norm, lambda t, half: ps[:, 4 + 2 * t + half, :])
                return at

            dve.memset(eps[:, :], LN_EPS).then_inc(eps_set, 1)
            dve.memset(tab[BUCKETS:BUCKETS + 1, :], NEG).then_inc(tab_set, 1)
            use[0].n += 2
            use[1].n += 1
            for pt in range(2):
                split_turned(pt)
            mixer(0, 0)
            if stop and stop["x_set"] <= 2:
                return
            at = dense_ffn(31, 1)
            use[0].n += 1
            for pt in range(2):
                split_turned(pt)
            if stop and stop["x_set"] <= 4:
                return
            mixer(1, at)
            dve.wait_ge(router_hi, 1)
            dve.tensor_tensor(rout_l, rout, rout_h.bitcast(F32), ALU.subtract).then_inc(router_lo, 1)
            is_full(0)
            link(dve.tensor_copy(r_logits, ps[:, 0:2, 0:NE]))
            dve.nop().then_inc(pair_free[0], 1)
            for t in range(TT):
                ins = dve.max(r_top[:, t, :], r_logits[:, t, :])
            link(ins)
            for t in range(TT):
                ins = dve.max_index(r_index[:, t, :].bitcast(U32), r_top[:, t, :], r_logits[:, t, :])
            link(ins)
            link(dve.tensor_copy(r_indexf, r_index.bitcast(U32)))
            iota8 = table[:, K_IOTA:K_IOTA + NE]
            for k, one in enumerate((r_one, r_two)):
                for t in range(TT):
                    ins = dve.tensor_scalar(one[:, t, :], iota8, r_indexf[:, t, k:k + 1], None, ALU.is_equal)
            link(ins)
            link(dve.tensor_tensor(r_mask, r_one, r_two, ALU.add))
            dve.nop().then_inc(picks_set, 1)
            link(dve.tensor_tensor(r_w[:, 0, :], free(r_top[:, 0, 1:2], [[NE, 2]]), free(r_top[:, 0, 0:1], [[NE, 2]]),
                                   ALU.subtract))
            dve.nop().then_inc(top_set, 1)
            dve.wait_ge(texp_set, 1)
            link(dve.tensor_scalar(r_w[:, 0, :], r_w[:, 1, :], 1.0, None, ALU.add))
            link(dve.reciprocal(r_w[:, 2, :], r_w[:, 0, :]))
            link(dve.tensor_tensor(r_w[:, 3, :], r_w[:, 1, :], r_w[:, 2, :], ALU.mult))
            dve.memset(r_slot[:, :, NE:NE + 1], FAR)
            for t in range(TT):
                ins = dve.tensor_scalar(r_gate[:, t, 0:NE], r_one[:, t, :], r_w[:, 2, t:t + 1], None, ALU.mult)
            link(ins)
            for t in range(TT):
                ins = dve.scalar_tensor_tensor(r_gate[:, t, 0:NE], r_two[:, t, :], r_w[:, 3, t:t + 1],
                                               r_gate[:, t, 0:NE], ALU.mult, ALU.add)
            link(ins)
            is_full(1)
            slots = r_slot[:, :, 0:NE]
            places = ps[:, 2, 0:2 * NE].rearrange("p (t e) -> p t e", t=TT)
            link(dve.scalar_tensor_tensor(slots, r_mask, -FAR, places, ALU.mult, ALU.add))
            link(dve.tensor_scalar(slots, slots, FAR, None, ALU.add))
            link(dve.tensor_reduce(r_count, ps[:, 2, 2 * NE:3 * NE], AX, ALU.max))
            dve.nop().then_inc(pair_free[1], 1)
            dve.tensor_scalar(flag[:, :], r_count, CAP + 0.5, None, ALU.is_gt).then_inc(flag_set, 1)
            link(dve.memset(acc, 0.0))

            def experts(S):
                unit = Tally(S.u0)

                def convert_to(n):
                    while unit.n < S.u0 + min(n, EU):
                        s = unit.n % CONV
                        dve.wait_ge(S.hi_ready, unit.at(1))
                        dve.tensor_tensor(lo[:, s, :], raw[:, unit.n % RAW, :], hi[:, s, :].bitcast(F32),
                                          ALU.subtract).then_inc(S.lo_ready, 1)
                        unit.n += 1

                def select(e):
                    dve.tensor_tensor(pick, free(table[:, K_IOTA:K_IOTA + 1], [[0, TT], [1, P]]),
                                      r_slot[:, :, bass.ds(e, 1)].broadcast_to([P, TT, P]), ALU.is_equal)\
                       .then_inc(S.pick_set, 1)

                def tokens_lo(n):
                    dve.wait_ge(S.xe_hi, n)
                    dve.tensor_tensor(xel, ps[:, 6:8, :].rearrange("p a b -> p (a b)"), xeh.bitcast(F32), ALU.subtract)\
                       .then_inc(S.xe_lo, 1)

                dve.nop().then_inc(S.hT_lo, 1)
                dve.nop().then_inc(S.ye_lo, 1)
                dve.nop().then_inc(S.sum_taken, 4)
                if S.p:
                    dve.tensor_scalar(slots, slots, float(CAP), None, ALU.subtract).then_inc(slots_moved, 1)
                    dve.wait_ge(slots_moved, 1)
                    dve.nop().then_inc(S.lo_ready, RAW)
                select(0)
                tokens_lo(1)
                with dve.Fori(0, NE) as e:
                    unit.enter(e, EU)
                    dve.wait_ge(S.pt_full, e + 1)
                    select(e + 1)
                    at = 0
                    for c in range(CH):
                        at += 4
                        convert_to(at + AHEAD)
                        dve.wait_ge(S.unit_used, e * EU + (S.u0 + at))
                        dve.wait_ge(S.act_h, e * CH + (c + 2))
                        dve.tensor_tensor(h[:, 0, :], h[:, 0, :], ps[:, 2, :], ALU.mult).then_inc(S.h_set, 1)
                        at += 2 if c else 0
                        convert_to(at + AHEAD)
                        dve.wait_ge(S.hT_hi, e * CH + (c + 1))
                        dve.tensor_tensor(hTl1, ps[:, 2, :], hTh1.bitcast(F32), ALU.subtract).then_inc(S.hT_lo, 1)
                    tokens_lo(e + 2)
                    convert_to(EU)
                    dve.wait_ge(S.ye_hi, e + 1)
                    dve.scalar_tensor_tensor(yel, ps[:, 4:6, :].rearrange("p a b -> p (a b)"), r_gs,
                                             yeh.bitcast(F32), ALU.mult, ALU.subtract).then_inc(S.ye_lo, 1)
                    for k in range(4):
                        t, half = divmod(k, 2)
                        to = acc[:, t, half * 512:(half + 1) * 512]
                        dve.wait_ge(S.sum_full, e * 4 + (k + 1))
                        dve.tensor_tensor(to, to, ps[:, sum_bank(k), :], ALU.add).then_inc(S.sum_taken, 1)
                    dve.wait_ge(S.sum_taken, e * 4 + 8)
                    unit.leave(NE)

            experts(passes[0])
            dve.wait_ge(flag_set, 1)
            again = dve.value_load(flag[0:1, 0:1], min_val=0, max_val=1)
            with dve.If(again == 1):
                experts(passes[1])
            norm(3, lambda t, half: acc[:, t, half * 512:(half + 1) * 512])


_INS = ["x", "w_in", "nsa_cmp_pe", "nsa_cmp_w1", "nsa_cmp_w2", "fox_f_bias", "w_nsa_branch", "w_fox_branch",
        "w_out", "rel_bias", "ln1_g", "ln1_b", "ln2_g", "ln2_b", "dense_w_gate", "dense_w_up", "dense_w_down",
        "moe_router", "moe_w_gate", "moe_w_up", "moe_w_down"]

STOP = None


def kernel(**inputs):
    import numpy as _np
    import concourse.bacc as _bacc
    from concourse import mybir as _mybir
    from concourse.bass_utils import run_bass_kernel_spmd as _run

    nc = _bacc.Bacc("TRN2", target_bir_lowering=False, num_devices=1)
    table, onehot = constants()
    arrays, io = {}, {}
    for name in _INS + ["table", "onehot"]:
        a = {"table": table, "onehot": onehot}[name] if name in ("table", "onehot") else _np.ascontiguousarray(inputs[name])
        if name == "w_in":
            q = a[:, :, :512].reshape(DEPTH, D, 2, 4, DH).transpose(0, 1, 3, 2, 4).reshape(DEPTH, D, 512)
            a = _np.concatenate([q, a[:, :, 512:]], axis=2)
        if name == "w_nsa_branch":
            a = _np.ascontiguousarray(a.reshape(DEPTH, 2, 4, DH, D).transpose(0, 2, 1, 3, 4).reshape(DEPTH, 512, D))
        arrays[f"in_{name}"] = a
        io[name] = nc.dram_tensor(f"in_{name}", a.shape, _mybir.dt.from_np(a.dtype), kind="ExternalInput").ap()
    io["out"] = nc.dram_tensor("out_0", (1, SEQ, D), _mybir.dt.float32, kind="ExternalOutput").ap()
    hybrid_kernel(nc, io, STOP)
    r = _run(nc, [arrays], core_ids=[0])
    return r.results[0]["out_0"]
```

```python
from contextlib import ExitStack

import numpy as np

import concourse.bass as bass
from concourse import mybir

F32 = mybir.dt.float32
F32R = mybir.dt.float32r
U32 = mybir.dt.uint32
I32 = mybir.dt.int32
ALU = mybir.AluOpType
ACT = mybir.ActivationFunctionType
AX = mybir.AxisListType.X

P = 128
D = 1024
KD = D // P
SEQ = 256
TT = SEQ // P
DEPTH = 2
DH = 64
NH = 8
NKV = 2
FH = 8
CMP_BLOCK, CMP_STRIDE, CMP_HID = 32, 16, 128
NC = SEQ // CMP_STRIDE - CMP_BLOCK // CMP_STRIDE + 1
NCP = 16
CM = CMP_BLOCK // 2
BUCKETS, MAX_DIST = 32, 128
FF = 2816
FE = 3584
NE = 8
ALPHA = (2 * DEPTH) ** 0.25
LN_EPS = 1e-5
NEG = -1e30
SCALE = DH ** -0.5
FAR = 1e4

C_Q, C_KC, C_KS, C_KW = 0, 512, 768, 1024
C_FQ, C_FK, C_FV = 1304, 1816, 2328
C_MERGE = 2848
NG = 3 * NH

RAW = 6
CONV = 3
UNIT = 2048
CHUNK = 512
CAP = P

K_ID, K_U, K_MASK, K_VIS, K_IOTA, K_SU, K_ONE, K_BLK = 0, 128, 384, 640, 896, 1024, 1152, 1280
K_END = K_BLK + NH
OH_DOWN, OH_UP0 = 384, 272
OH_UP = OH_UP0 + SEQ


def constants():
    c = np.zeros((P, K_END), np.float32)
    p = np.arange(P)[:, None]
    c[:, K_ID:K_ID + P] = np.eye(P)
    c[:, K_U:K_U + SEQ] = p <= np.arange(SEQ)[None]
    c[:, K_MASK:K_MASK + SEQ] = np.where(np.arange(SEQ)[None] > p + P, NEG, 0.0)
    end = np.arange(NCP) * CMP_STRIDE + CMP_BLOCK - 1
    for t in range(TT):
        vis = (end[None] <= t * P + p) & (np.arange(NCP)[None] < NC)
        for hp in range(2):
            for i in range(NH // 2):
                at = K_VIS + hp * P + t * 64 + i * NCP
                c[:, at:at + NCP] = vis
    c[:, K_IOTA:K_IOTA + P] = np.where(np.arange(P) < CAP, np.arange(P), -2 * FAR)[None]
    c[:, K_SU:K_SU + P] = p < np.arange(P)[None]
    c[:, K_ONE:K_ONE + P] = 1.0
    c[:, K_BLK:K_BLK + NH] = p // NCP == np.arange(NH)[None]

    def onehot(dist):
        n = np.maximum(dist, 0)
        exact = BUCKETS // 2
        far = exact + (np.log(np.maximum(n, 1).astype(np.float32) / exact) / np.log(MAX_DIST / exact)
                       * (BUCKETS - exact)).astype(np.int32)
        bucket = np.where(n < exact, n, np.minimum(far, BUCKETS - 1))
        out = np.zeros((BUCKETS + 1, len(dist)), np.float32)
        out[bucket, np.arange(len(dist))] = dist >= 0
        out[BUCKETS] = dist < 0
        return out

    oh = np.concatenate([onehot(SEQ - 1 - np.arange(OH_DOWN)), onehot(np.arange(OH_UP) - OH_UP0)], 1)
    return c, np.ascontiguousarray(oh)


def free(ap, dims):
    return bass.AP(tensor=ap.tensor, offset=ap.offset, ap=[list(ap.ap[0])] + [list(d) for d in dims])


class Tally:

    def __init__(self, n=0):
        self.n, self.reg, self.per, self.start = n, None, 0, 0

    def at(self, more=0):
        v = self.n + more
        return v if self.reg is None else self.reg * self.per + v

    def enter(self, reg, per):
        self.reg, self.per, self.start = reg, per, self.n

    def leave(self, trips):
        assert self.n == self.start + self.per, (self.n, self.start, self.per)
        self.reg, self.n = None, self.start + self.per * trips


def wait(eng, sem, value):
    if isinstance(value, int) and value <= 0:
        return
    eng.wait_ge(sem, value)


def hybrid_kernel(nc, io, stop=None):
    w_in, w_nb, w_fb, w_out = io["w_in"], io["w_nsa_branch"], io["w_fox_branch"], io["w_out"]

    units = []

    def add(nk, width, parts):
        units.append((nk, width, parts))

    def rows(w, k0, nk, c0, width):
        return w[k0 * P:(k0 + nk) * P, c0:c0 + width].rearrange("(k p) n -> p k n", p=P)

    def add_cols(w, c0, width, kt=KD):
        n = 1 if kt * width <= UNIT else 2
        for h in range(n):
            add(kt // n, width, rows(w, h * kt // n, kt // n, c0, width))

    def add_mixer(L):
        add_cols(w_in[L], C_KC, 256)
        add_cols(w_in[L], C_Q, 512)
        for kv in range(2):
            add(CM, CMP_HID, rows(io["nsa_cmp_w1"][L, kv], 0, CM, 0, CMP_HID))
        add_cols(w_in[L], C_KS, 256)
        add_cols(w_in[L], C_KW, 256 + NG)
        add_cols(w_in[L], C_FV + 256, 256 + FH)
        add_cols(w_in[L], C_FQ, 512)
        add_cols(w_in[L], C_FK, 512)
        add_cols(w_in[L], C_FV, 256)
        for half in range(2):
            for g in range(2):
                add_cols(w_in[L], C_MERGE + g * D + half * 512, 512)
            add_cols(w_nb[L], half * 512, 512, 4)
            add_cols(w_fb[L], half * 512, 512, 4)
        for half in range(2):
            add_cols(w_out[L], half * 512, 512)

    def chunks(total):
        return [min(CHUNK, total - c) for c in range(0, total, CHUNK)]

    def down_units(width):
        return width // P // 2

    def ffn_order(total):
        ws = chunks(total)
        out = []
        for c, width in enumerate(ws):
            out += [("gate", c, 0), ("gate", c, 1), ("up", c, 0), ("up", c, 1)]
            if c:
                out += [("down", c - 1, i) for i in range(down_units(ws[c - 1]))]
        return out + [("down", len(ws) - 1, i) for i in range(down_units(ws[-1]))]

    def ffn_unit(gate, up, down, total, kind, c, i):
        width = chunks(total)[c]
        if kind == "down":
            return 2, D, rows(down, c * CHUNK // P + 2 * i, 2, 0, D)
        return KD // 2, width, rows(gate if kind == "gate" else up, i * KD // 2, KD // 2, c * CHUNK, width)

    add_mixer(0)
    for u in ffn_order(FF):
        add(*ffn_unit(io["dense_w_gate"][0], io["dense_w_up"][0], io["dense_w_down"][0], FF, *u))
    add_mixer(1)
    CH = len(chunks(FE))
    moe_first = [(w, 0, i) for w in ("gate", "up") for i in range(2)]
    moe_body = [u for c in range(1, CH) for u in
                [("gate", c, 0), ("gate", c, 1), ("up", c, 0), ("up", c, 1), ("down", c - 1, 0), ("down", c - 1, 1)]]
    moe_down = [("down", CH - 1, i) for i in range(2)]

    ctx = ExitStack()
    with ctx:
        def sb(name, shape, dt=F32):
            return ctx.enter_context(nc.sbuf_tensor(name, shape, dt))

        def sem(name):
            return ctx.enter_context(nc.semaphore(name))

        raw = sb("raw", [P, RAW, UNIT])
        hi = sb("hi", [P, CONV, UNIT], F32R)
        lo = sb("lo", [P, CONV, UNIT], F32R)
        x = sb("x", [P, TT, D])
        xTh = sb("xTh", [P, KD, SEQ], F32R)
        xTl = sb("xTl", [P, KD, SEQ], F32R)
        yTh = sb("yTh", [P, KD, SEQ], F32R)
        yTl = sb("yTl", [P, KD, SEQ], F32R)
        table = sb("table", [P, K_END])
        toep = sb("toep", [P, NH, SEQ])
        cbias = sb("cbias", [P, 2, TT * 4 * NCP])
        qk = sb("qk", [P, 8, SEQ])
        kv = sb("kv", [P, 8, SEQ])
        ksw = sb("ksw", [P, 2, SEQ])
        vsw = sb("vsw", [P, 2, TT, P])
        gates = sb("gates", [P, TT, NG])
        logf = sb("logf", [P, 4, TT, FH])
        fcum = sb("fcum", [P, TT, FH])
        blocks = sb("blocks", [P, 2, CM, 2 * NCP])
        small = sb("small", [P, 480])
        pbuf = sb("pbuf", [P, 3, 2, SEQ])
        ptb = sb("ptb", [P, 2, 512])
        lng = sb("lng", [P, 2, D])
        hTh = sb("hTh", [P, 4, SEQ], F32R)
        hTl = sb("hTl", [P, 4, SEQ], F32R)
        vcb = sb("vcb", [P, NH, DH])
        cmpw2 = sb("cmpw2", [P, 2, DH])
        pe_rows = sb("pe_rows", [32, P])
        pe_cols = sb("pe_cols", [P, 2, CM])
        fbias = sb("fbias", [P, FH])
        stats = sb("stats", [P, TT, 16])
        eps = sb("eps", [P, 1])
        flag = sb("flag", [P, 1], I32)
        ps = ctx.enter_context(nc.psum_tensor("ps", [P, 8, 512], F32))

        ident = table[:, K_ID:K_ID + P]
        tri = table[:, K_U:K_U + SEQ]
        merged = qk[:, :, :].rearrange("p a b -> p (a b)").rearrange("p (t n) -> p t n", t=TT)
        fkT = kv[:, 0:4, :]
        fv = kv[:, 4:8, :].rearrange("p a b -> p (a b)").rearrange("p (t n) -> p t n", t=TT)
        blh = yTh[:, 0:4, :].rearrange("p a b -> p (a b)").rearrange("p (v m n) -> p v m n", v=2, m=CM)
        bll = yTl[:, 0:4, :].rearrange("p a b -> p (a b)").rearrange("p (v m n) -> p v m n", v=2, m=CM)
        h = blocks[:, :, :, :].rearrange("p v m n -> p (v m n)").rearrange("p (t n) -> p t n", t=TT)
        sig = [h, lng[:, 0, :].rearrange("p (t n) -> p t n", t=TT)]
        onehot = kv[0:BUCKETS + 1, 0:4, :].rearrange("p a b -> p (a b)")[:, 0:OH_DOWN + OH_UP]
        tab = small[0:BUCKETS + 1, 0:NH]
        vrow = ptb[0:NH, 0, 0:OH_DOWN]
        gkT = small[:, 0:2 * NCP]
        kcT = small[:, 64:64 + NCP]
        gvT = small[:, 128:256]
        pct = small[:, 128:384]
        csum = small[:, 384:448].rearrange("p (a b) -> p a b", a=4)
        cs = pbuf[:, 0, :, :].rearrange("p a b -> p (a b)")

        scratch = nc.dram_tensor("bias_rows", (P, NH, OH_DOWN), F32, kind="Internal").ap()

        const_in, x_in, small_in, lng_in = sem("const_in"), sem("x_in"), sem("small_in"), sem("lng_in")
        onehot_in, vrow_out, toep_in = sem("onehot_in"), sem("vrow_out"), sem("toep_in")
        raw_in = [sem(f"raw_in{i}") for i in range(RAW)]
        hi_ready, lo_ready, unit_used = sem("hi_ready"), sem("lo_ready"), sem("unit_used")
        pair_full = [sem("pair_full0"), sem("pair_full1")]
        pair_free = [sem("pair_free0"), sem("pair_free1")]
        dve_step, act_step = sem("dve_step"), sem("act_step")
        eps_set, tab_set, vrow_full, vrow_set, pe_turned, pe_cols_set, cbias_full = (
            sem("eps_set"), sem("tab_set"), sem("vrow_full"), sem("vrow_set"), sem("pe_turned"), sem("pe_cols_set"),
            sem("cbias_full"))
        kcv_full, cscores_full = sem("kcv_full"), sem("cscores_full")
        split_hi, split_lo = sem("split_hi"), sem("split_lo")
        q_set, keys_set, blocks_set, blh_set, bll_set = (
            sem("q_set"), sem("keys_set"), sem("blocks_set"), sem("blh_set"), sem("bll_set"))
        gelu_set, kc_set, vc_set, fox_set, logits_set, lexp_set, lln_set, logf_set, fcum_set = (
            sem("gelu_set"), sem("kc_set"), sem("vc_set"), sem("fox_set"), sem("logits_set"), sem("lexp_set"),
            sem("lln_set"), sem("logf_set"), sem("fcum_set"))
        cs_ready, cs_exp, cs_prob, pct_turned, pct_set, cs_sub = (
            sem("cs_ready"), sem("cs_exp"), sem("cs_prob"), sem("pct_turned"), sem("pct_set"), sem("cs_sub"))
        s_ready, s_taken, negmax_set, exp_done, norm_set, p_scaled = (
            sem("s_ready"), sem("s_taken"), sem("negmax_set"), sem("exp_done"), sem("norm_set"), sem("p_scaled"))
        pt_ready, pt_copied, o_ready, y_hi, y_lo = (
            sem("pt_ready"), sem("pt_copied"), sem("o_ready"), sem("y_hi"), sem("y_lo"))
        sig_set, merged_set = sem("sig_set"), sem("merged_set")
        var_set, std_set, x_set, y_full = sem("var_set"), sem("std_set"), sem("x_set"), sem("y_full")
        act_h, h_set, hT_hi, hT_lo = sem("act_h"), sem("h_set"), sem("hT_hi"), sem("hT_lo")
        out_done = sem("out_done")
        router_in, router_hi, router_lo = sem("router_in"), sem("router_hi"), sem("router_lo")
        top_set, texp_set, picks_set, routed, flag_set = (
            sem("top_set"), sem("texp_set"), sem("picks_set"), sem("routed"), sem("flag_set"))

        route = pbuf[:, 2, :, :].rearrange("p a b -> p (a b)")

        def routing(at, n, width):
            return route[:, at:at + n * width].rearrange("p (t e) -> p t e", t=n)

        r_logits, r_top, r_index = routing(0, 2, NE), routing(16, 2, 8), routing(32, 2, 8)
        r_indexf, r_one, r_two, r_mask = routing(48, 2, 8), routing(64, 2, NE), routing(80, 2, NE), routing(96, 2, NE)
        r_gate, r_slot = routing(112, 2, NE), routing(130, 2, NE)
        r_w = route[:, 148:156].rearrange("p (a t) -> p a t", t=2)
        r_count, r_gs = route[:, 156:157], route[:, 157:158]
        pick = pbuf[:, 0, :, 0:P]
        rout = small[:, 0:KD * NE]
        rout_h = hTh[:, 0, 0:KD * NE]
        rout_l = hTl[:, 0, 0:KD * NE]
        pickT = xTh[:, 0, :]
        xeh = yTh[:, 0:4, :].rearrange("p a b -> p (a b)")
        xel = yTl[:, 0:4, :].rearrange("p a b -> p (a b)")
        yeh = yTh[:, 4:8, :].rearrange("p a b -> p (a b)")
        yel = yTl[:, 4:8, :].rearrange("p a b -> p (a b)")
        acc = merged

        class Pass:

            def __init__(self, p):
                def own(name):
                    return sem(f"{name}_pass{p}")
                self.p = p
                if p == 0:
                    self.u0, self.raw_in, self.hi_ready, self.lo_ready, self.unit_used = (
                        len(units), raw_in, hi_ready, lo_ready, unit_used)
                else:
                    self.u0, self.raw_in = RAW, [own(f"raw_in{i}") for i in range(RAW)]
                    self.hi_ready, self.lo_ready, self.unit_used = own("hi_ready"), own("lo_ready"), own("unit_used")
                self.pick_set, self.pt_full, self.pt_set = own("pick_set"), own("pt_full"), own("pt_set")
                self.xe_full, self.xe_hi, self.xe_lo = own("xe_full"), own("xe_hi"), own("xe_lo")
                self.act_h, self.h_set, self.hT_full = own("act_h"), own("h_set"), own("hT_full")
                self.hT_hi, self.hT_lo = own("hT_hi"), own("hT_lo")
                self.ye_hi, self.ye_lo = own("ye_hi"), own("ye_lo")
                self.sum_full, self.sum_taken = own("sum_full"), own("sum_taken")

        passes = [Pass(0), Pass(1)]
        slots_moved = sem("slots_moved")
        NF, NB = len(moe_first), len(moe_body)
        EU = NF + NB + len(moe_down)
        FT = CHUNK // P

        hTh1 = hTh[:, 0:2, :].rearrange("p a b -> p (a b)")
        hTl1 = hTl[:, 0:2, :].rearrange("p a b -> p (a b)")

        def sum_bank(k):
            return (1, 3, 6, 7)[k]

        block = ctx.enter_context(nc.Block())

        def unit_view(buf, slot, nk, width):
            return buf[:, slot, 0:nk * width].rearrange("p (k n) -> p k n", k=nk)

        N_ATT = 2 * NH + FH
        SMALL = 4
        NLN = 2
        NSPLIT = 6

        def att_step(u):
            if u < 2 * NH:
                i, r = divmod(u, 4)
                return "nsa", r // 2, i + (NH // NKV) * (r % 2)
            i, t = divmod(u - 2 * NH, 2)
            return "fox", t, i

        SIDE = (("values_b", 4), ("queries", 4), ("cumulate", 0), ("keys", 4), ("values_a", 2),
                ("gate0", 4), ("gate1", 4), ("nsa_out", 2))
        BEFORE = 4
        CUM_AT = 4
        PRE = 8

        def halves_done(u):
            if u < -1:
                return 0
            return min(BEFORE + u + 1 - (u >= CUM_AT), sum(n for _, n in SIDE))

        def side_ended(u):
            out, end = [], 0
            for name, n in SIDE:
                end += n
                if n and halves_done(u - 1) < end <= halves_done(u):
                    out.append((name, end // 2))
            return out

        def norm_col(u):
            return stats[:, u % 2, 8:10]

        def scores_at(u, nk):
            kind, t, a = att_step(u)
            if kind == "nsa":
                return free(ps[:, 4 + a // 4, 0:1], [[SEQ, 2], [1, nk]])
            return free(ps[:, 4, (u % 2) * SEQ:(u % 2) * SEQ + 1], [[512, 2], [1, nk]])

        @block.sync
        def _(sp):
            sp.dma_start(ident, io["table"][:, 0:P]).then_inc(const_in, 16)
            sp.dma_start(x[:, :, :], io["x"][0].rearrange("(t p) n -> p t n", p=P)).then_inc(x_in, 16)
            for n, (nk, width, src) in enumerate(units):
                wait(sp, lo_ready, n - RAW + 1)
                sp.dma_start(unit_view(raw, n % RAW, nk, width), src).then_inc(raw_in[n % RAW], 16)
                if n == 2:
                    sp.dma_start(table[:, P:K_END], io["table"][:, P:K_END]).then_inc(const_in, 16)
                if stop and n == stop.get("units", 10 ** 9) - 1:
                    break

            def experts(S):
                def load(n, e, u, after=0, following=None):
                    nk, width, src = ffn_unit(*(io[f"moe_w_{w}"][0, 0] for w in ("gate", "up", "down")), FE, *u)
                    if isinstance(e, int):
                        start = (e + after) * (FE * D) + src.offset
                        need = e * EU + (n - RAW + 1)
                    else:
                        start = sp.snap(e * (FE * D) + (src.offset + FE * D) if after else
                                        following * (FE * D) + (src.offset - FE * D))
                        need = sp.snap(e * EU + (n - RAW + 1))
                    src = bass.AP(tensor=src.tensor, offset=start, ap=[list(d) for d in src.ap])
                    sp.wait_ge(S.lo_ready, need)
                    sp.dma_start(unit_view(raw, n % RAW, nk, width), src).then_inc(S.raw_in[n % RAW], 16)

                for k, u in enumerate(moe_first):
                    load(S.u0 + k, 0, u)

                def body(e, last, following=None):
                    n = S.u0 + NF
                    for u in moe_body:
                        load(n, e, u, 0, following)
                        n += 1
                    if last:
                        for u in moe_down:
                            load(n, e, u)
                            n += 1
                    else:
                        for u, after in ([(u, 1) for u in moe_first[:2]] + [(u, 0) for u in moe_down]
                                         + [(u, 1) for u in moe_first[2:]]):
                            load(n, e, u, after, following)
                            n += 1

                with sp.Fori(0, NE - 1) as e:
                    body(e, False, sp.snap(e + 1))
                body(NE - 1, True)

            if not stop:
                experts(passes[0])
                sp.wait_ge(flag_set, 1)
                again = sp.value_load(flag[0:1, 0:1], min_val=0, max_val=1)
                with sp.If(again == 1):
                    sp.wait_ge(lo_ready, len(units) + NE * EU)
                    experts(passes[1])
            last = stop["x_set"] if stop else 4 * TT
            sp.wait_ge(x_set, last)
            sp.dma_start(io["out"][0].rearrange("(t p) n -> p t n", p=P), x[:, :, :]).then_inc(out_done, 16)
            sp.wait_ge(out_done, 16)

        @block.gpsimd
        def _(pool):
            pool.dma_start(onehot, io["onehot"]).then_inc(onehot_in, 16)
            pool.dma_start(tab[0:BUCKETS, :], io["rel_bias"]).then_inc(onehot_in, 16)

            def small_loads(L):
                if L:
                    pool.wait_ge(y_lo, N_ATT * L)
                pool.dma_start(pe_rows[:, :],
                               io["nsa_cmp_pe"][L].rearrange("v l d -> (v l d)").rearrange("(r n) -> r n", n=P)
                               ).then_inc(small_in, 16)
                pool.dma_start(cmpw2[:, :, :], io["nsa_cmp_w2"][L].rearrange("v p d -> p v d")).then_inc(small_in, 16)
                pool.dma_start(fbias[:, :], io["fox_f_bias"][L].partition_broadcast(P)).then_inc(small_in, 16)

            def norm_loads(L, which):
                wait(pool, x_set, TT * (NLN * L + which))
                if which == 0:
                    pool.wait_ge(merged_set, 2 * (L + 1))
                pool.dma_start(lng[:, 0, :], io[f"ln{which + 1}_g"][L].partition_broadcast(P)).then_inc(lng_in, 16)
                pool.dma_start(lng[:, 1, :], io[f"ln{which + 1}_b"][L].partition_broadcast(P)).then_inc(lng_in, 16)

            def attention(L):
                for u in range(N_ATT):
                    t = att_step(u)[1]
                    nk = P * (t + 1)
                    pool.wait_ge(norm_set, N_ATT * L + u + 1)
                    pu = pbuf[:, u % 3, :, 0:nk]
                    pool.tensor_tensor(pu, pu, free(norm_col(u), [[1, 2], [0, nk]]), ALU.mult).then_inc(p_scaled, 1)

            small_loads(0)
            pool.wait_ge(vrow_set, 1)
            pool.dma_start(scratch.rearrange("p h n -> h p n"), free(vrow, [[0, P], [1, OH_DOWN]])
                           ).then_inc(vrow_out, 16)
            pool.wait_ge(vrow_out, 16)
            pool.dma_start(toep[:, :, :], bass.AP(tensor=scratch.tensor, offset=scratch.offset + P - 1,
                                                  ap=[[NH * OH_DOWN - 1, P], [OH_DOWN, NH], [1, SEQ]])).then_inc(toep_in, 16)
            attention(0)
            small_loads(1)
            norm_loads(0, 0)
            norm_loads(0, 1)
            if stop and stop["x_set"] <= 4:
                return
            attention(1)
            pool.wait_ge(y_lo, 2 * N_ATT)
            pool.dma_start(rout.rearrange("p (k e) -> p k e", k=KD),
                           io["moe_router"][0].rearrange("(k p) e -> p k e", p=P)).then_inc(router_in, 16)
            norm_loads(1, 0)
            norm_loads(1, 1)

        @block.tensor
        def _(pe):
            unit, step = Tally(), [Tally(), Tally()]

            def next_unit():
                nk, width, _ = units[unit.n]
                pe.wait_ge(lo_ready, unit.at(1))
                s = unit.n % CONV
                return nk, unit_view(hi, s, nk, width), unit_view(lo, s, nk, width)

            def used(mm):
                mm.then_inc(unit_used, 1)
                unit.n += 1

            def claim(pair):
                wait(pe, pair_free[pair], step[pair].at())

            def full(mm, pair):
                mm.then_inc(pair_full[pair], 1)
                step[pair].n += 1

            def three(out, stat_h, stat_l, mov_h, mov_l, start, stop_):
                pe.matmul(out, stat_h, mov_h, start=start, stop=False, skip_group_check=True)
                pe.matmul(out, stat_h, mov_l, start=False, stop=False, skip_group_check=True)
                return pe.matmul(out, stat_l, mov_h, start=False, stop=stop_, skip_group_check=True)

            def project(outs, pair, k_units):
                for _ in project_halves(outs, pair, k_units):
                    pass

            def project_halves(outs, pair, k_units):
                claim(pair)
                k = 0
                for un in range(k_units):
                    nk, wh, wl = next_unit()
                    for j in range(nk):
                        last = un == k_units - 1 and j == nk - 1
                        for out, kind, c0, a, first in outs:
                            start = first and k == 0
                            if kind == "T":
                                mm = three(out, wh[:, j, c0:c0 + P], wl[:, j, c0:c0 + P],
                                           xTh[:, k, :], xTl[:, k, :], start, last)
                            else:
                                xs = slice(kind * P, kind * P + P)
                                mm = three(out, xTh[:, k, xs], xTl[:, k, xs],
                                           wh[:, j, c0:c0 + a], wl[:, j, c0:c0 + a], start, last)
                        k += 1
                        if j == nk // 2 - 1:
                            yield
                    used(mm)
                    if un == k_units - 1:
                        step[pair].n += 1
                    yield

            def turn(src):
                for pair in range(2):
                    claim(pair)
                    for k in range(4 * pair, 4 * pair + 4):
                        for t in range(TT):
                            mm = pe.transpose(ps[:, k // 2, (k % 2) * SEQ + t * P:(k % 2) * SEQ + (t + 1) * P],
                                              src[:, t, k * P:(k + 1) * P], ident)
                    full(mm, pair)

            def mixer(L):
                pe.wait_ge(split_lo, NSPLIT * L + 2)
                project([(ps[:, v, 0:SEQ], "T", v * P, 0, True) for v in range(2)], 0, 1)
                pe.wait_ge(small_in, 16 * 3 * (L + 1))
                pe.transpose(ps[:, 5, 0:32], pe_rows[:, :], ident[0:32, 0:32]).then_inc(pe_turned, 1)
                if L == 0:
                    for t in range(TT):
                        for c in range(NCP):
                            a = OH_DOWN + OH_UP0 + t * P - (c * CMP_STRIDE + CMP_BLOCK - 1)
                            mm = pe.matmul(ps[:, 6 + t, c * NH:(c + 1) * NH], onehot[:, a:a + P], tab,
                                           start=True, stop=True)
                    mm.then_inc(cbias_full, 1)
                project([(ps[:, 2 + b // 2, (b % 2) * SEQ:(b % 2 + 1) * SEQ], "T", b * P, 0, b % 2 == 0)
                         for b in range(4)], 1, 2)
                claim(0)
                pe.wait_ge(bll_set, L + 1)
                for v in range(2):
                    nk, wh, wl = next_unit()
                    for m in range(nk):
                        mm = three(ps[:, v, 0:2 * NCP], wh[:, m, :], wl[:, m, :], blh[:, v, m, :], bll[:, v, m, :],
                                   m == 0, m == nk - 1)
                    used(mm)
                step[0].n += 1
                project([(ps[:, 2, 0:SEQ], "T", 0, 0, True)]
                        + [(ps[:, 3, t * SEQ:t * SEQ + P], t, P, P, t == 0) for t in range(2)], 1, 1)
                pe.wait_ge(gelu_set, L + 1)
                for g in range(NKV):
                    pe.matmul(ps[g * DH:(g + 1) * DH, 4, 0:NCP], cmpw2[:, 0, :], gkT[:, g * NCP:(g + 1) * NCP],
                              start=True, stop=True)
                pe.matmul(ps[:, 5, 0:DH], gvT, cmpw2[:, 1, :], start=True, stop=True).then_inc(kcv_full, 1)
                window = project_halves(
                    [(ps[:, 0, 0:SEQ], "T", 0, 0, True)]
                    + [(ps[:, 1, t * SEQ:t * SEQ + P + NG], t, P, P + NG, t == 0) for t in range(2)], 0, 2)
                next(window)
                next(window)
                pe.wait_ge(kc_set, L + 1)
                pe.wait_ge(q_set, L + 1)
                for t in range(TT):
                    for hd in range(NH):
                        g, i = divmod(hd, NH // NKV)
                        b = DH * g
                        at = t * 64 + i * NCP
                        mm = pe.matmul(ps[:, 6 + g, at:at + NCP], qk[b:b + DH, i, t * P:(t + 1) * P],
                                       kcT[b:b + DH, :], start=True, stop=True)
                mm.then_inc(cscores_full, 1)
                for _ in window:
                    pass
                attention(L)

                def branch(g, pt):
                    claim(pt)
                    nk, wh, wl = next_unit()
                    for t in range(TT):
                        for j in range(nk):
                            k = 4 * g + j
                            mm = three(ps[:, 2 * pt + t, :], yTh[:, k, t * P:(t + 1) * P],
                                       yTl[:, k, t * P:(t + 1) * P], wh[:, j, :], wl[:, j, :], j == 0, j == nk - 1)
                    used(mm)
                    step[pt].n += 1

                branch(1, 0)
                for g in range(2):
                    project([(ps[:, 2 * (1 - g) + t, :], t, 0, 512, True) for t in range(2)], 1 - g, 2)
                for g in range(2):
                    branch(g, 1 - g)
                pe.wait_ge(merged_set, 2 * (L + 1))
                turn(merged)
                pe.wait_ge(split_lo, NSPLIT * L + 4)
                for half in range(2):
                    project([(ps[:, 2 * half + t, :], t, 0, 512, True) for t in range(2)], half, 2)

            def attention(L):
                a0 = N_ATT * L

                def scores(u):
                    kind, t, a = att_step(u)
                    nk = P * (t + 1)
                    wait(pe, s_taken, a0 + (u - 1 if kind == "nsa" else u))
                    if kind == "nsa":
                        g, i = divmod(a, NH // NKV)
                        b = DH * g
                        for br in range(2):
                            mm = pe.matmul(ps[:, 4 + a // 4, br * SEQ:br * SEQ + nk],
                                           qk[b:b + DH, i, t * P:(t + 1) * P], ksw[b:b + DH, br, 0:nk],
                                           start=True, stop=True)
                    else:
                        c0 = (u % 2) * SEQ
                        for hh in range(2):
                            b, head = DH * hh, 2 * a + hh
                            out = ps[:, 4 + hh, c0:c0 + nk]
                            pe.matmul(out, qk[b:b + DH, 4 + a, t * P:(t + 1) * P], fkT[b:b + DH, a, 0:nk],
                                      start=True, stop=False, skip_group_check=True)
                            for j in range(t + 1):
                                mm = pe.matmul(ps[:, 4 + hh, c0 + j * P:c0 + nk],
                                               free(logf[:, 3, j, head:head + 1], [[0, P]]), tri[:, 0:nk - j * P],
                                               start=False, stop=(j == t), skip_group_check=True)
                    mm.then_inc(s_ready, 1)

                def turn_probs(u):
                    t = att_step(u)[1]
                    pe.wait_ge(p_scaled, a0 + u + 1)
                    wait(pe, pt_copied, a0 + u - 1)
                    for br in range(2):
                        for j in range(t + 1):
                            c = (br * (t + 1) + j) * P
                            mm = pe.transpose(ps[:, 6 + u % 2, c:c + P], pbuf[:, u % 3, br, j * P:(j + 1) * P], ident)
                    mm.then_inc(pt_ready, 1)

                def values(u):
                    kind, t, a = att_step(u)
                    pe.wait_ge(pt_copied, a0 + u + 1)
                    wait(pe, y_lo, a0 + u - 1)
                    for br in range(2):
                        b = DH * (a // 4 if kind == "nsa" else br)
                        out = ps[b:b + DH, u % 2, 0:P]
                        for j in range(t + 1):
                            c = (br * (t + 1) + j) * P
                            if kind == "nsa":
                                g = a // (NH // NKV)
                                mm = pe.matmul(out, vsw[:, br, j, g * DH:(g + 1) * DH], ptb[:, u % 2, c:c + P],
                                               start=(br == 0 and j == 0), stop=False, skip_group_check=True)
                            else:
                                head = 2 * a + br
                                mm = pe.matmul(out, fv[:, j, head * DH:(head + 1) * DH], ptb[:, u % 2, c:c + P],
                                               start=(j == 0), stop=(j == t), skip_group_check=True)
                    if kind == "nsa":
                        mm = pe.matmul(out, vcb[:, a, :], pct[:, t * P:(t + 1) * P],
                                       start=False, stop=True, skip_group_check=True)
                    mm.then_inc(o_ready, 1)

                def side():
                    transposed = [(ps[:, 2 + b // 2, (b % 2) * SEQ:(b % 2 + 1) * SEQ], "T", b * P, 0, b % 2 == 0)
                                  for b in range(4)]
                    yield from project_halves([(ps[:, 2 + t, 0:256 + FH], t, 0, 256 + FH, True) for t in range(2)],
                                              1, 2)
                    yield from project_halves(transposed, 1, 2)
                    yield from project_halves(transposed, 1, 2)
                    yield from project_halves([(ps[:, 2 + t, 0:256], t, 0, 256, True) for t in range(2)], 1, 1)
                    for g in range(2):
                        yield from project_halves([(ps[:, 2 + t, :], t, 0, 512, True) for t in range(2)], 1, 2)
                    pe.wait_ge(y_lo, a0 + 2 * NH)
                    claim(1)
                    nk, wh, wl = next_unit()
                    for t in range(TT):
                        for j in range(nk):
                            mm = three(ps[:, 2 + t, :], yTh[:, j, t * P:(t + 1) * P], yTl[:, j, t * P:(t + 1) * P],
                                       wh[:, j, :], wl[:, j, :], j == 0, j == nk - 1)
                        if t == 0:
                            yield
                    used(mm)
                    step[1].n += 1
                    yield

                work = side()

                pe.wait_ge(keys_set, 2 * (L + 1))
                pe.wait_ge(vc_set, L + 1)
                scores(0)
                scores(1)
                for _ in range(BEFORE // 2):
                    next(work)
                pe.wait_ge(cs_prob, L + 1)
                for t in range(TT):
                    mm = pe.transpose(ps[:, 6, t * P:(t + 1) * P],
                                      pbuf[:, 1, :, :].rearrange("p a b -> p (a b)")[:, t * P:(t + 1) * P], ident)
                mm.then_inc(pct_turned, 1)
                for _ in range(BEFORE // 2):
                    next(work)
                pe.wait_ge(pct_set, L + 1)
                claim(0)
                for u in range(N_ATT):
                    if u + 2 < N_ATT:
                        if u + 2 == 2 * NH:
                            pe.wait_ge(fox_set, 4 * L + 3)
                        scores(u + 2)
                    turn_probs(u)
                    if u:
                        if u - 1 == 2 * NH:
                            pe.wait_ge(fox_set, 4 * (L + 1))
                        values(u - 1)
                    if u == CUM_AT:
                        claim(1)
                        pe.wait_ge(logf_set, L + 1)
                        pe.wait_ge(const_in, 32)
                        for t in range(TT):
                            for j in range(t + 1):
                                mm = pe.matmul(ps[:, 2, t * FH:(t + 1) * FH], tri[:, (t - j) * P:(t - j + 1) * P],
                                               logf[:, 2, j, :], start=(t == 0), stop=(j == t), skip_group_check=True)
                        full(mm, 1)
                    for _ in range(halves_done(u) - halves_done(u - 1)):
                        next(work)
                values(N_ATT - 1)
                pe.wait_ge(y_lo, a0 + N_ATT)

            def dense_ffn(names):
                ws = chunks(FF)

                def down(c):
                    pe.wait_ge(hT_lo, names["h0"] + c + 1)
                    kt = ws[c] // P
                    for i in range(down_units(ws[c])):
                        nk, wh, wl = next_unit()
                        for j in range(nk):
                            k = 2 * i + j
                            for t in range(TT):
                                for half in range(2):
                                    cs_ = slice(half * 512, (half + 1) * 512)
                                    mm = three(ps[:, 4 + 2 * t + half, :], hTh[:, k, t * P:(t + 1) * P],
                                               hTl[:, k, t * P:(t + 1) * P], wh[:, j, cs_], wl[:, j, cs_],
                                               c == 0 and k == 0, c == len(ws) - 1 and k == kt - 1)
                        used(mm)

                for c, width in enumerate(ws):
                    for g in range(2):
                        project([(ps[:, 2 * g + t, 0:width], t, 0, width, True) for t in range(2)], g, 2)
                    if c:
                        down(c - 1)
                    claim(1)
                    pe.wait_ge(h_set, names["h0"] + c + 1)
                    for f in range(width // P):
                        for t in range(TT):
                            a = (f % 2) * SEQ + t * P
                            mm = pe.transpose(ps[:, 2 + f // 2, a:a + P], h[:, t, f * P:(f + 1) * P], ident)
                    full(mm, 1)
                down(len(ws) - 1)

            pe.wait_ge(tab_set, 1)
            pe.wait_ge(onehot_in, 32)
            pe.matmul(ps[0:NH, 4, 0:OH_DOWN], tab, onehot[:, 0:OH_DOWN], start=True, stop=True).then_inc(vrow_full, 1)
            pe.wait_ge(const_in, 16)
            pe.wait_ge(x_in, 16)
            turn(x)
            mixer(0)
            pe.wait_ge(x_set, TT)
            turn(x)
            pe.wait_ge(split_lo, 6)
            if stop and stop["x_set"] <= 2:
                return
            dense_ffn({"h0": 0})
            pe.wait_ge(x_set, 2 * TT)
            turn(x)
            if stop and stop["x_set"] <= 4:
                return
            mixer(1)
            pe.wait_ge(x_set, 3 * TT)
            turn(x)
            pe.wait_ge(split_lo, 12)
            pe.wait_ge(router_lo, 1)
            claim(0)
            for t in range(TT):
                for k in range(KD):
                    es = slice(k * NE, (k + 1) * NE)
                    mm = three(ps[:, t, 0:NE], xTh[:, k, t * P:(t + 1) * P], xTl[:, k, t * P:(t + 1) * P],
                               rout_h[:, es], rout_l[:, es], k == 0, k == KD - 1)
            full(mm, 0)
            claim(1)
            pe.wait_ge(picks_set, 1)
            before, ones = table[:, K_SU:K_SU + P], table[:, K_ONE:K_ONE + P]
            for at, lhs in ((0, (before,)), (NE, (ones, before)), (2 * NE, (ones, ones))):
                for j, m in enumerate(lhs):
                    mm = pe.matmul(ps[:, 2, at:at + NE], m, r_mask[:, j, :], start=(at == 0), stop=(j == len(lhs) - 1),
                                   skip_group_check=True)
            full(mm, 1)

            claim(0)
            claim(1)

            def experts(S):
                unit = Tally(S.u0)

                def gather():
                    for k in range(KD):
                        for t in range(TT):
                            mm = pe.matmul(ps[:, 6 + k // 4, (k % 4) * P:(k % 4 + 1) * P], x[:, t, k * P:(k + 1) * P],
                                           pick[:, t, :], start=(t == 0), stop=(t == TT - 1), skip_group_check=True)
                    mm.then_inc(S.xe_full, 1)

                def take(nk, width):
                    pe.wait_ge(S.lo_ready, unit.at(1))
                    s = unit.n % CONV
                    return unit_view(hi, s, nk, width), unit_view(lo, s, nk, width)

                def leave_unit(mm):
                    mm.then_inc(S.unit_used, 1)
                    unit.n += 1

                def gate_or_up(bank):
                    for i in range(2):
                        wh, wl = take(KD // 2, CHUNK)
                        for j in range(KD // 2):
                            k = i * KD // 2 + j
                            mm = three(ps[:, bank, :], xeh[:, k * P:(k + 1) * P], xel[:, k * P:(k + 1) * P],
                                       wh[:, j, :], wl[:, j, :], k == 0, k == KD - 1)
                        leave_unit(mm)

                def gates_of(e, c):
                    pe.wait_ge(S.act_h, e * CH + (c + 1))
                    gate_or_up(0)

                def ups_of(e, c):
                    pe.wait_ge(S.hT_lo, e * CH + (c + 1))
                    gate_or_up(2)

                def turn_h(e, c):
                    pe.wait_ge(S.h_set, e * CH + (c + 1))
                    for f in range(FT):
                        mm = pe.transpose(ps[:, 2, f * P:(f + 1) * P], h[:, 0, f * P:(f + 1) * P], ident)
                    mm.then_inc(S.hT_full, 1)

                def down(e, c):
                    pe.wait_ge(S.hT_lo, e * CH + (c + 2))
                    for i in range(FT // 2):
                        wh, wl = take(2, D)
                        for j in range(2):
                            k = 2 * i + j
                            for half in range(2):
                                cols = slice(half * 512, (half + 1) * 512)
                                mm = three(ps[:, 4 + half, :], hTh1[:, k * P:(k + 1) * P], hTl1[:, k * P:(k + 1) * P],
                                           wh[:, j, cols], wl[:, j, cols], c == 0 and k == 0,
                                           c == CH - 1 and k == FT - 1)
                        leave_unit(mm)

                def body(e, last):
                    for c in range(1, CH):
                        gates_of(e, c)
                        ups_of(e, c)
                        if c == 1:
                            pe.wait_ge(S.sum_taken, e * 4 + 1)
                            for t in range(TT):
                                pe.transpose(ps[:, 1, t * P:(t + 1) * P], pick[:, t, :], ident)
                            for t in range(TT):
                                mm = pe.matmul(ps[:, 1, SEQ:SEQ + 1], pick[:, t, :], r_gate[:, t, bass.ds(e, 1)],
                                               start=False, stop=(t == TT - 1), skip_group_check=True)
                            mm.then_inc(S.pt_full, 1)
                            pe.wait_ge(S.ye_lo, e + 1)
                        if c == CH - 1 and not last:
                            pe.wait_ge(S.pick_set, e + 2)
                            pe.wait_ge(S.sum_taken, e * 4 + 4)
                            gather()
                        down(e, c - 1)
                        turn_h(e, c)
                    if not last:
                        pe.wait_ge(S.xe_lo, e + 2)
                        gates_of(e, CH)
                    down(e, CH - 1)
                    if not last:
                        ups_of(e, CH)
                    pe.wait_ge(S.ye_lo, e + 2)
                    pe.wait_ge(S.sum_taken, e * 4 + 4)
                    for k in range(4):
                        t, half = divmod(k, 2)
                        out, cols = ps[:, sum_bank(k), :], slice(half * 512, (half + 1) * 512)
                        pe.matmul(out, pickT[:, t * P:(t + 1) * P], yeh[:, cols], start=True, stop=False)
                        pe.matmul(out, pickT[:, t * P:(t + 1) * P], yel[:, cols], start=False, stop=True)\
                          .then_inc(S.sum_full, 1)
                    if not last:
                        turn_h(e, CH)

                if S.p:
                    pe.wait_ge(passes[0].sum_taken, 4 * (NE + 1))
                    pe.nop().then_inc(S.unit_used, RAW)
                pe.wait_ge(S.pick_set, 1)
                gather()
                pe.wait_ge(S.xe_lo, 1)
                gates_of(0, 0)
                ups_of(0, 0)
                turn_h(0, 0)
                with pe.Fori(0, NE - 1) as e:
                    unit.enter(e, EU)
                    body(e, False)
                    unit.leave(NE - 1)
                body(NE - 1, True)

            experts(passes[0])
            pe.wait_ge(flag_set, 1)
            again = pe.value_load(flag[0:1, 0:1], min_val=0, max_val=1)
            with pe.If(again == 1):
                experts(passes[1])

        AHEAD = 2

        @block.scalar
        def _(act):
            unit, use = Tally(), [Tally(), Tally()]

            def convert_to(n):
                while unit.n < min(n, len(units)):
                    nk, width, _ = units[unit.n]
                    size = nk * width
                    act.wait_ge(raw_in[unit.n % RAW], 16 * (unit.n // RAW + 1))
                    wait(act, unit_used, unit.n - CONV + 1)
                    act.activation(hi[:, unit.n % CONV, 0:size], raw[:, unit.n % RAW, 0:size], ACT.Copy
                                   ).then_inc(hi_ready, 1)
                    unit.n += 1

            def is_full(pair):
                use[pair].n += 1
                act.wait_ge(pair_full[pair], use[pair].at())

            def projected(n):
                act.wait_ge(unit_used, n)

            chain = Tally()

            def link(ins):
                chain.n += 1
                ins.then_inc(act_step, 1)
                act.wait_ge(act_step, chain.at())

            def pair(i):
                return ps[:, 2 * i:2 * i + 2, :].rearrange("p a b -> p (a b)")

            splits = Tally()

            def split_turned(pt):
                is_full(pt)
                act.activation(xTh[:, 4 * pt:4 * pt + 4, :].rearrange("p a b -> p (a b)"), pair(pt), ACT.Copy
                               ).then_inc(split_hi, 1)

            def mixer(L, u0):
                convert_to(u0 + 1 + AHEAD)
                act.wait_ge(pe_turned, L + 1)
                act.activation(pe_cols[:, :, :].rearrange("p v m -> p (v m)"), ps[:, 5, 0:32], ACT.Copy)\
                   .then_inc(pe_cols_set, 1)
                if L == 0:
                    act.wait_ge(cbias_full, 1)
                    for t in range(TT):
                        for hp in range(2):
                            act.activation(cbias[:, hp, t * 64:(t + 1) * 64].rearrange("p (i c) -> p i c", c=NCP),
                                           free(ps[:, 6 + t, 4 * hp:4 * hp + 1], [[1, 4], [NH, NCP]]), ACT.Copy)
                convert_to(u0 + 2 + AHEAD)
                act.wait_ge(blocks_set, L + 1)
                act.activation(yTh[:, 0:4, :].rearrange("p a b -> p (a b)"),
                               blocks[:, :, :, :].rearrange("p v m n -> p (v m n)"), ACT.Copy).then_inc(blh_set, 1)
                convert_to(u0 + 3 + AHEAD)
                projected(u0 + 3)
                act.activation(qk[:, 0:4, :].rearrange("p a b -> p (a b)"), pair(1), ACT.Copy, scale=SCALE)\
                   .then_inc(q_set, 1)
                act.wait_ge(q_set, L + 1)
                act.nop().then_inc(pair_free[1], 1)
                convert_to(u0 + 5 + AHEAD)
                projected(u0 + 5)
                act.activation(gkT, ps[:, 0, 0:2 * NCP], ACT.Gelu_apprx_tanh)
                act.activation(gvT.rearrange("p (g i c) -> p g i c", g=2, i=4),
                               free(ps[:, 1, 0:1], [[NCP, 2], [0, 4], [1, NCP]]), ACT.Gelu_apprx_tanh)\
                   .then_inc(gelu_set, 1)
                act.wait_ge(gelu_set, L + 1)
                act.nop().then_inc(pair_free[0], 1)
                convert_to(u0 + 6 + AHEAD)
                projected(u0 + 6)
                act.activation(ksw[:, 0, :], ps[:, 2, 0:SEQ], ACT.Copy)
                act.activation(vsw[:, 0, :, :], free(ps[:, 3, 0:1], [[SEQ, 2], [1, P]]), ACT.Copy)\
                   .then_inc(pair_free[1], 1)
                act.wait_ge(kcv_full, L + 1)
                act.activation(kcT, ps[:, 4, 0:NCP], ACT.Copy).then_inc(kc_set, 1)
                convert_to(u0 + 7 + AHEAD)
                act.wait_ge(cs_sub, L + 1)
                act.activation(cs[:, 0:256], cs[:, 0:256], ACT.Exp).then_inc(cs_exp, 1)
                convert_to(u0 + 8 + AHEAD)
                projected(u0 + 8)
                act.activation(ksw[:, 1, :], ps[:, 0, 0:SEQ], ACT.Copy)
                act.activation(vsw[:, 1, :, :], free(ps[:, 1, 0:1], [[SEQ, 2], [1, P]]), ACT.Copy)\
                   .then_inc(keys_set, 1)
                act.activation(gates[:, :, :], free(ps[:, 1, P:P + 1], [[SEQ, 2], [1, NG]]), ACT.Sigmoid)\
                   .then_inc(keys_set, 1)
                act.wait_ge(keys_set, 2 * (L + 1))
                act.nop().then_inc(pair_free[0], 1)
                attention(L, u0 + PRE)
                m0 = u0 + 15
                convert_to(m0 + 8 + AHEAD)
                act.wait_ge(merged_set, 2 * L + 1)
                for g in range(2):
                    convert_to(m0 + 6 + 2 * g + 2 + AHEAD)
                    projected(m0 + 6 + 2 * g + 2)
                    act.activation(sig[g], ps[:, 2 * (1 - g):2 * (1 - g) + 2, :], ACT.Sigmoid).then_inc(sig_set, 1)
                    act.wait_ge(sig_set, 4 * L + 2 + g + 1)
                    act.nop().then_inc(pair_free[1 - g], 1)
                convert_to(m0 + 12 + AHEAD)
                for pt in range(2):
                    split_turned(pt)
                convert_to(m0 + 12 + 4)
                norm(L * NLN)
                for pt in range(2):
                    split_turned(pt)

            def attention(L, s0):
                a0 = N_ATT * L

                def exps(u):
                    t = att_step(u)[1]
                    nk = P * (t + 1)
                    act.wait_ge(negmax_set, a0 + u + 1)
                    wait(act, pt_ready, a0 + u - 2)
                    for br in range(2):
                        ins = act.activation(pbuf[:, u % 3, br, 0:nk], pbuf[:, u % 3, br, 0:nk], ACT.Exp,
                                             bias=stats[:, u % 2, br:br + 1],
                                             accum_out=stats[:, u % 2, 4 + br:5 + br])
                    ins.then_inc(exp_done, 1)

                def copy_probs(u):
                    t = att_step(u)[1]
                    n = 2 * (t + 1) * P
                    act.wait_ge(pt_ready, a0 + u + 1)
                    wait(act, o_ready, a0 + u - 1)
                    act.activation(ptb[:, u % 2, 0:n], ps[:, 6 + u % 2, 0:n], ACT.Copy).then_inc(pt_copied, 1)

                def out_hi(u):
                    kind, t, a = att_step(u)
                    act.wait_ge(o_ready, a0 + u + 1)
                    b, n = (DH * (a // 4), DH) if kind == "nsa" else (0, P)
                    k = a % 4 if kind == "nsa" else 4 + a
                    act.activation(yTh[b:b + n, k, t * P:(t + 1) * P], ps[b:b + n, u % 2, 0:P], ACT.Copy)\
                       .then_inc(y_hi, 1)

                def side(u):
                    for name, n in side_ended(u):
                        projected(s0 + n)
                        if name == "values_b":
                            act.activation(fv[:, :, 256:512], free(ps[:, 2, 0:1], [[512, 2], [1, 256]]), ACT.Copy)\
                               .then_inc(fox_set, 1)
                        elif name == "queries":
                            act.activation(qk[:, 4:8, :].rearrange("p a b -> p (a b)"), pair(1), ACT.Copy,
                                           scale=SCALE).then_inc(fox_set, 1)
                            act.wait_ge(fox_set, 4 * L + 2)
                            act.nop().then_inc(pair_free[1], 1)
                        elif name == "keys":
                            act.activation(kv[:, 0:4, :].rearrange("p a b -> p (a b)"), pair(1), ACT.Copy)\
                               .then_inc(fox_set, 1)
                            act.wait_ge(fox_set, 4 * L + 3)
                            act.nop().then_inc(pair_free[1], 1)
                        elif name == "values_a":
                            act.activation(fv[:, :, 0:256], free(ps[:, 2, 0:1], [[512, 2], [1, 256]]), ACT.Copy)\
                               .then_inc(fox_set, 1)
                            act.wait_ge(fox_set, 4 * L + 4)
                            act.nop().then_inc(pair_free[1], 1)
                        elif name in ("gate0", "gate1"):
                            g = int(name[-1])
                            act.activation(sig[g], ps[:, 2:4, :], ACT.Sigmoid).then_inc(sig_set, 1)
                            act.wait_ge(sig_set, 4 * L + g + 1)
                            act.nop().then_inc(pair_free[1], 1)

                exps(0)
                act.wait_ge(pct_turned, L + 1)
                act.activation(pct, ps[:, 6, 0:256], ACT.Copy).then_inc(pct_set, 1)
                convert_to(s0 + BEFORE // 2 + AHEAD)
                side(-1)
                for u in range(N_ATT):
                    if u + 1 < N_ATT:
                        exps(u + 1)
                    if u:
                        side(u - 1)
                    else:
                        act.wait_ge(logits_set, L + 1)
                        act.activation(logf[:, 1, :, :], logf[:, 1, :, :], ACT.Exp, scale=-1.0).then_inc(lexp_set, 1)
                        act.wait_ge(lexp_set, L + 1)
                        act.activation(logf[:, 1, :, :], logf[:, 1, :, :], ACT.Ln, bias=1.0).then_inc(lln_set, 1)
                    copy_probs(u)
                    if u:
                        out_hi(u - 1)
                    convert_to(s0 + max(halves_done(u - 2), BEFORE) // 2 + CONV)
                use[1].n += 1
                out_hi(N_ATT - 1)

            def norm(n):
                for t in range(TT):
                    act.wait_ge(var_set, TT * n + t + 1)
                    act.activation(stats[:, t, 14:15], stats[:, t, 13:14], ACT.Sqrt, bias=eps[:, 0:1])\
                       .then_inc(std_set, 1)

            def dense_ffn(u0, n_norm):
                ws = chunks(FF)
                at = u0
                for c, width in enumerate(ws):
                    convert_to(at + 2 + AHEAD)
                    projected(at + 2)
                    at += 4
                    for t in range(TT):
                        ins = act.activation(h[:, t, 0:width], ps[:, t, 0:width], ACT.Silu)
                    ins.then_inc(act_h, 1)
                    if c:
                        at += down_units(ws[c - 1])
                    convert_to(at + AHEAD)
                    is_full(1)
                    act.activation(hTh[:, 0:width // P, :].rearrange("p a b -> p (a b)"), pair(1)[:, 0:2 * width], ACT.Copy)\
                       .then_inc(hT_hi, 1)
                at += down_units(ws[-1])
                convert_to(at)
                norm(n_norm)
                return at

            act.wait_ge(eps_set, 1)
            act.wait_ge(vrow_full, 1)
            act.activation(vrow, ps[0:NH, 4, 0:OH_DOWN], ACT.Copy).then_inc(vrow_set, 1)
            for pt in range(2):
                split_turned(pt)
            mixer(0, 0)
            if stop and stop["x_set"] <= 2:
                return
            at = dense_ffn(31, 1)
            for pt in range(2):
                split_turned(pt)
            if stop and stop["x_set"] <= 4:
                return
            mixer(1, at)
            act.wait_ge(router_in, 16)
            act.activation(rout_h, rout, ACT.Copy).then_inc(router_hi, 1)
            act.wait_ge(top_set, 1)
            act.activation(r_w[:, 1, :], r_w[:, 0, :], ACT.Exp).then_inc(texp_set, 1)

            def experts(S):
                unit = Tally(S.u0)

                def convert_to(n):
                    while unit.n < base + shift + n:
                        landed = 16 * (unit.n // RAW + 1 - S.p)
                        if unit.reg is not None:
                            landed = unit.reg * (16 * EU // RAW) + landed
                        act.wait_ge(S.raw_in[unit.n % RAW], landed)
                        act.wait_ge(S.unit_used, unit.at(1 - CONV))
                        act.activation(hi[:, unit.n % CONV, :], raw[:, unit.n % RAW, :], ACT.Copy
                                       ).then_inc(S.hi_ready, 1)
                        unit.n += 1

                def tokens_hi(n):
                    act.wait_ge(S.xe_full, n)
                    act.activation(xeh, ps[:, 6:8, :].rearrange("p a b -> p (a b)"), ACT.Copy).then_inc(S.xe_hi, 1)

                def silu(e, c, at):
                    act.wait_ge(S.unit_used, e * EU + (base + at + 2))
                    act.activation(h[:, 0, :], ps[:, 0, :], ACT.Silu).then_inc(S.act_h, 1)

                def turned_hi(e, c):
                    act.wait_ge(S.hT_full, e * CH + (c + 1))
                    act.activation(hTh1, ps[:, 2, :], ACT.Copy).then_inc(S.hT_hi, 1)

                def outputs_hi(e, n):
                    act.wait_ge(S.unit_used, e * EU + (base + n))
                    act.wait_ge(S.pt_set, e + 1)
                    act.activation(yeh, ps[:, 4:6, :].rearrange("p a b -> p (a b)"), ACT.Copy, scale=r_gs)\
                       .then_inc(S.ye_hi, 1)

                def body(e, last):
                    at = 0
                    for c in range(1, CH):
                        convert_to(at + 2 + AHEAD)
                        silu(e, c, at)
                        if c == 1:
                            convert_to(at + 4 + AHEAD)
                            act.wait_ge(S.pt_full, e + 1)
                            act.activation(pickT, ps[:, 1, 0:SEQ], ACT.Copy)
                            act.activation(r_gs, ps[:, 1, SEQ:SEQ + 1], ACT.Copy).then_inc(S.pt_set, 1)
                        if c == CH - 1 and not last:
                            convert_to(at + 4 + AHEAD)
                            tokens_hi(e + 2)
                        at += 6
                        convert_to(at + AHEAD)
                        turned_hi(e, c)
                    if not last:
                        convert_to(at + 2 + AHEAD)
                        silu(e, CH, at)
                        convert_to(at + 4 + AHEAD)
                        outputs_hi(e, at + 4)
                        convert_to(at + 6 + AHEAD)
                        turned_hi(e, CH)
                    else:
                        outputs_hi(e, at + 2)

                act.nop().then_inc(S.act_h, 1)
                if S.p:
                    act.nop().then_inc(S.hi_ready, RAW)
                tokens_hi(1)
                base, shift = S.u0, 0
                convert_to(2 + AHEAD)
                silu(0, 0, 0)
                convert_to(NF + AHEAD)
                turned_hi(0, 0)
                base = S.u0 + NF
                with act.Fori(0, NE - 1) as e:
                    unit.enter(e, EU)
                    body(e, False)
                    unit.leave(NE - 1)
                shift = EU * (NE - 1)
                body(NE - 1, True)

            experts(passes[0])
            act.wait_ge(flag_set, 1)
            again = act.value_load(flag[0:1, 0:1], min_val=0, max_val=1)
            with act.If(again == 1):
                experts(passes[1])
            norm(3)

        @block.vector
        def _(dve):
            unit, use, chain, splits = Tally(), [Tally(), Tally()], Tally(), Tally()

            def link(ins):
                chain.n += 1
                ins.then_inc(dve_step, 1)
                dve.wait_ge(dve_step, chain.at())

            def convert_to(n):
                while unit.n < min(n, len(units)):
                    nk, width, _ = units[unit.n]
                    size = nk * width
                    s = unit.n % CONV
                    dve.wait_ge(hi_ready, unit.at(1))
                    dve.tensor_tensor(lo[:, s, 0:size], raw[:, unit.n % RAW, 0:size], hi[:, s, 0:size].bitcast(F32),
                                      ALU.subtract).then_inc(lo_ready, 1)
                    unit.n += 1

            def is_full(pair):
                use[pair].n += 1
                dve.wait_ge(pair_full[pair], use[pair].at())

            def projected(n):
                dve.wait_ge(unit_used, n)

            def pair(i):
                return ps[:, 2 * i:2 * i + 2, :].rearrange("p a b -> p (a b)")

            def split_turned(pt):
                splits.n += 1
                use[pt].n += 1
                dve.wait_ge(split_hi, splits.n)
                sl = (slice(None), slice(4 * pt, 4 * pt + 4), slice(None))
                dve.tensor_tensor(xTl[sl].rearrange("p a b -> p (a b)"), pair(pt),
                                  xTh[sl].rearrange("p a b -> p (a b)").bitcast(F32), ALU.subtract)\
                   .then_inc(split_lo, 1)
                dve.wait_ge(split_lo, splits.n)
                dve.nop().then_inc(pair_free[pt], 1)

            def mixer(L, u0):
                convert_to(u0 + 1 + AHEAD)
                projected(u0 + 1)
                dve.wait_ge(pe_cols_set, L + 1)
                dve.memset(free(blocks[:, 0, 0, NC:NC + 1], [[NCP, 4 * CM]]), 0.0)
                for v in range(2):
                    for g in range(2):
                        for j in range(2):
                            src = ps[g * DH:(g + 1) * DH, v, j:j + 1]
                            ins = dve.tensor_tensor(
                                free(blocks[j * DH:(j + 1) * DH, v, 0, g * NCP:g * NCP + 1], [[2 * NCP, CM], [1, NC]]),
                                free(src, [[2, CM], [CMP_STRIDE, NC]]),
                                free(pe_cols[j * DH:(j + 1) * DH, v, 0:1], [[1, CM], [0, NC]]), ALU.add)
                link(ins)
                dve.nop().then_inc(blocks_set, 1)
                dve.nop().then_inc(pair_free[0], 1)
                convert_to(u0 + 2 + AHEAD)
                dve.wait_ge(blh_set, L + 1)
                dve.tensor_tensor(yTl[:, 0:4, :].rearrange("p a b -> p (a b)"),
                                  blocks[:, :, :, :].rearrange("p v m n -> p (v m n)"),
                                  yTh[:, 0:4, :].rearrange("p a b -> p (a b)").bitcast(F32), ALU.subtract)\
                   .then_inc(bll_set, 1)
                convert_to(u0 + 6 + AHEAD)
                dve.wait_ge(const_in, 32)
                dve.wait_ge(kcv_full, L + 1)
                link(dve.tensor_tensor(vcb[:, :, :], free(ps[:, 5, 0:1], [[0, NH], [1, DH]]),
                                       free(table[:, K_BLK:K_BLK + 1], [[1, NH], [0, DH]]), ALU.mult))
                dve.nop().then_inc(vc_set, 1)
                convert_to(u0 + 7 + AHEAD)
                dve.wait_ge(cscores_full, L + 1)
                c3 = cs[:, 0:256].rearrange("p (a c) -> p a c", c=NCP)
                if L:
                    dve.wait_ge(pt_ready, N_ATT * L)
                link(dve.tensor_tensor(cs[:, 0:256].rearrange("p (a b) -> p a b", a=2), ps[:, 6:8, 0:P],
                                       cbias[:, :, :], ALU.add))
                link(dve.tensor_reduce(csum[:, 0, :], c3, AX, ALU.max))
                link(dve.tensor_tensor(c3, c3, free(csum[:, 0, 0:1], [[1, 16], [0, NCP]]), ALU.subtract))
                dve.nop().then_inc(cs_sub, 1)
                dve.wait_ge(cs_exp, L + 1)
                link(dve.tensor_tensor(cs[:, 0:256], cs[:, 0:256], table[:, K_VIS:K_VIS + 256], ALU.mult))
                link(dve.tensor_reduce(csum[:, 1, :], c3, AX, ALU.add))
                link(dve.tensor_scalar(csum[:, 1, :], csum[:, 1, :], 1e-30, None, ALU.max))
                link(dve.reciprocal(csum[:, 2, :], csum[:, 1, :]))
                convert_to(u0 + 8 + AHEAD)
                dve.wait_ge(keys_set, 2 * (L + 1))
                link(dve.tensor_tensor(csum[:, 3, :].rearrange("p (a t i) -> p a t i", a=2, t=2),
                                       csum[:, 2, :].rearrange("p (a t i) -> p a t i", a=2, t=2),
                                       free(gates[:, 0, 0:1], [[12, 2], [NG, 2], [3, 4]]), ALU.mult))
                cp = pbuf[:, 1, :, :].rearrange("p a b -> p (a b)")
                for hp in range(2):
                    ins = dve.tensor_tensor(
                        free(cp[:, hp * 64:hp * 64 + 1], [[P, 2], [NCP, 4], [1, NCP]]),
                        c3[:, 8 * hp:8 * hp + 8, :].rearrange("p (t i) c -> p t i c", t=2),
                        free(csum[:, 3, 8 * hp:8 * hp + 1], [[4, 2], [1, 4], [0, NCP]]), ALU.mult)
                link(ins)
                dve.nop().then_inc(cs_prob, 1)
                attention(L, u0 + PRE)
                m0 = u0 + 15
                for half in range(2):
                    if half:
                        convert_to(m0 + 11 + AHEAD)
                        projected(m0 + 11)
                        dve.wait_ge(sig_set, 4 * L + 3)
                        link(dve.tensor_tensor(sig[0], ps[:, 2:4, :], sig[0], ALU.mult))
                        dve.nop().then_inc(pair_free[1], 1)
                    convert_to(m0 + 6 * half + 6 + AHEAD)
                    mh = merged[:, :, half * 512:(half + 1) * 512]
                    projected(m0 + 6 * half + 6)
                    dve.wait_ge(sig_set, 4 * L + 2 * half + 2)
                    link(dve.tensor_tensor(sig[1], ps[:, 0:2, :], sig[1], ALU.mult))
                    dve.nop().then_inc(pair_free[0], 1)
                    link(dve.tensor_tensor(mh, sig[0], sig[1], ALU.add))
                    dve.nop().then_inc(merged_set, 1)
                for pt in range(2):
                    split_turned(pt)
                convert_to(m0 + 12 + 4)
                projected(m0 + 12 + 4)
                norm(L * NLN, lambda t, half: ps[:, 2 * half + t, :])
                for pt in range(2):
                    dve.nop().then_inc(pair_free[pt], 1)
                for pt in range(2):
                    split_turned(pt)

            def attention(L, s0):
                a0 = N_ATT * L

                def scores(u):
                    kind, t, a = att_step(u)
                    nk = P * (t + 1)
                    dve.wait_ge(s_ready, a0 + u + 1)
                    wait(dve, pt_ready, a0 + u - 2)
                    pu = pbuf[:, u % 3, :, 0:nk]
                    k0 = SEQ - nk
                    if kind == "nsa":
                        ins = dve.tensor_tensor(pu, scores_at(u, nk), free(toep[:, a, k0:k0 + 1], [[0, 2], [1, nk]]),
                                                ALU.add)
                    else:
                        for hh in range(2):
                            c0 = (u % 2) * SEQ
                            ins = dve.scalar_tensor_tensor(pu[:, hh, :], ps[:, 4 + hh, c0:c0 + nk],
                                                           fcum[:, t, 2 * a + hh:2 * a + hh + 1],
                                                           table[:, K_MASK + k0:K_MASK + SEQ], ALU.add, ALU.add)
                    link(ins)
                    dve.nop().then_inc(s_taken, 1)
                    dve.tensor_reduce(stats[:, u % 2, 0:2], pu, AX, ALU.max, negate=True).then_inc(negmax_set, 1)

                def factors(u):
                    kind, t, a = att_step(u)
                    dve.wait_ge(exp_done, a0 + u + 1)
                    wait(dve, p_scaled, a0 + u - 1)
                    st = stats[:, u % 2, :]
                    link(dve.tensor_scalar(st[:, 4:6], st[:, 4:6], 1e-30, None, ALU.max))
                    if kind == "nsa":
                        link(dve.reciprocal(st[:, 6:8], st[:, 4:6]))
                        ins = dve.tensor_tensor(st[:, 8:10], st[:, 6:8], gates[:, t, 3 * a + 1:3 * a + 3], ALU.mult)
                    else:
                        ins = dve.reciprocal(st[:, 8:10], st[:, 4:6])
                    ins.then_inc(norm_set, 1)

                def out_lo(u):
                    kind, t, a = att_step(u)
                    dve.wait_ge(y_hi, a0 + u + 1)
                    b, n = (DH * (a // 4), DH) if kind == "nsa" else (0, P)
                    k = a % 4 if kind == "nsa" else 4 + a
                    dve.tensor_tensor(yTl[b:b + n, k, t * P:(t + 1) * P], ps[b:b + n, u % 2, 0:P],
                                      yTh[b:b + n, k, t * P:(t + 1) * P].bitcast(F32), ALU.subtract).then_inc(y_lo, 1)

                if L == 0:
                    dve.wait_ge(toep_in, 16)
                scores(0)
                dve.wait_ge(pct_turned, L + 1)
                scores(1)
                convert_to(s0 + BEFORE // 2 + AHEAD)
                projected(s0 + BEFORE // 2)
                dve.wait_ge(fox_set, 4 * L + 1)
                link(dve.tensor_tensor(logf[:, 0, :, :], free(ps[:, 2, 256:257], [[512, 2], [1, FH]]),
                                       free(fbias[:, 0:1], [[0, 2], [1, FH]]), ALU.add))
                dve.nop().then_inc(pair_free[1], 1)
                link(dve.tensor_scalar(logf[:, 2, :, :], logf[:, 0, :, :], 0.0, None, ALU.min))
                link(dve.scalar_tensor_tensor(logf[:, 1, :, :], logf[:, 2, :, :], -2.0, logf[:, 0, :, :],
                                              ALU.mult, ALU.add))
                dve.nop().then_inc(logits_set, 1)
                for u in range(N_ATT):
                    factors(u)
                    if u + 2 < N_ATT:
                        scores(u + 2)
                    if u == 1:
                        dve.wait_ge(lln_set, L + 1)
                        link(dve.tensor_tensor(logf[:, 2, :, :], logf[:, 2, :, :], logf[:, 1, :, :], ALU.subtract))
                        link(dve.tensor_scalar(logf[:, 3, :, :], logf[:, 2, :, :], -1.0, None, ALU.mult))
                        dve.nop().then_inc(logf_set, 1)
                    if u == CUM_AT + 1:
                        is_full(1)
                        link(dve.tensor_copy(fcum[:, :, :].rearrange("p t h -> p (t h)"), ps[:, 2, 0:TT * FH]))
                        dve.nop().then_inc(pair_free[1], 1)
                    if ("nsa_out", 12) in side_ended(u - 1):
                        projected(s0 + 12)
                        dve.wait_ge(sig_set, 4 * L + 1)
                        link(dve.tensor_tensor(sig[0], ps[:, 2:4, :], sig[0], ALU.mult))
                        dve.nop().then_inc(pair_free[1], 1)
                    if u > 1:
                        out_lo(u - 2)
                    convert_to(s0 + max(halves_done(u - 3), BEFORE) // 2 + CONV)
                out_lo(N_ATT - 2)
                out_lo(N_ATT - 1)

            def norm(n, src, tiles=range(TT)):
                dve.wait_ge(lng_in, 32 * (n + 1))
                for t in tiles:
                    st = stats[:, t, :]
                    for half in range(2):
                        xs = x[:, t, half * 512:(half + 1) * 512]
                        ins = dve.scalar_tensor_tensor(xs, xs, ALPHA, src(t, half), ALU.mult, ALU.add)
                    link(ins)
                    bn = small[:, 448 + 16 * t:448 + 16 * t + 12].rearrange("p (a b) -> p a b", a=2)
                    for half in range(2):
                        ins = dve.bn_stats(bn[:, half, :], x[:, t, half * 512:(half + 1) * 512])
                    link(ins)
                    dve.bn_aggr(st[:, 12:14], small[:, 448 + 16 * t:448 + 16 * t + 12]).then_inc(var_set, 1)
                for t in tiles:
                    st, xs = stats[:, t, :], x[:, t, :]
                    dve.wait_ge(std_set, TT * n + t + 1)
                    link(dve.reciprocal(st[:, 15:16], st[:, 14:15]))
                    link(dve.tensor_scalar(xs, xs, st[:, 12:13], st[:, 15:16], ALU.subtract, ALU.mult))
                    link(dve.tensor_tensor(xs, xs, lng[:, 0, :], ALU.mult))
                    dve.tensor_tensor(xs, xs, lng[:, 1, :], ALU.add).then_inc(x_set, 1)
                dve.wait_ge(x_set, TT * (n + 1))

            def dense_ffn(u0, n_norm):
                ws = chunks(FF)
                at = u0
                for c, width in enumerate(ws):
                    at += 4
                    convert_to(at + AHEAD)
                    projected(at)
                    dve.wait_ge(act_h, c + 1)
                    dve.nop().then_inc(pair_free[0], 1)
                    hc = h[:, :, 0:width]
                    link(dve.tensor_tensor(hc, hc, ps[:, 2:4, 0:width], ALU.mult))
                    dve.nop().then_inc(h_set, 1)
                    dve.nop().then_inc(pair_free[1], 1)
                    if c:
                        at += down_units(ws[c - 1])
                    convert_to(at + AHEAD)
                    use[1].n += 1
                    dve.wait_ge(hT_hi, c + 1)
                    n = 2 * width
                    link(dve.tensor_tensor(hTl[:, 0:width // P, :].rearrange("p a b -> p (a b)"), pair(1)[:, 0:n],
                                           hTh[:, 0:width // P, :].rearrange("p a b -> p (a b)").bitcast(F32),
                                           ALU.subtract))
                    dve.nop().then_inc(hT_lo, 1)
                    dve.nop().then_inc(pair_free[1], 1)
                at += down_units(ws[-1])
                convert_to(at)
                projected(at)
                norm(n_norm, lambda t, half: ps[:, 4 + 2 * t + half, :])
                return at

            dve.memset(eps[:, :], LN_EPS).then_inc(eps_set, 1)
            dve.memset(tab[BUCKETS:BUCKETS + 1, :], NEG).then_inc(tab_set, 1)
            for pt in range(2):
                split_turned(pt)
            mixer(0, 0)
            if stop and stop["x_set"] <= 2:
                return
            at = dense_ffn(31, 1)
            for pt in range(2):
                split_turned(pt)
            if stop and stop["x_set"] <= 4:
                return
            mixer(1, at)
            dve.wait_ge(router_hi, 1)
            dve.tensor_tensor(rout_l, rout, rout_h.bitcast(F32), ALU.subtract).then_inc(router_lo, 1)
            is_full(0)
            link(dve.tensor_copy(r_logits, ps[:, 0:2, 0:NE]))
            dve.nop().then_inc(pair_free[0], 1)
            for t in range(TT):
                ins = dve.max(r_top[:, t, :], r_logits[:, t, :])
            link(ins)
            for t in range(TT):
                ins = dve.max_index(r_index[:, t, :].bitcast(U32), r_top[:, t, :], r_logits[:, t, :])
            link(ins)
            link(dve.tensor_copy(r_indexf, r_index.bitcast(U32)))
            iota8 = table[:, K_IOTA:K_IOTA + NE]
            for k, one in enumerate((r_one, r_two)):
                for t in range(TT):
                    ins = dve.tensor_scalar(one[:, t, :], iota8, r_indexf[:, t, k:k + 1], None, ALU.is_equal)
            link(ins)
            link(dve.tensor_tensor(r_mask, r_one, r_two, ALU.add))
            dve.nop().then_inc(picks_set, 1)
            link(dve.tensor_tensor(r_w[:, 0, :], free(r_top[:, 0, 1:2], [[NE, 2]]), free(r_top[:, 0, 0:1], [[NE, 2]]),
                                   ALU.subtract))
            dve.nop().then_inc(top_set, 1)
            dve.wait_ge(texp_set, 1)
            link(dve.tensor_scalar(r_w[:, 0, :], r_w[:, 1, :], 1.0, None, ALU.add))
            link(dve.reciprocal(r_w[:, 2, :], r_w[:, 0, :]))
            link(dve.tensor_tensor(r_w[:, 3, :], r_w[:, 1, :], r_w[:, 2, :], ALU.mult))
            for t in range(TT):
                ins = dve.tensor_scalar(r_gate[:, t, 0:NE], r_one[:, t, :], r_w[:, 2, t:t + 1], None, ALU.mult)
            link(ins)
            for t in range(TT):
                ins = dve.scalar_tensor_tensor(r_gate[:, t, 0:NE], r_two[:, t, :], r_w[:, 3, t:t + 1],
                                               r_gate[:, t, 0:NE], ALU.mult, ALU.add)
            link(ins)
            is_full(1)
            slots = r_slot[:, :, 0:NE]
            places = ps[:, 2, 0:2 * NE].rearrange("p (t e) -> p t e", t=TT)
            link(dve.scalar_tensor_tensor(slots, r_mask, -FAR, places, ALU.mult, ALU.add))
            link(dve.tensor_scalar(slots, slots, FAR, None, ALU.add))
            link(dve.tensor_reduce(r_count, ps[:, 2, 2 * NE:3 * NE], AX, ALU.max))
            dve.nop().then_inc(pair_free[1], 1)
            dve.tensor_scalar(flag[:, :], r_count, CAP + 0.5, None, ALU.is_gt).then_inc(flag_set, 1)
            link(dve.memset(acc, 0.0))

            def experts(S):
                unit = Tally(S.u0)

                def convert_to(n):
                    while unit.n < base + shift + n:
                        s = unit.n % CONV
                        dve.wait_ge(S.hi_ready, unit.at(1))
                        dve.tensor_tensor(lo[:, s, :], raw[:, unit.n % RAW, :], hi[:, s, :].bitcast(F32),
                                          ALU.subtract).then_inc(S.lo_ready, 1)
                        unit.n += 1

                def select(e):
                    dve.tensor_tensor(pick, free(table[:, K_IOTA:K_IOTA + 1], [[0, TT], [1, P]]),
                                      r_slot[:, :, bass.ds(e, 1)].broadcast_to([P, TT, P]), ALU.is_equal)\
                       .then_inc(S.pick_set, 1)

                def tokens_lo(n):
                    dve.wait_ge(S.xe_hi, n)
                    dve.tensor_tensor(xel, ps[:, 6:8, :].rearrange("p a b -> p (a b)"), xeh.bitcast(F32), ALU.subtract)\
                       .then_inc(S.xe_lo, 1)

                def times_up(e, c, at):
                    dve.wait_ge(S.unit_used, e * EU + (base + at))
                    dve.wait_ge(S.act_h, e * CH + (c + 2))
                    dve.tensor_tensor(h[:, 0, :], h[:, 0, :], ps[:, 2, :], ALU.mult).then_inc(S.h_set, 1)

                def turned_lo(e, c):
                    dve.wait_ge(S.hT_hi, e * CH + (c + 1))
                    dve.tensor_tensor(hTl1, ps[:, 2, :], hTh1.bitcast(F32), ALU.subtract).then_inc(S.hT_lo, 1)

                def outputs_lo(e):
                    dve.wait_ge(S.ye_hi, e + 1)
                    dve.scalar_tensor_tensor(yel, ps[:, 4:6, :].rearrange("p a b -> p (a b)"), r_gs,
                                             yeh.bitcast(F32), ALU.mult, ALU.subtract).then_inc(S.ye_lo, 1)

                def sums(e):
                    dve.wait_ge(S.sum_taken, e * 4 + 4)
                    for k in range(4):
                        t, half = divmod(k, 2)
                        to = acc[:, t, half * 512:(half + 1) * 512]
                        dve.wait_ge(S.sum_full, e * 4 + (k + 1))
                        dve.tensor_tensor(to, to, ps[:, sum_bank(k), :], ALU.add).then_inc(S.sum_taken, 1)

                def body(e, last):
                    at = 0
                    for c in range(1, CH):
                        at += 4
                        convert_to(at + AHEAD)
                        times_up(e, c, at)
                        if c == 1 and not last:
                            dve.wait_ge(S.pt_full, e + 1)
                            select(e + 1)
                        if c == CH - 1 and not last:
                            tokens_lo(e + 2)
                        at += 2
                        convert_to(at + AHEAD)
                        turned_lo(e, c)
                    if not last:
                        convert_to(at + 4 + AHEAD)
                        outputs_lo(e)
                        convert_to(at + 6 + AHEAD)
                        times_up(e, CH, at + 6)
                        sums(e)
                        turned_lo(e, CH)
                    else:
                        outputs_lo(e)
                        sums(e)
                        dve.wait_ge(S.sum_taken, 4 * (NE + 1))

                dve.nop().then_inc(S.hT_lo, 1)
                dve.nop().then_inc(S.ye_lo, 1)
                dve.nop().then_inc(S.sum_taken, 4)
                if S.p:
                    dve.tensor_scalar(slots, slots, float(CAP), None, ALU.subtract).then_inc(slots_moved, 1)
                    dve.wait_ge(slots_moved, 1)
                    dve.nop().then_inc(S.lo_ready, RAW)
                select(0)
                tokens_lo(1)
                base, shift = S.u0, 0
                convert_to(NF + AHEAD)
                times_up(0, 0, NF)
                turned_lo(0, 0)
                base = S.u0 + NF
                with dve.Fori(0, NE - 1) as e:
                    unit.enter(e, EU)
                    body(e, False)
                    unit.leave(NE - 1)
                shift = EU * (NE - 1)
                body(NE - 1, True)

            experts(passes[0])
            dve.wait_ge(flag_set, 1)
            again = dve.value_load(flag[0:1, 0:1], min_val=0, max_val=1)
            with dve.If(again == 1):
                experts(passes[1])
            norm(3, lambda t, half: acc[:, t, half * 512:(half + 1) * 512])


_INS = ["x", "w_in", "nsa_cmp_pe", "nsa_cmp_w1", "nsa_cmp_w2", "fox_f_bias", "w_nsa_branch", "w_fox_branch",
        "w_out", "rel_bias", "ln1_g", "ln1_b", "ln2_g", "ln2_b", "dense_w_gate", "dense_w_up", "dense_w_down",
        "moe_router", "moe_w_gate", "moe_w_up", "moe_w_down"]

STOP = None


def kernel(**inputs):
    import numpy as _np
    import concourse.bacc as _bacc
    from concourse import mybir as _mybir
    from concourse.bass_utils import run_bass_kernel_spmd as _run

    nc = _bacc.Bacc("TRN2", target_bir_lowering=False, num_devices=1)
    table, onehot = constants()
    arrays, io = {}, {}
    for name in _INS + ["table", "onehot"]:
        a = {"table": table, "onehot": onehot}[name] if name in ("table", "onehot") else _np.ascontiguousarray(inputs[name])
        if name == "w_in":
            q = a[:, :, :512].reshape(DEPTH, D, 2, 4, DH).transpose(0, 1, 3, 2, 4).reshape(DEPTH, D, 512)
            a = _np.concatenate([q, a[:, :, 512:]], axis=2)
        if name == "w_nsa_branch":
            a = _np.ascontiguousarray(a.reshape(DEPTH, 2, 4, DH, D).transpose(0, 2, 1, 3, 4).reshape(DEPTH, 512, D))
        arrays[f"in_{name}"] = a
        io[name] = nc.dram_tensor(f"in_{name}", a.shape, _mybir.dt.from_np(a.dtype), kind="ExternalInput").ap()
    io["out"] = nc.dram_tensor("out_0", (1, SEQ, D), _mybir.dt.float32, kind="ExternalOutput").ap()
    hybrid_kernel(nc, io, STOP)
    r = _run(nc, [arrays], core_ids=[0])
    return r.results[0]["out_0"]
```

```python
from contextlib import ExitStack

import numpy as np

import concourse.bass as bass
from concourse import mybir

F32 = mybir.dt.float32
F32R = mybir.dt.float32r
U32 = mybir.dt.uint32
I32 = mybir.dt.int32
ALU = mybir.AluOpType
ACT = mybir.ActivationFunctionType
AX = mybir.AxisListType.X

P = 128
D = 1024
KD = D // P
SEQ = 256
TT = SEQ // P
DEPTH = 2
DH = 64
NH = 8
NKV = 2
FH = 8
CMP_BLOCK, CMP_STRIDE, CMP_HID = 32, 16, 128
NC = SEQ // CMP_STRIDE - CMP_BLOCK // CMP_STRIDE + 1
NCP = 16
CM = CMP_BLOCK // 2
BUCKETS, MAX_DIST = 32, 128
FF = 2816
FE = 3584
NE = 8
ALPHA = (2 * DEPTH) ** 0.25
LN_EPS = 1e-5
NEG = -1e30
SCALE = DH ** -0.5
FAR = 1e4

C_Q, C_KC, C_KS, C_KW = 0, 512, 768, 1024
C_FQ, C_FK, C_FV = 1304, 1816, 2328
C_MERGE = 2848
NG = 3 * NH

RAW = 6
CONV = 3
UNIT = 2048
CHUNK = 512
CAP = P

K_ID, K_U, K_MASK, K_VIS, K_IOTA, K_SU, K_ONE, K_BLK = 0, 128, 384, 640, 896, 1024, 1152, 1280
K_END = K_BLK + NH
OH_DOWN, OH_UP0 = 384, 272
OH_UP = OH_UP0 + SEQ


def constants():
    c = np.zeros((P, K_END), np.float32)
    p = np.arange(P)[:, None]
    c[:, K_ID:K_ID + P] = np.eye(P)
    c[:, K_U:K_U + SEQ] = p <= np.arange(SEQ)[None]
    c[:, K_MASK:K_MASK + SEQ] = np.where(np.arange(SEQ)[None] > p + P, NEG, 0.0)
    end = np.arange(NCP) * CMP_STRIDE + CMP_BLOCK - 1
    for t in range(TT):
        vis = (end[None] <= t * P + p) & (np.arange(NCP)[None] < NC)
        for hp in range(2):
            for i in range(NH // 2):
                at = K_VIS + hp * P + t * 64 + i * NCP
                c[:, at:at + NCP] = vis
    c[:, K_IOTA:K_IOTA + P] = np.where(np.arange(P) < CAP, np.arange(P), -2 * FAR)[None]
    c[:, K_SU:K_SU + P] = p < np.arange(P)[None]
    c[:, K_ONE:K_ONE + P] = 1.0
    c[:, K_BLK:K_BLK + NH] = p // NCP == np.arange(NH)[None]

    def onehot(dist):
        n = np.maximum(dist, 0)
        exact = BUCKETS // 2
        far = exact + (np.log(np.maximum(n, 1).astype(np.float32) / exact) / np.log(MAX_DIST / exact)
                       * (BUCKETS - exact)).astype(np.int32)
        bucket = np.where(n < exact, n, np.minimum(far, BUCKETS - 1))
        out = np.zeros((BUCKETS + 1, len(dist)), np.float32)
        out[bucket, np.arange(len(dist))] = dist >= 0
        out[BUCKETS] = dist < 0
        return out

    oh = np.concatenate([onehot(SEQ - 1 - np.arange(OH_DOWN)), onehot(np.arange(OH_UP) - OH_UP0)], 1)
    return c, np.ascontiguousarray(oh)


def free(ap, dims):
    return bass.AP(tensor=ap.tensor, offset=ap.offset, ap=[list(ap.ap[0])] + [list(d) for d in dims])


class Tally:

    def __init__(self, n=0):
        self.n, self.reg, self.per, self.start = n, None, 0, 0

    def at(self, more=0):
        v = self.n + more
        return v if self.reg is None else self.reg * self.per + v

    def enter(self, reg, per):
        self.reg, self.per, self.start = reg, per, self.n

    def leave(self, trips):
        assert self.n == self.start + self.per, (self.n, self.start, self.per)
        self.reg, self.n = None, self.start + self.per * trips


def wait(eng, sem, value):
    if isinstance(value, int) and value <= 0:
        return
    eng.wait_ge(sem, value)


def hybrid_kernel(nc, io):
    w_in, w_nb, w_fb, w_out = io["w_in"], io["w_nsa_branch"], io["w_fox_branch"], io["w_out"]

    units = []

    def add(nk, width, parts):
        units.append((nk, width, parts))

    def rows(w, k0, nk, c0, width):
        return w[k0 * P:(k0 + nk) * P, c0:c0 + width].rearrange("(k p) n -> p k n", p=P)

    def add_cols(w, c0, width, kt=KD):
        n = 1 if kt * width <= UNIT else 2
        for h in range(n):
            add(kt // n, width, rows(w, h * kt // n, kt // n, c0, width))

    def add_mixer(L):
        add_cols(w_in[L], C_KC, 256)
        add_cols(w_in[L], C_Q, 512)
        for kv in range(2):
            add(CM, CMP_HID, rows(io["nsa_cmp_w1"][L, kv], 0, CM, 0, CMP_HID))
        add_cols(w_in[L], C_KS, 256)
        add_cols(w_in[L], C_KW, 256 + NG)
        add_cols(w_in[L], C_FV + 256, 256 + FH)
        add_cols(w_in[L], C_FQ, 512)
        add_cols(w_in[L], C_FK, 512)
        add_cols(w_in[L], C_FV, 256)
        for half in range(2):
            for g in range(half, 2):
                add_cols(w_in[L], C_MERGE + g * D + half * 512, 512)
            add_cols(w_nb[L], half * 512, 512, 4)
            if half == 0:
                add_cols(w_in[L], C_MERGE + 512, 512)
            add_cols(w_fb[L], half * 512, 512, 4)
        for h in range(2):
            for half in range(2):
                add(KD // 2, 512, rows(w_out[L], h * KD // 2, KD // 2, half * 512, 512))

    def chunks(total):
        return [min(CHUNK, total - c) for c in range(0, total, CHUNK)]

    def down_units(width):
        return width // P // 2

    def ffn_order(total):
        ws = chunks(total)
        out = []
        for c, width in enumerate(ws):
            out += [("gate", c, 0), ("gate", c, 1), ("up", c, 0), ("up", c, 1)]
            if c:
                out += [("down", c - 1, i) for i in range(down_units(ws[c - 1]))]
        return out + [("down", len(ws) - 1, i) for i in range(down_units(ws[-1]))]

    def ffn_unit(gate, up, down, total, kind, c, i):
        width = chunks(total)[c]
        if kind == "down":
            return 2, D, rows(down, c * CHUNK // P + 2 * i, 2, 0, D)
        return KD // 2, width, rows(gate if kind == "gate" else up, i * KD // 2, KD // 2, c * CHUNK, width)

    add_mixer(0)
    mixer_units = len(units)
    for u in ffn_order(FF):
        add(*ffn_unit(io["dense_w_gate"][0], io["dense_w_up"][0], io["dense_w_down"][0], FF, *u))
    add_mixer(1)
    CH = len(chunks(FE))
    moe_first = [(w, 0, i) for w in ("gate", "up") for i in range(2)]
    moe_body = [u for c in range(1, CH) for u in
                [("gate", c, 0), ("gate", c, 1), ("up", c, 0), ("up", c, 1), ("down", c - 1, 0), ("down", c - 1, 1)]]
    moe_down = [("down", CH - 1, i) for i in range(2)]

    ctx = ExitStack()
    with ctx:
        def sb(name, shape, dt=F32):
            return ctx.enter_context(nc.sbuf_tensor(name, shape, dt))

        def sem(name):
            return ctx.enter_context(nc.semaphore(name))

        raw = sb("raw", [P, RAW, UNIT])
        hi = sb("hi", [P, CONV, UNIT], F32R)
        lo = sb("lo", [P, CONV, UNIT], F32R)
        x = sb("x", [P, TT, D])
        xTh = sb("xTh", [P, KD, SEQ], F32R)
        xTl = sb("xTl", [P, KD, SEQ], F32R)
        yTh = sb("yTh", [P, KD, SEQ], F32R)
        yTl = sb("yTl", [P, KD, SEQ], F32R)
        table = sb("table", [P, K_END])
        toep = sb("toep", [P, NH, SEQ])
        cbias = sb("cbias", [P, 2, TT * 4 * NCP])
        qk = sb("qk", [P, 8, SEQ])
        kv = sb("kv", [P, 8, SEQ])
        ksw = sb("ksw", [P, 2, SEQ])
        vsw = sb("vsw", [P, 2, TT, P])
        gates = sb("gates", [P, TT, NG])
        logf = sb("logf", [P, 4, TT, FH])
        fcum = sb("fcum", [P, TT, FH])
        blocks = sb("blocks", [P, 2, CM, 2 * NCP])
        small = sb("small", [P, 480])
        pbuf = sb("pbuf", [P, 3, 2, SEQ])
        ptb = sb("ptb", [P, 2, 512])
        lng = sb("lng", [P, 2, D])
        hTh = sb("hTh", [P, 4, SEQ], F32R)
        hTl = sb("hTl", [P, 4, SEQ], F32R)
        vcb = sb("vcb", [P, NH, DH])
        cmpw2 = sb("cmpw2", [P, 2, DH])
        pe_rows = sb("pe_rows", [32, P])
        pe_cols = sb("pe_cols", [P, 2, CM])
        fbias = sb("fbias", [P, FH])
        stats = sb("stats", [P, TT, 16])
        eps = sb("eps", [P, 1])
        flag = sb("flag", [P, 1], I32)
        ps = ctx.enter_context(nc.psum_tensor("ps", [P, 8, 512], F32))

        ident = table[:, K_ID:K_ID + P]
        tri = table[:, K_U:K_U + SEQ]
        merged = qk[:, :, :].rearrange("p a b -> p (a b)").rearrange("p (t n) -> p t n", t=TT)
        fkT = kv[:, 0:4, :]
        fv = kv[:, 4:8, :].rearrange("p a b -> p (a b)").rearrange("p (t n) -> p t n", t=TT)
        blh = yTh[:, 0:4, :].rearrange("p a b -> p (a b)").rearrange("p (v m n) -> p v m n", v=2, m=CM)
        bll = yTl[:, 0:4, :].rearrange("p a b -> p (a b)").rearrange("p (v m n) -> p v m n", v=2, m=CM)
        h = blocks[:, :, :, :].rearrange("p v m n -> p (v m n)").rearrange("p (t n) -> p t n", t=TT)
        sig = [h, lng[:, 0, :].rearrange("p (t n) -> p t n", t=TT)]
        onehot = kv[0:BUCKETS + 1, 0:4, :].rearrange("p a b -> p (a b)")[:, 0:OH_DOWN + OH_UP]
        tab = small[0:BUCKETS + 1, 0:NH]
        vrow = ptb[0:NH, 0, 0:OH_DOWN]
        gkT = small[:, 0:2 * NCP]
        kcT = small[:, 64:64 + NCP]
        gvT = small[:, 128:256]
        pct = small[:, 128:384]
        csum = small[:, 384:448].rearrange("p (a b) -> p a b", a=4)
        cs = pbuf[:, 0, :, :].rearrange("p a b -> p (a b)")

        scratch = nc.dram_tensor("bias_rows", (P, NH, OH_DOWN), F32, kind="Internal").ap()

        const_in, x_in, small_in, lng_in = sem("const_in"), sem("x_in"), sem("small_in"), sem("lng_in")
        onehot_in, vrow_out, toep_in = sem("onehot_in"), sem("vrow_out"), sem("toep_in")
        raw_in = [sem(f"raw_in{i}") for i in range(RAW)]
        hi_ready, lo_ready, unit_used = sem("hi_ready"), sem("lo_ready"), sem("unit_used")
        pair_full = [sem("pair_full0"), sem("pair_full1")]
        pair_free = [sem("pair_free0"), sem("pair_free1")]
        dve_step = sem("dve_step")
        eps_set, tab_set, vrow_full, vrow_set, pe_turned, pe_cols_set, cbias_full = (
            sem("eps_set"), sem("tab_set"), sem("vrow_full"), sem("vrow_set"), sem("pe_turned"), sem("pe_cols_set"),
            sem("cbias_full"))
        kcv_full, cscores_full = sem("kcv_full"), sem("cscores_full")
        turned, split_hi, split_lo = sem("turned"), sem("split_hi"), sem("split_lo")
        q_set, keys_set, blocks_set, blh_set, bll_set = (
            sem("q_set"), sem("keys_set"), sem("blocks_set"), sem("blh_set"), sem("bll_set"))
        gelu_set, kc_set, vc_set, fox_set, logits_set, lexp_set, lln_set, logf_set = (
            sem("gelu_set"), sem("kc_set"), sem("vc_set"), sem("fox_set"), sem("logits_set"), sem("lexp_set"),
            sem("lln_set"), sem("logf_set"))
        cs_exp, cs_prob, pct_turned, pct_set, cs_sub = (
            sem("cs_exp"), sem("cs_prob"), sem("pct_turned"), sem("pct_set"), sem("cs_sub"))
        s_ready, s_taken, negmax_set, exp_done, norm_set, p_scaled = (
            sem("s_ready"), sem("s_taken"), sem("negmax_set"), sem("exp_done"), sem("norm_set"), sem("p_scaled"))
        pt_ready, pt_copied, o_ready, y_hi, y_lo = (
            sem("pt_ready"), sem("pt_copied"), sem("o_ready"), sem("y_hi"), sem("y_lo"))
        sig_set, merged_set = sem("sig_set"), sem("merged_set")
        tile_full = sem("tile_full")
        var_set, std_set, x_set = sem("var_set"), sem("std_set"), sem("x_set")
        act_h, h_set, hT_hi, hT_lo = sem("act_h"), sem("h_set"), sem("hT_hi"), sem("hT_lo")
        out_done = sem("out_done")
        router_in, router_hi, router_lo = sem("router_in"), sem("router_hi"), sem("router_lo")
        logits_full, logits_copied, acc_zero = sem("logits_full"), sem("logits_copied"), sem("acc_zero")
        top_set, texp_set, picks_set, routed, flag_set = (
            sem("top_set"), sem("texp_set"), sem("picks_set"), sem("routed"), sem("flag_set"))

        route = pbuf[:, 2, :, :].rearrange("p a b -> p (a b)")

        def routing(at, n, width):
            return route[:, at:at + n * width].rearrange("p (t e) -> p t e", t=n)

        r_logits, r_top, r_index = routing(0, 2, NE), routing(16, 2, 8), routing(32, 2, 8)
        r_indexf, r_one, r_two, r_mask = routing(48, 2, 8), routing(64, 2, NE), routing(80, 2, NE), routing(96, 2, NE)
        r_gate, r_slot = routing(112, 2, NE), routing(130, 2, NE)
        r_w = route[:, 148:156].rearrange("p (a t) -> p a t", t=2)
        r_count, r_gs = route[:, 156:157], route[:, 157:158]
        logitsT = pbuf[0:NE, 1, 0, :]
        pick = pbuf[:, 0, :, 0:P]
        rout = small[:, 0:KD * NE]
        rout_h = hTh[:, 0, 0:KD * NE]
        rout_l = hTl[:, 0, 0:KD * NE]
        pickT = xTh[:, 0, :]
        xeh = yTh[:, 0:4, :].rearrange("p a b -> p (a b)")
        xel = yTl[:, 0:4, :].rearrange("p a b -> p (a b)")
        yeh = yTh[:, 4:8, :].rearrange("p a b -> p (a b)")
        yel = yTl[:, 4:8, :].rearrange("p a b -> p (a b)")
        acc = merged

        class Pass:

            def __init__(self, p):
                def own(name):
                    return sem(f"{name}_pass{p}")
                self.p = p
                if p == 0:
                    self.u0, self.raw_in, self.hi_ready, self.lo_ready, self.unit_used = (
                        len(units), raw_in, hi_ready, lo_ready, unit_used)
                else:
                    self.u0, self.raw_in = RAW, [own(f"raw_in{i}") for i in range(RAW)]
                    self.hi_ready, self.lo_ready, self.unit_used = own("hi_ready"), own("lo_ready"), own("unit_used")
                self.pick_set, self.pt_full, self.pt_set = own("pick_set"), own("pt_full"), own("pt_set")
                self.xe_full, self.xe_hi, self.xe_lo = own("xe_full"), own("xe_hi"), own("xe_lo")
                self.act_h, self.h_set, self.hT_full = own("act_h"), own("h_set"), own("hT_full")
                self.hT_hi, self.hT_lo = own("hT_hi"), own("hT_lo")
                self.ye_hi, self.ye_lo = own("ye_hi"), own("ye_lo")
                self.sum_full, self.sum_taken = own("sum_full"), own("sum_taken")

        passes = [Pass(0), Pass(1)]
        slots_moved = sem("slots_moved")
        NF, NB = len(moe_first), len(moe_body)
        EU = NF + NB + len(moe_down)
        FT = CHUNK // P

        hTh1 = hTh[:, 0:2, :].rearrange("p a b -> p (a b)")
        hTl1 = hTl[:, 0:2, :].rearrange("p a b -> p (a b)")

        def sum_bank(k):
            return (1, 3, 6, 7)[k]

        block = ctx.enter_context(nc.Block())

        def unit_view(buf, slot, nk, width):
            return buf[:, slot, 0:nk * width].rearrange("p (k n) -> p k n", k=nk)

        N_ATT = 2 * NH + FH
        NLN = 2
        NSPLIT = 6

        def att_step(u):
            if u < 2 * NH:
                i, r = divmod(u, 4)
                return "nsa", r // 2, i + (NH // NKV) * (r % 2)
            i, t = divmod(u - 2 * NH, 2)
            return "fox", t, i

        SIDE = (("values_b", 4), ("queries", 4), ("cumulate", 0), ("keys", 4), ("values_a", 2),
                ("gate0", 4), ("gate1", 4), ("nsa_out", 2), ("gate0_later", 4))
        BEFORE = 4
        CUM_AT = 4
        PRE = 8

        def halves_done(u):
            if u < -1:
                return 0
            return min(BEFORE + u + 1 - (u >= CUM_AT), sum(n for _, n in SIDE))

        def side_ended(u):
            out, end = [], 0
            for name, n in SIDE:
                end += n
                if n and halves_done(u - 1) < end <= halves_done(u):
                    out.append((name, end // 2))
            return out

        def norm_col(u):
            return stats[:, u % 2, 8:10]

        def scores_at(u, nk):
            kind, t, a = att_step(u)
            if kind == "nsa":
                return free(ps[:, 4 + a // 4, 0:1], [[SEQ, 2], [1, nk]])
            return free(ps[:, 4, (u % 2) * SEQ:(u % 2) * SEQ + 1], [[512, 2], [1, nk]])

        @block.sync
        def _(sp):
            sp.dma_start(ident, io["table"][:, 0:P]).then_inc(const_in, 16)
            sp.dma_start(x[:, :, :], io["x"][0].rearrange("(t p) n -> p t n", p=P)).then_inc(x_in, 16)
            for n, (nk, width, src) in enumerate(units):
                wait(sp, lo_ready, n - RAW + 1)
                sp.dma_start(unit_view(raw, n % RAW, nk, width), src).then_inc(raw_in[n % RAW], 16)
                if n == 2:
                    sp.dma_start(table[:, P:K_END], io["table"][:, P:K_END]).then_inc(const_in, 16)

            def experts(S):
                def load(n, e, u, after=0, following=None):
                    nk, width, src = ffn_unit(*(io[f"moe_w_{w}"][0, 0] for w in ("gate", "up", "down")), FE, *u)
                    if isinstance(e, int):
                        start = (e + after) * (FE * D) + src.offset
                        need = e * EU + (n - RAW + 1)
                    else:
                        start = sp.snap(e * (FE * D) + (src.offset + FE * D) if after else
                                        following * (FE * D) + (src.offset - FE * D))
                        need = sp.snap(e * EU + (n - RAW + 1))
                    src = bass.AP(tensor=src.tensor, offset=start, ap=[list(d) for d in src.ap])
                    sp.wait_ge(S.lo_ready, need)
                    sp.dma_start(unit_view(raw, n % RAW, nk, width), src).then_inc(S.raw_in[n % RAW], 16)

                for k, u in enumerate(moe_first):
                    load(S.u0 + k, 0, u)

                def body(e, last, following=None):
                    n = S.u0 + NF
                    for u in moe_body:
                        load(n, e, u, 0, following)
                        n += 1
                    if last:
                        for u in moe_down:
                            load(n, e, u)
                            n += 1
                    else:
                        for u, after in ([(u, 1) for u in moe_first[:2]] + [(u, 0) for u in moe_down]
                                         + [(u, 1) for u in moe_first[2:]]):
                            load(n, e, u, after, following)
                            n += 1

                with sp.Fori(0, NE - 1) as e:
                    body(e, False, sp.snap(e + 1))
                body(NE - 1, True)

            experts(passes[0])
            sp.wait_ge(flag_set, 1)
            again = sp.value_load(flag[0:1, 0:1], min_val=0, max_val=1)
            with sp.If(again == 1):
                sp.wait_ge(lo_ready, len(units) + NE * EU)
                experts(passes[1])
            last = DEPTH * NLN * TT
            for t in range(TT):
                sp.wait_ge(x_set, last - TT + t + 1)
                sp.dma_start(io["out"][0, t * P:(t + 1) * P, :], x[:, t, :]).then_inc(out_done, 16)
            sp.wait_ge(out_done, 16 * TT)

        @block.gpsimd
        def _(pool):
            pool.dma_start(onehot, io["onehot"]).then_inc(onehot_in, 16)
            pool.dma_start(tab[0:BUCKETS, :], io["rel_bias"]).then_inc(onehot_in, 16)

            def small_loads(L):
                if L:
                    pool.wait_ge(y_lo, N_ATT * L)
                pool.dma_start(pe_rows[:, :],
                               io["nsa_cmp_pe"][L].rearrange("v l d -> (v l d)").rearrange("(r n) -> r n", n=P)
                               ).then_inc(small_in, 16)
                pool.dma_start(cmpw2[:, :, :], io["nsa_cmp_w2"][L].rearrange("v p d -> p v d")).then_inc(small_in, 16)
                pool.dma_start(fbias[:, :], io["fox_f_bias"][L].partition_broadcast(P)).then_inc(small_in, 16)

            def norm_loads(L, which):
                wait(pool, x_set, TT * (NLN * L + which))
                if which == 0:
                    pool.wait_ge(merged_set, 2 * (L + 1))
                pool.dma_start(lng[:, 0, :], io[f"ln{which + 1}_g"][L].partition_broadcast(P)).then_inc(lng_in, 16)
                pool.dma_start(lng[:, 1, :], io[f"ln{which + 1}_b"][L].partition_broadcast(P)).then_inc(lng_in, 16)

            def attention(L):
                for u in range(N_ATT):
                    t = att_step(u)[1]
                    nk = P * (t + 1)
                    pool.wait_ge(norm_set, N_ATT * L + u + 1)
                    pu = pbuf[:, u % 3, :, 0:nk]
                    pool.tensor_tensor(pu, pu, free(norm_col(u), [[1, 2], [0, nk]]), ALU.mult).then_inc(p_scaled, 1)

            small_loads(0)
            pool.wait_ge(vrow_set, 1)
            pool.dma_start(scratch.rearrange("p h n -> h p n"), free(vrow, [[0, P], [1, OH_DOWN]])
                           ).then_inc(vrow_out, 16)
            pool.wait_ge(vrow_out, 16)
            pool.dma_start(toep[:, :, :], bass.AP(tensor=scratch.tensor, offset=scratch.offset + P - 1,
                                                  ap=[[NH * OH_DOWN - 1, P], [OH_DOWN, NH], [1, SEQ]])).then_inc(toep_in, 16)
            attention(0)
            small_loads(1)
            norm_loads(0, 0)
            norm_loads(0, 1)
            attention(1)
            pool.wait_ge(y_lo, 2 * N_ATT)
            pool.dma_start(rout.rearrange("p (k e) -> p k e", k=KD),
                           io["moe_router"][0].rearrange("(k p) e -> p k e", p=P)).then_inc(router_in, 16)
            norm_loads(1, 0)
            norm_loads(1, 1)
            pool.memset(acc, 0.0).then_inc(acc_zero, 1)

        @block.tensor
        def _(pe):
            unit, step = Tally(), [Tally(), Tally()]

            def next_unit():
                nk, width, _ = units[unit.n]
                pe.wait_ge(lo_ready, unit.at(1))
                s = unit.n % CONV
                return nk, unit_view(hi, s, nk, width), unit_view(lo, s, nk, width)

            def used(mm):
                mm.then_inc(unit_used, 1)
                unit.n += 1

            def claim(pair):
                wait(pe, pair_free[pair], step[pair].at())

            def full(mm, pair):
                mm.then_inc(pair_full[pair], 1)
                step[pair].n += 1

            def three(out, stat_h, stat_l, mov_h, mov_l, start, stop_):
                pe.matmul(out, stat_h, mov_h, start=start, stop=False, skip_group_check=True)
                pe.matmul(out, stat_h, mov_l, start=False, stop=False, skip_group_check=True)
                return pe.matmul(out, stat_l, mov_h, start=False, stop=stop_, skip_group_check=True)

            def project(outs, pair, k_units, second=None):
                for _ in project_halves(outs, pair, k_units, second):
                    pass

            def project_halves(outs, pair, k_units, second=None):
                claim(pair)
                k = 0
                for un in range(k_units):
                    nk, wh, wl = next_unit()
                    for j in range(nk):
                        last = un == k_units - 1 and j == nk - 1
                        if second and k == KD // 2:
                            pe.wait_ge(split_lo, second)
                        for out, kind, c0, a, first in outs:
                            start = first and k == 0
                            if kind == "T":
                                mm = three(out, wh[:, j, c0:c0 + P], wl[:, j, c0:c0 + P],
                                           xTh[:, k, :], xTl[:, k, :], start, last)
                            else:
                                xs = slice(kind * P, kind * P + P)
                                mm = three(out, xTh[:, k, xs], xTl[:, k, xs],
                                           wh[:, j, c0:c0 + a], wl[:, j, c0:c0 + a], start, last)
                        k += 1
                        if j == nk // 2 - 1:
                            yield
                    used(mm)
                    if un == k_units - 1:
                        step[pair].n += 1
                    yield

            def turn_half(src, b, k0, tiles=range(TT)):
                for t in tiles:
                    for k in range(4):
                        mm = pe.transpose(ps[:, b + k // 2, (k % 2) * SEQ + t * P:(k % 2) * SEQ + (t + 1) * P],
                                          src[:, t, (k0 + k) * P:(k0 + k + 1) * P], ident)
                return mm

            def turn_x(n, b):
                for t in range(TT - 1):
                    wait(pe, x_set, TT * (n - 1) + t + 1)
                    for h in range(2):
                        turn_half(x, b + 2 * h, 4 * h, (t,))
                wait(pe, x_set, TT * n)
                for h in range(2):
                    turn_half(x, b + 2 * h, 4 * h, (TT - 1,)).then_inc(turned, 1)

            def mixer(L):
                pe.wait_ge(split_lo, NSPLIT * L + 1)
                project([(ps[:, v, 0:SEQ], "T", v * P, 0, True) for v in range(2)], 0, 1, NSPLIT * L + 2)
                if L == 0:
                    pe.wait_ge(tab_set, 1)
                    pe.wait_ge(onehot_in, 32)
                    pe.matmul(ps[0:NH, 4, 0:OH_DOWN], tab, onehot[:, 0:OH_DOWN], start=True, stop=True)\
                      .then_inc(vrow_full, 1)
                pe.wait_ge(small_in, 16 * 3 * (L + 1))
                pe.transpose(ps[:, 5, 0:32], pe_rows[:, :], ident[0:32, 0:32]).then_inc(pe_turned, 1)
                if L == 0:
                    for t in range(TT):
                        for c in range(NCP):
                            a = OH_DOWN + OH_UP0 + t * P - (c * CMP_STRIDE + CMP_BLOCK - 1)
                            mm = pe.matmul(ps[:, 6 + t, c * NH:(c + 1) * NH], onehot[:, a:a + P], tab,
                                           start=True, stop=True)
                    mm.then_inc(cbias_full, 1)
                project([(ps[:, 2 + b // 2, (b % 2) * SEQ:(b % 2 + 1) * SEQ], "T", b * P, 0, b % 2 == 0)
                         for b in range(4)], 1, 2)
                claim(0)
                pe.wait_ge(bll_set, L + 1)
                for v in range(2):
                    nk, wh, wl = next_unit()
                    for m in range(nk):
                        mm = three(ps[:, v, 0:2 * NCP], wh[:, m, :], wl[:, m, :], blh[:, v, m, :], bll[:, v, m, :],
                                   m == 0, m == nk - 1)
                    used(mm)
                step[0].n += 1
                project([(ps[:, 2, 0:SEQ], "T", 0, 0, True)]
                        + [(ps[:, 3, t * SEQ:t * SEQ + P], t, P, P, t == 0) for t in range(2)], 1, 1)
                pe.wait_ge(gelu_set, L + 1)
                for g in range(NKV):
                    pe.matmul(ps[g * DH:(g + 1) * DH, 4, 0:NCP], cmpw2[:, 0, :], gkT[:, g * NCP:(g + 1) * NCP],
                              start=True, stop=True)
                pe.matmul(ps[:, 5, 0:DH], gvT, cmpw2[:, 1, :], start=True, stop=True).then_inc(kcv_full, 1)
                window = project_halves(
                    [(ps[:, 0, 0:SEQ], "T", 0, 0, True)]
                    + [(ps[:, 1, t * SEQ:t * SEQ + P + NG], t, P, P + NG, t == 0) for t in range(2)], 0, 2)
                next(window)
                next(window)
                pe.wait_ge(kc_set, L + 1)
                pe.wait_ge(q_set, L + 1)
                for t in range(TT):
                    for hd in range(NH):
                        g, i = divmod(hd, NH // NKV)
                        b = DH * g
                        at = t * 64 + i * NCP
                        mm = pe.matmul(ps[:, 6 + g, at:at + NCP], qk[b:b + DH, i, t * P:(t + 1) * P],
                                       kcT[b:b + DH, :], start=True, stop=True)
                mm.then_inc(cscores_full, 1)
                for _ in window:
                    pass
                attention(L)

                def branch(g, pt):
                    claim(pt)
                    nk, wh, wl = next_unit()
                    for t in range(TT):
                        for j in range(nk):
                            k = 4 * g + j
                            mm = three(ps[:, 2 * pt + t, :], yTh[:, k, t * P:(t + 1) * P],
                                       yTl[:, k, t * P:(t + 1) * P], wh[:, j, :], wl[:, j, :], j == 0, j == nk - 1)
                    used(mm)
                    step[pt].n += 1

                branch(1, 0)
                project([(ps[:, t, :], t, 0, 512, True) for t in range(2)], 0, 2)
                pe.wait_ge(merged_set, 2 * L + 1)
                turn_half(merged, 4, 0).then_inc(turned, 1)
                for g in range(2):
                    branch(g, 1 - g)
                for h in range(2):
                    for half in range(2):
                        pt = 1 - half
                        if h == 0:
                            claim(pt)
                            pe.wait_ge(split_lo, NSPLIT * L + 3)
                        else:
                            pe.wait_ge(split_lo, NSPLIT * L + 4)
                        nk, wh, wl = next_unit()
                        for t in range(TT):
                            xs = slice(t * P, (t + 1) * P)
                            for j in range(nk):
                                k = h * nk + j
                                mm = three(ps[:, 2 * pt + t, :], xTh[:, k, xs], xTl[:, k, xs], wh[:, j, :], wl[:, j, :],
                                           k == 0, k == KD - 1)
                            if t == 0 and h and half:
                                mm.then_inc(tile_full, 1)
                        used(mm)
                        if h == 0 and half == 0:
                            pe.wait_ge(merged_set, 2 * (L + 1))
                            turn_half(merged, 6, 4).then_inc(turned, 1)
                for pt in range(2):
                    step[pt].n += 1

            def attention(L):
                a0 = N_ATT * L

                def scores(u):
                    kind, t, a = att_step(u)
                    nk = P * (t + 1)
                    wait(pe, s_taken, a0 + (u - 1 if kind == "nsa" else u))
                    if kind == "nsa":
                        g, i = divmod(a, NH // NKV)
                        b = DH * g
                        for br in range(2):
                            mm = pe.matmul(ps[:, 4 + a // 4, br * SEQ:br * SEQ + nk],
                                           qk[b:b + DH, i, t * P:(t + 1) * P], ksw[b:b + DH, br, 0:nk],
                                           start=True, stop=True)
                    else:
                        c0 = (u % 2) * SEQ
                        for hh in range(2):
                            b, head = DH * hh, 2 * a + hh
                            out = ps[:, 4 + hh, c0:c0 + nk]
                            pe.matmul(out, qk[b:b + DH, 4 + a, t * P:(t + 1) * P], fkT[b:b + DH, a, 0:nk],
                                      start=True, stop=False, skip_group_check=True)
                            for j in range(t + 1):
                                mm = pe.matmul(ps[:, 4 + hh, c0 + j * P:c0 + nk],
                                               free(logf[:, 3, j, head:head + 1], [[0, P]]), tri[:, 0:nk - j * P],
                                               start=False, stop=(j == t), skip_group_check=True)
                    mm.then_inc(s_ready, 1)

                def turn_probs(u):
                    t = att_step(u)[1]
                    pe.wait_ge(p_scaled, a0 + u + 1)
                    wait(pe, pt_copied, a0 + u - 1)
                    for br in range(2):
                        for j in range(t + 1):
                            c = (br * (t + 1) + j) * P
                            mm = pe.transpose(ps[:, 6 + u % 2, c:c + P], pbuf[:, u % 3, br, j * P:(j + 1) * P], ident)
                    mm.then_inc(pt_ready, 1)

                def values(u):
                    kind, t, a = att_step(u)
                    pe.wait_ge(pt_copied, a0 + u + 1)
                    wait(pe, y_lo, a0 + u - 1)
                    for br in range(2):
                        b = DH * (a // 4 if kind == "nsa" else br)
                        out = ps[b:b + DH, u % 2, 0:P]
                        for j in range(t + 1):
                            c = (br * (t + 1) + j) * P
                            if kind == "nsa":
                                g = a // (NH // NKV)
                                mm = pe.matmul(out, vsw[:, br, j, g * DH:(g + 1) * DH], ptb[:, u % 2, c:c + P],
                                               start=(br == 0 and j == 0), stop=False, skip_group_check=True)
                            else:
                                head = 2 * a + br
                                mm = pe.matmul(out, fv[:, j, head * DH:(head + 1) * DH], ptb[:, u % 2, c:c + P],
                                               start=(j == 0), stop=(j == t), skip_group_check=True)
                    if kind == "nsa":
                        mm = pe.matmul(out, vcb[:, a, :], pct[:, t * P:(t + 1) * P],
                                       start=False, stop=True, skip_group_check=True)
                    mm.then_inc(o_ready, 1)

                def side():
                    transposed = [(ps[:, 2 + b // 2, (b % 2) * SEQ:(b % 2 + 1) * SEQ], "T", b * P, 0, b % 2 == 0)
                                  for b in range(4)]
                    yield from project_halves([(ps[:, 2 + t, 0:256 + FH], t, 0, 256 + FH, True) for t in range(2)],
                                              1, 2)
                    yield from project_halves(transposed, 1, 2)
                    yield from project_halves(transposed, 1, 2)
                    yield from project_halves([(ps[:, 2 + t, 0:256], t, 0, 256, True) for t in range(2)], 1, 1)
                    for g in range(2):
                        yield from project_halves([(ps[:, 2 + t, :], t, 0, 512, True) for t in range(2)], 1, 2)
                    pe.wait_ge(y_lo, a0 + 2 * NH)
                    claim(1)
                    nk, wh, wl = next_unit()
                    for t in range(TT):
                        for j in range(nk):
                            mm = three(ps[:, 2 + t, :], yTh[:, j, t * P:(t + 1) * P], yTl[:, j, t * P:(t + 1) * P],
                                       wh[:, j, :], wl[:, j, :], j == 0, j == nk - 1)
                        if t == 0:
                            yield
                    used(mm)
                    step[1].n += 1
                    yield
                    yield from project_halves([(ps[:, 2 + t, :], t, 0, 512, True) for t in range(2)], 1, 2)

                work = side()

                pe.wait_ge(keys_set, 2 * (L + 1))
                pe.wait_ge(vc_set, L + 1)
                scores(0)
                scores(1)
                for _ in range(BEFORE // 2):
                    next(work)
                pe.wait_ge(cs_prob, L + 1)
                for t in range(TT):
                    mm = pe.transpose(ps[:, 6, t * P:(t + 1) * P],
                                      pbuf[:, 1, :, :].rearrange("p a b -> p (a b)")[:, t * P:(t + 1) * P], ident)
                mm.then_inc(pct_turned, 1)
                for _ in range(BEFORE // 2):
                    next(work)
                pe.wait_ge(pct_set, L + 1)
                claim(0)
                for u in range(N_ATT):
                    if u + 2 < N_ATT:
                        if u + 2 == 2 * NH:
                            pe.wait_ge(fox_set, 4 * L + 3)
                        scores(u + 2)
                    turn_probs(u)
                    if u:
                        if u - 1 == 2 * NH:
                            pe.wait_ge(fox_set, 4 * (L + 1))
                        values(u - 1)
                    if u == CUM_AT:
                        claim(1)
                        pe.wait_ge(logf_set, L + 1)
                        pe.wait_ge(const_in, 32)
                        for t in range(TT):
                            for j in range(t + 1):
                                mm = pe.matmul(ps[:, 2, t * FH:(t + 1) * FH], tri[:, (t - j) * P:(t - j + 1) * P],
                                               logf[:, 2, j, :], start=(t == 0), stop=(j == t), skip_group_check=True)
                        full(mm, 1)
                    for _ in range(halves_done(u) - halves_done(u - 1)):
                        next(work)
                values(N_ATT - 1)
                for _ in work:
                    pass
                pe.wait_ge(y_lo, a0 + N_ATT)

            def dense_ffn():
                ws = chunks(FF)

                def down(c):
                    pe.wait_ge(hT_lo, c + 1)
                    kt = ws[c] // P
                    for i in range(down_units(ws[c])):
                        nk, wh, wl = next_unit()
                        for t in range(TT):
                            for j in range(nk):
                                k = 2 * i + j
                                for half in range(2):
                                    cs_ = slice(half * 512, (half + 1) * 512)
                                    mm = three(ps[:, 4 + 2 * t + half, :], hTh[:, k, t * P:(t + 1) * P],
                                               hTl[:, k, t * P:(t + 1) * P], wh[:, j, cs_], wl[:, j, cs_],
                                               c == 0 and k == 0, c == len(ws) - 1 and k == kt - 1)
                            if t == 0 and c == len(ws) - 1 and k == kt - 1:
                                mm.then_inc(tile_full, 1)
                        used(mm)

                for c, width in enumerate(ws):
                    for g in range(2):
                        project([(ps[:, 2 * g + t, 0:width], t, 0, width, True) for t in range(2)], g, 2,
                                NSPLIT if c == 0 and g == 0 else None)
                    if c:
                        down(c - 1)
                    claim(1)
                    pe.wait_ge(h_set, c + 1)
                    for f in range(width // P):
                        for t in range(TT):
                            a = (f % 2) * SEQ + t * P
                            mm = pe.transpose(ps[:, 2 + f // 2, a:a + P], h[:, t, f * P:(f + 1) * P], ident)
                    full(mm, 1)
                down(len(ws) - 1)

            pe.wait_ge(const_in, 16)
            pe.wait_ge(x_in, 16)
            turn_x(0, 0)
            mixer(0)
            turn_x(1, 4)
            pe.wait_ge(split_lo, NSPLIT - 1)
            dense_ffn()
            turn_x(2, 0)
            mixer(1)
            turn_x(3, 4)
            pe.wait_ge(split_lo, DEPTH * NSPLIT - 1)
            pe.wait_ge(router_lo, 1)
            claim(0)
            for k in range(KD):
                if k == KD // 2:
                    pe.wait_ge(split_lo, DEPTH * NSPLIT)
                es = slice(k * NE, (k + 1) * NE)
                mm = three(ps[0:NE, 0, 0:SEQ], rout_h[:, es], rout_l[:, es], xTh[:, k, :], xTl[:, k, :],
                           k == 0, k == KD - 1)
            mm.then_inc(logits_full, 1)
            pe.wait_ge(logits_copied, 1)
            for t in range(TT):
                mm = pe.transpose(ps[:, 1, t * NE:(t + 1) * NE], logitsT[:, t * P:(t + 1) * P], ident[0:NE, 0:NE])
            full(mm, 0)
            claim(1)
            pe.wait_ge(picks_set, 1)
            before, ones = table[:, K_SU:K_SU + P], table[:, K_ONE:K_ONE + P]
            for at, lhs in ((0, (before,)), (NE, (ones, before)), (2 * NE, (ones, ones))):
                for j, m in enumerate(lhs):
                    mm = pe.matmul(ps[:, 2, at:at + NE], m, r_mask[:, j, :], start=(at == 0), stop=(j == len(lhs) - 1),
                                   skip_group_check=True)
            full(mm, 1)

            claim(0)
            claim(1)

            def experts(S):
                unit = Tally(S.u0)

                def gather():
                    for k in range(KD):
                        for t in range(TT):
                            mm = pe.matmul(ps[:, 6 + k // 4, (k % 4) * P:(k % 4 + 1) * P], x[:, t, k * P:(k + 1) * P],
                                           pick[:, t, :], start=(t == 0), stop=(t == TT - 1), skip_group_check=True)
                    mm.then_inc(S.xe_full, 1)

                def take(nk, width):
                    pe.wait_ge(S.lo_ready, unit.at(1))
                    s = unit.n % CONV
                    return unit_view(hi, s, nk, width), unit_view(lo, s, nk, width)

                def leave_unit(mm):
                    mm.then_inc(S.unit_used, 1)
                    unit.n += 1

                def gate_or_up(bank):
                    for i in range(2):
                        wh, wl = take(KD // 2, CHUNK)
                        for j in range(KD // 2):
                            k = i * KD // 2 + j
                            mm = three(ps[:, bank, :], xeh[:, k * P:(k + 1) * P], xel[:, k * P:(k + 1) * P],
                                       wh[:, j, :], wl[:, j, :], k == 0, k == KD - 1)
                        leave_unit(mm)

                def gates_of(e, c):
                    pe.wait_ge(S.act_h, e * CH + (c + 1))
                    gate_or_up(0)

                def ups_of(e, c):
                    pe.wait_ge(S.hT_lo, e * CH + (c + 1))
                    gate_or_up(2)

                def turn_h(e, c):
                    pe.wait_ge(S.h_set, e * CH + (c + 1))
                    for f in range(FT):
                        mm = pe.transpose(ps[:, 2, f * P:(f + 1) * P], h[:, 0, f * P:(f + 1) * P], ident)
                    mm.then_inc(S.hT_full, 1)

                def down(e, c):
                    pe.wait_ge(S.hT_lo, e * CH + (c + 2))
                    for i in range(FT // 2):
                        wh, wl = take(2, D)
                        for j in range(2):
                            k = 2 * i + j
                            for half in range(2):
                                cols = slice(half * 512, (half + 1) * 512)
                                mm = three(ps[:, 4 + half, :], hTh1[:, k * P:(k + 1) * P], hTl1[:, k * P:(k + 1) * P],
                                           wh[:, j, cols], wl[:, j, cols], c == 0 and k == 0,
                                           c == CH - 1 and k == FT - 1)
                        leave_unit(mm)

                def body(e, last):
                    for c in range(1, CH):
                        gates_of(e, c)
                        ups_of(e, c)
                        if c == 1:
                            pe.wait_ge(S.sum_taken, e * 4 + 1)
                            for t in range(TT):
                                pe.transpose(ps[:, 1, t * P:(t + 1) * P], pick[:, t, :], ident)
                            for t in range(TT):
                                mm = pe.matmul(ps[:, 1, SEQ:SEQ + 1], pick[:, t, :], r_gate[:, t, bass.ds(e, 1)],
                                               start=False, stop=(t == TT - 1), skip_group_check=True)
                            mm.then_inc(S.pt_full, 1)
                            pe.wait_ge(S.ye_lo, e + 1)
                        if c == CH - 1 and not last:
                            pe.wait_ge(S.pick_set, e + 2)
                            pe.wait_ge(S.sum_taken, e * 4 + 4)
                            gather()
                        down(e, c - 1)
                        turn_h(e, c)
                    if not last:
                        pe.wait_ge(S.xe_lo, e + 2)
                        gates_of(e, CH)
                    down(e, CH - 1)
                    if not last:
                        ups_of(e, CH)
                    pe.wait_ge(S.ye_lo, e + 2)
                    pe.wait_ge(S.sum_taken, e * 4 + 4)
                    for k in range(4):
                        t, half = divmod(k, 2)
                        out, cols = ps[:, sum_bank(k), :], slice(half * 512, (half + 1) * 512)
                        pe.matmul(out, pickT[:, t * P:(t + 1) * P], yeh[:, cols], start=True, stop=False)
                        pe.matmul(out, pickT[:, t * P:(t + 1) * P], yel[:, cols], start=False, stop=True)\
                          .then_inc(S.sum_full, 1)
                    if not last:
                        turn_h(e, CH)

                if S.p:
                    pe.wait_ge(passes[0].sum_taken, 4 * (NE + 1))
                    pe.nop().then_inc(S.unit_used, RAW)
                pe.wait_ge(S.pick_set, 1)
                gather()
                pe.wait_ge(S.xe_lo, 1)
                gates_of(0, 0)
                ups_of(0, 0)
                turn_h(0, 0)
                with pe.Fori(0, NE - 1) as e:
                    unit.enter(e, EU)
                    body(e, False)
                    unit.leave(NE - 1)
                body(NE - 1, True)

            experts(passes[0])
            pe.wait_ge(flag_set, 1)
            again = pe.value_load(flag[0:1, 0:1], min_val=0, max_val=1)
            with pe.If(again == 1):
                experts(passes[1])

        AHEAD = 2

        @block.scalar
        def _(act):
            unit, use = Tally(), [Tally(), Tally()]

            def convert_to(n):
                while unit.n < min(n, len(units)):
                    nk, width, _ = units[unit.n]
                    size = nk * width
                    act.wait_ge(raw_in[unit.n % RAW], 16 * (unit.n // RAW + 1))
                    wait(act, unit_used, unit.n - CONV + 1)
                    act.activation(hi[:, unit.n % CONV, 0:size], raw[:, unit.n % RAW, 0:size], ACT.Copy
                                   ).then_inc(hi_ready, 1)
                    unit.n += 1

            def is_full(pair):
                use[pair].n += 1
                act.wait_ge(pair_full[pair], use[pair].at())

            def projected(n):
                act.wait_ge(unit_used, n)

            def pair(i):
                return ps[:, 2 * i:2 * i + 2, :].rearrange("p a b -> p (a b)")

            splits = Tally()

            def split_turned(half, b):
                splits.n += 1
                act.wait_ge(turned, splits.n)
                act.activation(xTh[:, 4 * half:4 * half + 4, :].rearrange("p a b -> p (a b)"),
                               ps[:, b:b + 2, :].rearrange("p a b -> p (a b)"), ACT.Copy).then_inc(split_hi, 1)

            def mixer(L, u0):
                convert_to(u0 + 1 + AHEAD)
                if L == 0:
                    act.wait_ge(vrow_full, 1)
                    act.activation(vrow, ps[0:NH, 4, 0:OH_DOWN], ACT.Copy).then_inc(vrow_set, 1)
                act.wait_ge(pe_turned, L + 1)
                act.activation(pe_cols[:, :, :].rearrange("p v m -> p (v m)"), ps[:, 5, 0:32], ACT.Copy)\
                   .then_inc(pe_cols_set, 1)
                if L == 0:
                    act.wait_ge(cbias_full, 1)
                    for t in range(TT):
                        for hp in range(2):
                            act.activation(cbias[:, hp, t * 64:(t + 1) * 64].rearrange("p (i c) -> p i c", c=NCP),
                                           free(ps[:, 6 + t, 4 * hp:4 * hp + 1], [[1, 4], [NH, NCP]]), ACT.Copy)
                convert_to(u0 + 2 + AHEAD)
                act.wait_ge(blocks_set, L + 1)
                act.activation(yTh[:, 0:4, :].rearrange("p a b -> p (a b)"),
                               blocks[:, :, :, :].rearrange("p v m n -> p (v m n)"), ACT.Copy).then_inc(blh_set, 1)
                convert_to(u0 + 3 + AHEAD)
                projected(u0 + 3)
                act.activation(qk[:, 0:4, :].rearrange("p a b -> p (a b)"), pair(1), ACT.Copy, scale=SCALE)\
                   .then_inc(q_set, 1)
                act.wait_ge(q_set, L + 1)
                act.nop().then_inc(pair_free[1], 1)
                convert_to(u0 + 5 + AHEAD)
                projected(u0 + 5)
                act.activation(gkT, ps[:, 0, 0:2 * NCP], ACT.Gelu_apprx_tanh)
                act.activation(gvT.rearrange("p (g i c) -> p g i c", g=2, i=4),
                               free(ps[:, 1, 0:1], [[NCP, 2], [0, 4], [1, NCP]]), ACT.Gelu_apprx_tanh)\
                   .then_inc(gelu_set, 1)
                act.wait_ge(gelu_set, L + 1)
                act.nop().then_inc(pair_free[0], 1)
                convert_to(u0 + 6 + AHEAD)
                projected(u0 + 6)
                act.activation(ksw[:, 0, :], ps[:, 2, 0:SEQ], ACT.Copy)
                act.activation(vsw[:, 0, :, :], free(ps[:, 3, 0:1], [[SEQ, 2], [1, P]]), ACT.Copy)\
                   .then_inc(pair_free[1], 1)
                act.wait_ge(kcv_full, L + 1)
                act.activation(kcT, ps[:, 4, 0:NCP], ACT.Copy).then_inc(kc_set, 1)
                convert_to(u0 + 7 + AHEAD)
                act.wait_ge(cs_sub, L + 1)
                act.activation(cs[:, 0:256], cs[:, 0:256], ACT.Exp).then_inc(cs_exp, 1)
                convert_to(u0 + 8 + AHEAD)
                projected(u0 + 8)
                act.activation(ksw[:, 1, :], ps[:, 0, 0:SEQ], ACT.Copy)
                act.activation(vsw[:, 1, :, :], free(ps[:, 1, 0:1], [[SEQ, 2], [1, P]]), ACT.Copy)\
                   .then_inc(keys_set, 1)
                act.activation(gates[:, :, :], free(ps[:, 1, P:P + 1], [[SEQ, 2], [1, NG]]), ACT.Sigmoid)\
                   .then_inc(keys_set, 1)
                act.wait_ge(keys_set, 2 * (L + 1))
                act.nop().then_inc(pair_free[0], 1)
                attention(L, u0 + PRE)
                m0 = u0 + PRE + 7
                convert_to(m0 + 8 + AHEAD)
                act.wait_ge(merged_set, 2 * L + 1)
                for g in range(2):
                    convert_to(m0 + (8, 10)[g] + AHEAD)
                    projected(m0 + (7, 10)[g])
                    act.activation(sig[g], ps[:, 2 * (1 - g):2 * (1 - g) + 2, :], ACT.Sigmoid).then_inc(sig_set, 1)
                    act.wait_ge(sig_set, 4 * L + 2 + g + 1)
                    act.nop().then_inc(pair_free[1 - g], 1)
                split_turned(0, 4)
                convert_to(m0 + 12 + AHEAD)
                split_turned(1, 6)
                convert_to(m0 + 16 + 1)
                norm(L * NLN)
                convert_to(m0 + 16 + AHEAD)
                for half in range(2):
                    split_turned(half, 4 + 2 * half)

            def attention(L, s0):
                a0 = N_ATT * L

                def exps(u):
                    t = att_step(u)[1]
                    nk = P * (t + 1)
                    act.wait_ge(negmax_set, a0 + u + 1)
                    wait(act, pt_ready, a0 + u - 2)
                    for br in range(2):
                        ins = act.activation(pbuf[:, u % 3, br, 0:nk], pbuf[:, u % 3, br, 0:nk], ACT.Exp,
                                             bias=stats[:, u % 2, br:br + 1],
                                             accum_out=stats[:, u % 2, 4 + br:5 + br])
                    ins.then_inc(exp_done, 1)

                def copy_probs(u):
                    t = att_step(u)[1]
                    n = 2 * (t + 1) * P
                    act.wait_ge(pt_ready, a0 + u + 1)
                    wait(act, o_ready, a0 + u - 1)
                    act.activation(ptb[:, u % 2, 0:n], ps[:, 6 + u % 2, 0:n], ACT.Copy).then_inc(pt_copied, 1)

                def out_hi(u):
                    kind, t, a = att_step(u)
                    act.wait_ge(o_ready, a0 + u + 1)
                    b, n = (DH * (a // 4), DH) if kind == "nsa" else (0, P)
                    k = a % 4 if kind == "nsa" else 4 + a
                    act.activation(yTh[b:b + n, k, t * P:(t + 1) * P], ps[b:b + n, u % 2, 0:P], ACT.Copy)\
                       .then_inc(y_hi, 1)

                def side(u):
                    for name, n in side_ended(u):
                        projected(s0 + n)
                        if name == "values_b":
                            act.activation(fv[:, :, 256:512], free(ps[:, 2, 0:1], [[512, 2], [1, 256]]), ACT.Copy)\
                               .then_inc(fox_set, 1)
                        elif name == "queries":
                            act.activation(qk[:, 4:8, :].rearrange("p a b -> p (a b)"), pair(1), ACT.Copy,
                                           scale=SCALE).then_inc(fox_set, 1)
                            act.wait_ge(fox_set, 4 * L + 2)
                            act.nop().then_inc(pair_free[1], 1)
                        elif name == "keys":
                            act.activation(kv[:, 0:4, :].rearrange("p a b -> p (a b)"), pair(1), ACT.Copy)\
                               .then_inc(fox_set, 1)
                            act.wait_ge(fox_set, 4 * L + 3)
                            act.nop().then_inc(pair_free[1], 1)
                        elif name == "values_a":
                            act.activation(fv[:, :, 0:256], free(ps[:, 2, 0:1], [[512, 2], [1, 256]]), ACT.Copy)\
                               .then_inc(fox_set, 1)
                            act.wait_ge(fox_set, 4 * L + 4)
                            act.nop().then_inc(pair_free[1], 1)
                        elif name in ("gate0", "gate1"):
                            g = int(name[-1])
                            act.activation(sig[g], ps[:, 2:4, :], ACT.Sigmoid).then_inc(sig_set, 1)
                            act.wait_ge(sig_set, 4 * L + g + 1)
                            act.nop().then_inc(pair_free[1], 1)

                exps(0)
                act.wait_ge(pct_turned, L + 1)
                act.activation(pct, ps[:, 6, 0:256], ACT.Copy).then_inc(pct_set, 1)
                convert_to(s0 + BEFORE // 2 + 1)
                for u in range(N_ATT):
                    if u + 1 < N_ATT:
                        exps(u + 1)
                    side(u - 1)
                    if u == 0:
                        act.wait_ge(logits_set, L + 1)
                        act.activation(logf[:, 1, :, :], logf[:, 1, :, :], ACT.Exp, scale=-1.0).then_inc(lexp_set, 1)
                        act.wait_ge(lexp_set, L + 1)
                        act.activation(logf[:, 1, :, :], logf[:, 1, :, :], ACT.Ln, bias=1.0).then_inc(lln_set, 1)
                    copy_probs(u)
                    if u:
                        out_hi(u - 1)
                    convert_to(s0 + max(halves_done(u - 2), BEFORE) // 2 + CONV)
                use[1].n += 1
                out_hi(N_ATT - 1)

            def norm(n):
                for t in range(TT):
                    act.wait_ge(var_set, TT * n + t + 1)
                    act.activation(stats[:, t, 14:15], stats[:, t, 13:14], ACT.Sqrt, bias=eps[:, 0:1])\
                       .then_inc(std_set, 1)

            def dense_ffn(u0, n_norm):
                ws = chunks(FF)
                at = u0
                for c, width in enumerate(ws):
                    convert_to(at + 2 + AHEAD)
                    projected(at + 2)
                    at += 4
                    for t in range(TT):
                        ins = act.activation(h[:, t, 0:width], ps[:, t, 0:width], ACT.Silu)
                    ins.then_inc(act_h, 1)
                    if c:
                        at += down_units(ws[c - 1])
                    convert_to(at + AHEAD)
                    is_full(1)
                    act.activation(hTh[:, 0:width // P, :].rearrange("p a b -> p (a b)"), pair(1)[:, 0:2 * width], ACT.Copy)\
                       .then_inc(hT_hi, 1)
                at += down_units(ws[-1])
                convert_to(at + 1)
                norm(n_norm)
                convert_to(at + AHEAD)
                return at

            act.wait_ge(eps_set, 1)
            for half in range(2):
                split_turned(half, 2 * half)
            mixer(0, 0)
            at = dense_ffn(mixer_units, 1)
            for half in range(2):
                split_turned(half, 2 * half)
            mixer(1, at)
            act.wait_ge(router_in, 16)
            act.activation(rout_h, rout, ACT.Copy).then_inc(router_hi, 1)
            for n in range(len(units), len(units) + CONV):
                if n == len(units) + CONV - 1:
                    act.wait_ge(logits_full, 1)
                    act.activation(logitsT, ps[0:NE, 0, 0:SEQ], ACT.Copy).then_inc(logits_copied, 1)
                act.wait_ge(raw_in[n % RAW], 16 * (n // RAW + 1))
                act.activation(hi[:, n % CONV, :], raw[:, n % RAW, :], ACT.Copy).then_inc(hi_ready, 1)
            act.wait_ge(top_set, 1)
            act.activation(r_w[:, 1, :], r_w[:, 0, :], ACT.Exp).then_inc(texp_set, 1)

            def experts(S):
                unit = Tally(S.u0 + (0 if S.p else CONV))

                def convert_to(n):
                    while unit.n < base + shift + n:
                        landed = 16 * (unit.n // RAW + 1 - S.p)
                        if unit.reg is not None:
                            landed = unit.reg * (16 * EU // RAW) + landed
                        act.wait_ge(S.raw_in[unit.n % RAW], landed)
                        act.wait_ge(S.unit_used, unit.at(1 - CONV))
                        act.activation(hi[:, unit.n % CONV, :], raw[:, unit.n % RAW, :], ACT.Copy
                                       ).then_inc(S.hi_ready, 1)
                        unit.n += 1

                def tokens_hi(n):
                    act.wait_ge(S.xe_full, n)
                    act.activation(xeh, ps[:, 6:8, :].rearrange("p a b -> p (a b)"), ACT.Copy).then_inc(S.xe_hi, 1)

                def silu(e, c, at):
                    act.wait_ge(S.unit_used, e * EU + (base + at + 2))
                    act.activation(h[:, 0, :], ps[:, 0, :], ACT.Silu).then_inc(S.act_h, 1)

                def turned_hi(e, c):
                    act.wait_ge(S.hT_full, e * CH + (c + 1))
                    act.activation(hTh1, ps[:, 2, :], ACT.Copy).then_inc(S.hT_hi, 1)

                def outputs_hi(e, n):
                    act.wait_ge(S.unit_used, e * EU + (base + n))
                    act.wait_ge(S.pt_set, e + 1)
                    act.activation(yeh, ps[:, 4:6, :].rearrange("p a b -> p (a b)"), ACT.Copy, scale=r_gs)\
                       .then_inc(S.ye_hi, 1)

                def body(e, last):
                    at = 0
                    for c in range(1, CH):
                        convert_to(at + 2 + AHEAD)
                        silu(e, c, at)
                        if c == 1:
                            convert_to(at + 4 + AHEAD)
                            act.wait_ge(S.pt_full, e + 1)
                            act.activation(pickT, ps[:, 1, 0:SEQ], ACT.Copy)
                            act.activation(r_gs, ps[:, 1, SEQ:SEQ + 1], ACT.Copy).then_inc(S.pt_set, 1)
                        if c == CH - 1 and not last:
                            convert_to(at + 4 + AHEAD)
                            tokens_hi(e + 2)
                        at += 6
                        convert_to(at + AHEAD)
                        turned_hi(e, c)
                    if not last:
                        convert_to(at + 2 + AHEAD)
                        silu(e, CH, at)
                        convert_to(at + 4 + AHEAD)
                        outputs_hi(e, at + 4)
                        convert_to(at + 6 + AHEAD)
                        turned_hi(e, CH)
                    else:
                        outputs_hi(e, at + 2)

                act.nop().then_inc(S.act_h, 1)
                if S.p:
                    act.nop().then_inc(S.hi_ready, RAW)
                tokens_hi(1)
                base, shift = S.u0, 0
                convert_to(2 + AHEAD)
                silu(0, 0, 0)
                convert_to(NF + AHEAD)
                turned_hi(0, 0)
                base = S.u0 + NF
                with act.Fori(0, NE - 1) as e:
                    unit.enter(e, EU)
                    body(e, False)
                    unit.leave(NE - 1)
                shift = EU * (NE - 1)
                body(NE - 1, True)

            experts(passes[0])
            act.wait_ge(flag_set, 1)
            again = act.value_load(flag[0:1, 0:1], min_val=0, max_val=1)
            with act.If(again == 1):
                experts(passes[1])
            norm(3)

        @block.vector
        def _(dve):
            unit, use, chain, splits = Tally(), [Tally(), Tally()], Tally(), Tally()

            def link(ins):
                chain.n += 1
                ins.then_inc(dve_step, 1)
                dve.wait_ge(dve_step, chain.at())

            def convert_to(n):
                while unit.n < min(n, len(units)):
                    nk, width, _ = units[unit.n]
                    size = nk * width
                    s = unit.n % CONV
                    dve.wait_ge(hi_ready, unit.at(1))
                    dve.tensor_tensor(lo[:, s, 0:size], raw[:, unit.n % RAW, 0:size], hi[:, s, 0:size].bitcast(F32),
                                      ALU.subtract).then_inc(lo_ready, 1)
                    unit.n += 1

            begun = Tally()

            def convert_halves(n):
                while 2 * unit.n + begun.n < min(n, 2 * len(units)):
                    nk, width, _ = units[unit.n]
                    half = nk * width // 2
                    s, part = unit.n % CONV, slice(begun.n * half, (begun.n + 1) * half)
                    dve.wait_ge(hi_ready, unit.at(1))
                    ins = dve.tensor_tensor(lo[:, s, part], raw[:, unit.n % RAW, part], hi[:, s, part].bitcast(F32),
                                            ALU.subtract)
                    if begun.n:
                        ins.then_inc(lo_ready, 1)
                        unit.n += 1
                    begun.n = 1 - begun.n

            def is_full(pair):
                use[pair].n += 1
                dve.wait_ge(pair_full[pair], use[pair].at())

            def projected(n):
                dve.wait_ge(unit_used, n)

            def pair(i):
                return ps[:, 2 * i:2 * i + 2, :].rearrange("p a b -> p (a b)")

            def split_turned(half, b):
                splits.n += 1
                dve.wait_ge(split_hi, splits.n)
                sl = (slice(None), slice(4 * half, 4 * half + 4), slice(None))
                dve.tensor_tensor(xTl[sl].rearrange("p a b -> p (a b)"), ps[:, b:b + 2, :].rearrange("p a b -> p (a b)"),
                                  xTh[sl].rearrange("p a b -> p (a b)").bitcast(F32), ALU.subtract)\
                   .then_inc(split_lo, 1)

            def mixer(L, u0):
                convert_to(u0 + 1 + AHEAD)
                projected(u0 + 1)
                dve.wait_ge(pe_cols_set, L + 1)
                dve.memset(free(blocks[:, 0, 0, NC:NC + 1], [[NCP, 4 * CM]]), 0.0)
                for v in range(2):
                    for g in range(2):
                        for j in range(2):
                            src = ps[g * DH:(g + 1) * DH, v, j:j + 1]
                            ins = dve.tensor_tensor(
                                free(blocks[j * DH:(j + 1) * DH, v, 0, g * NCP:g * NCP + 1], [[2 * NCP, CM], [1, NC]]),
                                free(src, [[2, CM], [CMP_STRIDE, NC]]),
                                free(pe_cols[j * DH:(j + 1) * DH, v, 0:1], [[1, CM], [0, NC]]), ALU.add)
                link(ins)
                dve.nop().then_inc(blocks_set, 1)
                dve.nop().then_inc(pair_free[0], 1)
                convert_to(u0 + 2 + AHEAD)
                dve.wait_ge(blh_set, L + 1)
                dve.tensor_tensor(yTl[:, 0:4, :].rearrange("p a b -> p (a b)"),
                                  blocks[:, :, :, :].rearrange("p v m n -> p (v m n)"),
                                  yTh[:, 0:4, :].rearrange("p a b -> p (a b)").bitcast(F32), ALU.subtract)\
                   .then_inc(bll_set, 1)
                convert_to(u0 + 6 + AHEAD)
                dve.wait_ge(const_in, 32)
                dve.wait_ge(kcv_full, L + 1)
                link(dve.tensor_tensor(vcb[:, :, :], free(ps[:, 5, 0:1], [[0, NH], [1, DH]]),
                                       free(table[:, K_BLK:K_BLK + 1], [[1, NH], [0, DH]]), ALU.mult))
                dve.nop().then_inc(vc_set, 1)
                convert_to(u0 + 7 + AHEAD)
                dve.wait_ge(cscores_full, L + 1)
                c3 = cs[:, 0:256].rearrange("p (a c) -> p a c", c=NCP)
                if L:
                    dve.wait_ge(pt_ready, N_ATT * L)
                link(dve.tensor_tensor(cs[:, 0:256].rearrange("p (a b) -> p a b", a=2), ps[:, 6:8, 0:P],
                                       cbias[:, :, :], ALU.add))
                link(dve.tensor_reduce(csum[:, 0, :], c3, AX, ALU.max))
                link(dve.tensor_tensor(c3, c3, free(csum[:, 0, 0:1], [[1, 16], [0, NCP]]), ALU.subtract))
                dve.nop().then_inc(cs_sub, 1)
                dve.wait_ge(cs_exp, L + 1)
                link(dve.tensor_tensor(cs[:, 0:256], cs[:, 0:256], table[:, K_VIS:K_VIS + 256], ALU.mult))
                link(dve.tensor_reduce(csum[:, 1, :], c3, AX, ALU.add))
                link(dve.tensor_scalar(csum[:, 1, :], csum[:, 1, :], 1e-30, None, ALU.max))
                link(dve.reciprocal(csum[:, 2, :], csum[:, 1, :]))
                convert_to(u0 + 8 + AHEAD)
                dve.wait_ge(keys_set, 2 * (L + 1))
                link(dve.tensor_tensor(csum[:, 3, :].rearrange("p (a t i) -> p a t i", a=2, t=2),
                                       csum[:, 2, :].rearrange("p (a t i) -> p a t i", a=2, t=2),
                                       free(gates[:, 0, 0:1], [[12, 2], [NG, 2], [3, 4]]), ALU.mult))
                cp = pbuf[:, 1, :, :].rearrange("p a b -> p (a b)")
                for hp in range(2):
                    ins = dve.tensor_tensor(
                        free(cp[:, hp * 64:hp * 64 + 1], [[P, 2], [NCP, 4], [1, NCP]]),
                        c3[:, 8 * hp:8 * hp + 8, :].rearrange("p (t i) c -> p t i c", t=2),
                        free(csum[:, 3, 8 * hp:8 * hp + 1], [[4, 2], [1, 4], [0, NCP]]), ALU.mult)
                link(ins)
                dve.nop().then_inc(cs_prob, 1)
                attention(L, u0 + PRE)
                m0 = u0 + PRE + 7
                for half in range(2):
                    if half:
                        convert_to(m0 + 10 + AHEAD)
                        split_turned(0, 4)
                        convert_to(m0 + 11 + AHEAD)
                        projected(m0 + 11)
                        dve.wait_ge(sig_set, 4 * L + 3)
                        link(dve.tensor_tensor(sig[0], ps[:, 2:4, :], sig[0], ALU.mult))
                        dve.nop().then_inc(pair_free[1], 1)
                    convert_to(m0 + (8, 12)[half] + AHEAD)
                    mh = merged[:, :, half * 512:(half + 1) * 512]
                    projected(m0 + (8, 12)[half])
                    dve.wait_ge(sig_set, 4 * L + 2 * half + 2)
                    link(dve.tensor_tensor(sig[1], ps[:, 0:2, :], sig[1], ALU.mult))
                    dve.nop().then_inc(pair_free[0], 1)
                    link(dve.tensor_tensor(mh, sig[0], sig[1], ALU.add))
                    dve.nop().then_inc(merged_set, 1)
                split_turned(1, 6)
                convert_to(m0 + 16 + 1)

                def ready(half, t):
                    if half == 0:
                        projected(m0 + 15)
                    elif t == 0:
                        dve.wait_ge(tile_full, NLN * L + 1)
                    else:
                        projected(m0 + 16)

                norm(L * NLN, lambda t, half: ps[:, 2 * (1 - half) + t, :], ready, True)
                for pt in range(2):
                    dve.nop().then_inc(pair_free[pt], 1)
                for half in range(2):
                    split_turned(half, 4 + 2 * half)

            def attention(L, s0):
                a0 = N_ATT * L

                def scores(u):
                    kind, t, a = att_step(u)
                    nk = P * (t + 1)
                    dve.wait_ge(s_ready, a0 + u + 1)
                    wait(dve, pt_ready, a0 + u - 2)
                    pu = pbuf[:, u % 3, :, 0:nk]
                    k0 = SEQ - nk
                    if kind == "nsa":
                        ins = dve.tensor_tensor(pu, scores_at(u, nk), free(toep[:, a, k0:k0 + 1], [[0, 2], [1, nk]]),
                                                ALU.add)
                    else:
                        for hh in range(2):
                            c0 = (u % 2) * SEQ
                            ins = dve.scalar_tensor_tensor(pu[:, hh, :], ps[:, 4 + hh, c0:c0 + nk],
                                                           fcum[:, t, 2 * a + hh:2 * a + hh + 1],
                                                           table[:, K_MASK + k0:K_MASK + SEQ], ALU.add, ALU.add)
                    link(ins)
                    dve.nop().then_inc(s_taken, 1)
                    dve.tensor_reduce(stats[:, u % 2, 0:2], pu, AX, ALU.max, negate=True).then_inc(negmax_set, 1)

                def factors(u):
                    kind, t, a = att_step(u)
                    dve.wait_ge(exp_done, a0 + u + 1)
                    wait(dve, p_scaled, a0 + u - 1)
                    st = stats[:, u % 2, :]
                    link(dve.tensor_scalar(st[:, 4:6], st[:, 4:6], 1e-30, None, ALU.max))
                    if kind == "nsa":
                        link(dve.reciprocal(st[:, 6:8], st[:, 4:6]))
                        ins = dve.tensor_tensor(st[:, 8:10], st[:, 6:8], gates[:, t, 3 * a + 1:3 * a + 3], ALU.mult)
                    else:
                        ins = dve.reciprocal(st[:, 8:10], st[:, 4:6])
                    ins.then_inc(norm_set, 1)

                def out_lo(u):
                    kind, t, a = att_step(u)
                    dve.wait_ge(y_hi, a0 + u + 1)
                    b, n = (DH * (a // 4), DH) if kind == "nsa" else (0, P)
                    k = a % 4 if kind == "nsa" else 4 + a
                    dve.tensor_tensor(yTl[b:b + n, k, t * P:(t + 1) * P], ps[b:b + n, u % 2, 0:P],
                                      yTh[b:b + n, k, t * P:(t + 1) * P].bitcast(F32), ALU.subtract).then_inc(y_lo, 1)

                if L == 0:
                    dve.wait_ge(toep_in, 16)
                scores(0)
                dve.wait_ge(pct_turned, L + 1)
                scores(1)
                convert_to(s0 + BEFORE // 2 + 1)
                for u in range(N_ATT):
                    factors(u)
                    if u + 2 < N_ATT:
                        scores(u + 2)
                    if u == 0:
                        projected(s0 + BEFORE // 2)
                        dve.wait_ge(fox_set, 4 * L + 1)
                        link(dve.tensor_tensor(logf[:, 0, :, :], free(ps[:, 2, 256:257], [[512, 2], [1, FH]]),
                                               free(fbias[:, 0:1], [[0, 2], [1, FH]]), ALU.add))
                        dve.nop().then_inc(pair_free[1], 1)
                        link(dve.tensor_scalar(logf[:, 2, :, :], logf[:, 0, :, :], 0.0, None, ALU.min))
                        link(dve.scalar_tensor_tensor(logf[:, 1, :, :], logf[:, 2, :, :], -2.0, logf[:, 0, :, :],
                                                      ALU.mult, ALU.add))
                        dve.nop().then_inc(logits_set, 1)
                    if u == 1:
                        dve.wait_ge(lln_set, L + 1)
                        link(dve.tensor_tensor(logf[:, 2, :, :], logf[:, 2, :, :], logf[:, 1, :, :], ALU.subtract))
                        link(dve.tensor_scalar(logf[:, 3, :, :], logf[:, 2, :, :], -1.0, None, ALU.mult))
                        dve.nop().then_inc(logf_set, 1)
                    if u == CUM_AT + 1:
                        is_full(1)
                        link(dve.tensor_copy(fcum[:, :, :].rearrange("p t h -> p (t h)"), ps[:, 2, 0:TT * FH]))
                        dve.nop().then_inc(pair_free[1], 1)
                    if ("nsa_out", 12) in side_ended(u - 1):
                        projected(s0 + 12)
                        dve.wait_ge(sig_set, 4 * L + 1)
                        link(dve.tensor_tensor(sig[0], ps[:, 2:4, :], sig[0], ALU.mult))
                        dve.nop().then_inc(pair_free[1], 1)
                    if u > 1:
                        out_lo(u - 2)
                    at = 2 * s0 + min(7 + u, 2 * CONV - 1 + max(halves_done(u - 3), BEFORE))
                    convert_halves(at)
                convert_halves(at + at % 2)
                out_lo(N_ATT - 2)
                out_lo(N_ATT - 1)

            def norm(n, src, ready=None, early=False):
                def add(t, half):
                    xs = x[:, t, half * 512:(half + 1) * 512]
                    return dve.scalar_tensor_tensor(xs, xs, ALPHA, src(t, half), ALU.mult, ALU.add)

                def spread(t, half):
                    at = 448 + 16 * t + 6 * half
                    return dve.bn_stats(small[:, at:at + 6], x[:, t, half * 512:(half + 1) * 512])

                if early:
                    ready(0, 0)
                    for t in range(TT):
                        ins = add(t, 0)
                    link(ins)
                    for t in range(TT):
                        spread(t, 0)
                dve.wait_ge(lng_in, 32 * (n + 1))
                for t in range(TT):
                    st, xs = stats[:, t, :], x[:, t, :]
                    halves = (1,) if early else (0, 1)
                    if ready:
                        ready(1, t)
                    for half in halves:
                        ins = add(t, half)
                    link(ins)
                    for half in halves:
                        ins = spread(t, half)
                    link(ins)
                    dve.bn_aggr(st[:, 12:14], small[:, 448 + 16 * t:448 + 16 * t + 12]).then_inc(var_set, 1)
                    dve.wait_ge(var_set, TT * n + t + 1)
                    link(dve.scalar_tensor_tensor(xs, xs, st[:, 12:13], lng[:, 0, :], ALU.subtract, ALU.mult))
                    dve.wait_ge(std_set, TT * n + t + 1)
                    link(dve.reciprocal(st[:, 15:16], st[:, 14:15]))
                    dve.scalar_tensor_tensor(xs, xs, st[:, 15:16], lng[:, 1, :], ALU.mult, ALU.add).then_inc(x_set, 1)

            def dense_ffn(u0, n_norm):
                ws = chunks(FF)
                at = u0
                for c, width in enumerate(ws):
                    at += 4
                    convert_to(at + AHEAD)
                    projected(at)
                    dve.wait_ge(act_h, c + 1)
                    dve.nop().then_inc(pair_free[0], 1)
                    hc = h[:, :, 0:width]
                    link(dve.tensor_tensor(hc, hc, ps[:, 2:4, 0:width], ALU.mult))
                    dve.nop().then_inc(h_set, 1)
                    dve.nop().then_inc(pair_free[1], 1)
                    if c:
                        at += down_units(ws[c - 1])
                    convert_to(at + AHEAD)
                    use[1].n += 1
                    dve.wait_ge(hT_hi, c + 1)
                    n = 2 * width
                    link(dve.tensor_tensor(hTl[:, 0:width // P, :].rearrange("p a b -> p (a b)"), pair(1)[:, 0:n],
                                           hTh[:, 0:width // P, :].rearrange("p a b -> p (a b)").bitcast(F32),
                                           ALU.subtract))
                    dve.nop().then_inc(hT_lo, 1)
                    dve.nop().then_inc(pair_free[1], 1)
                at += down_units(ws[-1])
                convert_to(at + 1)

                def ready(half, t):
                    if t == 0:
                        dve.wait_ge(tile_full, n_norm + 1)
                    else:
                        projected(at)

                norm(n_norm, lambda t, half: ps[:, 4 + 2 * t + half, :], ready)
                return at

            dve.memset(eps[:, :], LN_EPS).then_inc(eps_set, 1)
            dve.memset(tab[BUCKETS:BUCKETS + 1, :], NEG).then_inc(tab_set, 1)
            for half in range(2):
                split_turned(half, 2 * half)
            mixer(0, 0)
            at = dense_ffn(mixer_units, 1)
            for half in range(2):
                split_turned(half, 2 * half)
            mixer(1, at)
            dve.wait_ge(router_hi, 1)
            dve.tensor_tensor(rout_l, rout, rout_h.bitcast(F32), ALU.subtract).then_inc(router_lo, 1)
            n = len(units)
            dve.wait_ge(hi_ready, n + 1)
            dve.tensor_tensor(lo[:, n % CONV, :], raw[:, n % RAW, :], hi[:, n % CONV, :].bitcast(F32),
                              ALU.subtract).then_inc(lo_ready, 1)
            is_full(0)
            link(dve.tensor_copy(r_logits, ps[:, 1, 0:TT * NE].rearrange("p (t e) -> p t e", t=TT)))
            dve.nop().then_inc(pair_free[0], 1)
            for t in range(TT):
                ins = dve.max(r_top[:, t, :], r_logits[:, t, :])
            link(ins)
            for t in range(TT):
                ins = dve.max_index(r_index[:, t, :].bitcast(U32), r_top[:, t, :], r_logits[:, t, :])
            link(ins)
            link(dve.tensor_copy(r_indexf, r_index.bitcast(U32)))
            iota8 = table[:, K_IOTA:K_IOTA + NE]
            for k, one in enumerate((r_one, r_two)):
                for t in range(TT):
                    ins = dve.tensor_scalar(one[:, t, :], iota8, r_indexf[:, t, k:k + 1], None, ALU.is_equal)
            link(ins)
            link(dve.tensor_tensor(r_mask, r_one, r_two, ALU.add))
            dve.nop().then_inc(picks_set, 1)
            link(dve.tensor_tensor(r_w[:, 0, :], free(r_top[:, 0, 1:2], [[NE, 2]]), free(r_top[:, 0, 0:1], [[NE, 2]]),
                                   ALU.subtract))
            dve.nop().then_inc(top_set, 1)
            dve.wait_ge(texp_set, 1)
            link(dve.tensor_scalar(r_w[:, 0, :], r_w[:, 1, :], 1.0, None, ALU.add))
            link(dve.reciprocal(r_w[:, 2, :], r_w[:, 0, :]))
            link(dve.tensor_tensor(r_w[:, 3, :], r_w[:, 1, :], r_w[:, 2, :], ALU.mult))
            for t in range(TT):
                ins = dve.tensor_scalar(r_gate[:, t, 0:NE], r_one[:, t, :], r_w[:, 2, t:t + 1], None, ALU.mult)
            link(ins)
            for t in range(TT):
                ins = dve.scalar_tensor_tensor(r_gate[:, t, 0:NE], r_two[:, t, :], r_w[:, 3, t:t + 1],
                                               r_gate[:, t, 0:NE], ALU.mult, ALU.add)
            link(ins)
            is_full(1)
            slots = r_slot[:, :, 0:NE]
            places = ps[:, 2, 0:2 * NE].rearrange("p (t e) -> p t e", t=TT)
            link(dve.scalar_tensor_tensor(slots, r_mask, -FAR, places, ALU.mult, ALU.add))
            link(dve.tensor_scalar(slots, slots, FAR, None, ALU.add))
            link(dve.tensor_reduce(r_count, ps[:, 2, 2 * NE:3 * NE], AX, ALU.max))
            dve.nop().then_inc(pair_free[1], 1)
            dve.tensor_scalar(flag[:, :], r_count, CAP + 0.5, None, ALU.is_gt).then_inc(flag_set, 1)

            def experts(S):
                unit = Tally(S.u0 + (0 if S.p else 1))

                def convert_to(n):
                    while unit.n < base + shift + n:
                        s = unit.n % CONV
                        dve.wait_ge(S.hi_ready, unit.at(1))
                        dve.tensor_tensor(lo[:, s, :], raw[:, unit.n % RAW, :], hi[:, s, :].bitcast(F32),
                                          ALU.subtract).then_inc(S.lo_ready, 1)
                        unit.n += 1

                def select(e):
                    dve.tensor_tensor(pick, free(table[:, K_IOTA:K_IOTA + 1], [[0, TT], [1, P]]),
                                      r_slot[:, :, bass.ds(e, 1)].broadcast_to([P, TT, P]), ALU.is_equal)\
                       .then_inc(S.pick_set, 1)

                def tokens_lo(n):
                    dve.wait_ge(S.xe_hi, n)
                    dve.tensor_tensor(xel, ps[:, 6:8, :].rearrange("p a b -> p (a b)"), xeh.bitcast(F32), ALU.subtract)\
                       .then_inc(S.xe_lo, 1)

                def times_up(e, c, at):
                    dve.wait_ge(S.unit_used, e * EU + (base + at))
                    dve.wait_ge(S.act_h, e * CH + (c + 2))
                    dve.tensor_tensor(h[:, 0, :], h[:, 0, :], ps[:, 2, :], ALU.mult).then_inc(S.h_set, 1)

                def turned_lo(e, c):
                    dve.wait_ge(S.hT_hi, e * CH + (c + 1))
                    dve.tensor_tensor(hTl1, ps[:, 2, :], hTh1.bitcast(F32), ALU.subtract).then_inc(S.hT_lo, 1)

                def outputs_lo(e):
                    dve.wait_ge(S.ye_hi, e + 1)
                    dve.scalar_tensor_tensor(yel, ps[:, 4:6, :].rearrange("p a b -> p (a b)"), r_gs,
                                             yeh.bitcast(F32), ALU.mult, ALU.subtract).then_inc(S.ye_lo, 1)

                def sums(e):
                    dve.wait_ge(S.sum_taken, e * 4 + 4)
                    for k in range(4):
                        t, half = divmod(k, 2)
                        to = acc[:, t, half * 512:(half + 1) * 512]
                        dve.wait_ge(S.sum_full, e * 4 + (k + 1))
                        dve.tensor_tensor(to, to, ps[:, sum_bank(k), :], ALU.add).then_inc(S.sum_taken, 1)

                def body(e, last):
                    at = 0
                    for c in range(1, CH):
                        at += 4
                        convert_to(at + AHEAD)
                        times_up(e, c, at)
                        if c == 1 and not last:
                            dve.wait_ge(S.pt_full, e + 1)
                            select(e + 1)
                        if c == CH - 1 and not last:
                            tokens_lo(e + 2)
                        at += 2
                        convert_to(at + AHEAD)
                        turned_lo(e, c)
                    if not last:
                        convert_to(at + 4 + AHEAD)
                        outputs_lo(e)
                        convert_to(at + 6 + AHEAD)
                        times_up(e, CH, at + 6)
                        sums(e)
                        turned_lo(e, CH)
                    else:
                        outputs_lo(e)
                        sums(e)
                        dve.wait_ge(S.sum_taken, 4 * (NE + 1))

                dve.nop().then_inc(S.hT_lo, 1)
                dve.nop().then_inc(S.ye_lo, 1)
                dve.nop().then_inc(S.sum_taken, 4)
                if S.p:
                    dve.tensor_scalar(slots, slots, float(CAP), None, ALU.subtract).then_inc(slots_moved, 1)
                    dve.wait_ge(slots_moved, 1)
                    dve.nop().then_inc(S.lo_ready, RAW)
                select(0)
                base, shift = S.u0, 0
                convert_to(CONV)
                tokens_lo(1)
                dve.wait_ge(acc_zero, 1)
                convert_to(NF + AHEAD)
                times_up(0, 0, NF)
                turned_lo(0, 0)
                base = S.u0 + NF
                with dve.Fori(0, NE - 1) as e:
                    unit.enter(e, EU)
                    body(e, False)
                    unit.leave(NE - 1)
                shift = EU * (NE - 1)
                body(NE - 1, True)

            experts(passes[0])
            dve.wait_ge(flag_set, 1)
            again = dve.value_load(flag[0:1, 0:1], min_val=0, max_val=1)
            with dve.If(again == 1):
                experts(passes[1])
            norm(3, lambda t, half: acc[:, t, half * 512:(half + 1) * 512])


_INS = ["x", "w_in", "nsa_cmp_pe", "nsa_cmp_w1", "nsa_cmp_w2", "fox_f_bias", "w_nsa_branch", "w_fox_branch",
        "w_out", "rel_bias", "ln1_g", "ln1_b", "ln2_g", "ln2_b", "dense_w_gate", "dense_w_up", "dense_w_down",
        "moe_router", "moe_w_gate", "moe_w_up", "moe_w_down"]


def kernel(**inputs):
    import numpy as _np
    import concourse.bacc as _bacc
    from concourse import mybir as _mybir
    from concourse.bass_utils import run_bass_kernel_spmd as _run

    nc = _bacc.Bacc("TRN2", target_bir_lowering=False, num_devices=1)
    table, onehot = constants()
    arrays, io = {}, {}
    for name in _INS + ["table", "onehot"]:
        a = {"table": table, "onehot": onehot}[name] if name in ("table", "onehot") else _np.ascontiguousarray(inputs[name])
        if name == "w_in":
            q = a[:, :, :512].reshape(DEPTH, D, 2, 4, DH).transpose(0, 1, 3, 2, 4).reshape(DEPTH, D, 512)
            a = _np.concatenate([q, a[:, :, 512:]], axis=2)
        if name == "w_nsa_branch":
            a = _np.ascontiguousarray(a.reshape(DEPTH, 2, 4, DH, D).transpose(0, 2, 1, 3, 4).reshape(DEPTH, 512, D))
        arrays[f"in_{name}"] = a
        io[name] = nc.dram_tensor(f"in_{name}", a.shape, _mybir.dt.from_np(a.dtype), kind="ExternalInput").ap()
    io["out"] = nc.dram_tensor("out_0", (1, SEQ, D), _mybir.dt.float32, kind="ExternalOutput").ap()
    hybrid_kernel(nc, io)
    r = _run(nc, [arrays], core_ids=[0])
    return r.results[0]["out_0"]
```
